# Optimizing a Trainium2 kernel written in Bass

```python
import math
import jax, jax.numpy as jnp
from jax import lax
import numpy as np

D_MODEL = 1024
BATCH = 1
SEQ = 512
DEPTH = 1

D_MIX = D_MODEL
N_MIXERS = 4
GROUP_W = D_MIX // N_MIXERS
HEAD_DIM = 64
N_HEADS_G = GROUP_W // HEAD_DIM
SSD_STATE = 128
SSD_CONV = 4
SSD_CHUNK = 128
RWKV_DECAY_LORA = 32
RWKV_A_LORA = 32
RWKV_GATE_LORA = 64
RWKV_GN_EPS = 64e-5
GLA_DK = GROUP_W // 2
GLA_HEAD_K = GLA_DK // N_HEADS_G
GLA_GATE_LORA = 16
GLA_GATE_TAU = 16.0
GLA_CHUNK = 64
MLSTM_CONV = 4
MLSTM_CHUNK = 64
N_EXPERTS = 32
TOP_K = 4
D_EXPERT = D_MODEL
SWIGLU_LIMIT = 7.0
SWIGLU_ALPHA = 1.702
EXPERT_BLOCK = 128
PLE_DIM = 256
DEEPNORM_ALPHA = (2 * DEPTH) ** 0.25
DEEPNORM_BETA = (8 * DEPTH) ** -0.25
LN_EPS = 1e-5
NORM_EPS = 1e-5

SSD_SPLITS = (GROUP_W, GROUP_W, SSD_STATE, SSD_STATE, N_HEADS_G)
RWKV_SPLITS = (GROUP_W, GROUP_W, GROUP_W, RWKV_DECAY_LORA, RWKV_A_LORA, RWKV_GATE_LORA)
GLA_SPLITS = (GLA_DK, GLA_DK, GROUP_W, GLA_GATE_LORA, GROUP_W)
MLSTM_SPLITS = (GROUP_W, GROUP_W, GROUP_W, N_HEADS_G, N_HEADS_G, GROUP_W)
SSD_W = sum(SSD_SPLITS)
RWKV_W = sum(RWKV_SPLITS)
GLA_W = sum(GLA_SPLITS)
MLSTM_W = sum(MLSTM_SPLITS)
D_IN_PROJ = SSD_W + RWKV_W + GLA_W + MLSTM_W


def _split(u, sizes):
    idx = np.cumsum(sizes)[:-1].tolist()
    return jnp.split(u, idx, axis=-1)

def _causal_mask(n):
    return jnp.tril(jnp.ones((n, n), dtype=bool))

def _causal_dwconv(u, w, b):
    k, c = w.shape
    y = lax.conv_general_dilated(u, w[:, None, :].astype(u.dtype), window_strides=(1,),
                                 padding=[(k - 1, 0)], dimension_numbers=("NWC", "WIO", "NWC"),
                                 feature_group_count=c)
    return y + b

def _token_shift(u):
    return jnp.pad(u, ((0, 0), (1, 0), (0, 0)))[:, :-1]

def _heads(u, n_heads):
    return u.reshape(*u.shape[:-1], n_heads, u.shape[-1] // n_heads)

def _to_chunks(u, size):
    b, s, h = u.shape[:3]
    u = u.reshape(b, s // size, size, h, *u.shape[3:])
    return jnp.moveaxis(u, 3, 1)

def _from_chunks(y):
    y = jnp.moveaxis(y, 1, 3)
    return y.reshape(y.shape[0], y.shape[1] * y.shape[2], *y.shape[3:])

def _chunk_states(decay, contrib):
    d = jnp.moveaxis(decay, 2, 0)
    u = jnp.moveaxis(contrib, 2, 0)

    def step(s, inp):
        dc, uc = inp
        return dc * s + uc, s

    _, prev = lax.scan(step, jnp.zeros_like(u[0]), (d, u))
    return jnp.moveaxis(prev, 0, 2)

def _layer_norm(x, g, b):
    xf = x.astype(jnp.float32)
    mu = jnp.mean(xf, -1, keepdims=True)
    xc = xf - mu
    var = jnp.mean(xc * xc, -1, keepdims=True)
    return (xc * lax.rsqrt(var + LN_EPS) * g + b).astype(x.dtype)

def _group_norm(y, n_heads, gain, bias, eps, center):
    yf = _heads(y.astype(jnp.float32), n_heads)
    if center:
        yf = yf - jnp.mean(yf, -1, keepdims=True)
    yf = yf * lax.rsqrt(jnp.mean(yf * yf, -1, keepdims=True) + eps)
    yf = yf.reshape(y.shape) * gain
    if bias is not None:
        yf = yf + bias
    return yf

def _ssd_mixer(u, conv_w, conv_b, a_log, dt_bias, d_skip, norm_g):
    bsz, seq, _ = u.shape
    z, xr, bm, cm, dt = _split(u, SSD_SPLITS)
    xbc = jax.nn.silu(_causal_dwconv(jnp.concatenate([xr, bm, cm], -1), conv_w, conv_b))
    xs, bm, cm = _split(xbc, (GROUP_W, SSD_STATE, SSD_STATE))
    xs = _heads(xs, N_HEADS_G)
    dt = jax.nn.softplus(dt + dt_bias)
    nc = seq // SSD_CHUNK
    xc = _to_chunks(xs * dt[..., None], SSD_CHUNK)
    adt = _to_chunks(dt * (-jnp.exp(a_log)), SSD_CHUNK)
    bc = bm.reshape(bsz, nc, SSD_CHUNK, SSD_STATE)
    cc = cm.reshape(bsz, nc, SSD_CHUNK, SSD_STATE)
    acum = jnp.cumsum(adt, axis=-1)
    lmat = jnp.exp(jnp.where(_causal_mask(SSD_CHUNK), acum[..., :, None] - acum[..., None, :], -jnp.inf))
    y_diag = jnp.einsum("bcln,bcsn,bhcls,bhcsp->bhclp", cc, bc, lmat, xc)
    decay_states = jnp.exp(acum[..., -1:] - acum)
    states = jnp.einsum("bcsn,bhcs,bhcsp->bhcpn", bc, decay_states, xc)
    prev = _chunk_states(jnp.exp(acum[..., -1])[..., None, None], states)
    y_off = jnp.einsum("bcln,bhcpn,bhcl->bhclp", cc, prev, jnp.exp(acum))
    y = _from_chunks(y_diag + y_off) + xs * d_skip[:, None]
    y = y.reshape(bsz, seq, GROUP_W) * jax.nn.silu(z)
    return _group_norm(y, 1, norm_g, None, NORM_EPS, center=False)

def _rwkv7_mixer(u, mu, w0, w_up, a0, a_up, g_up, k_k, k_a, r_k, ln_g, ln_b):
    bsz, seq, _ = u.shape
    u = u + (_token_shift(u) - u) * mu
    r, k, v, wd, ad, gd = _split(u, RWKV_SPLITS)
    w = -jax.nn.softplus(-(w0 + jnp.tanh(wd) @ w_up)) - 0.5
    decay = jnp.exp(-jnp.exp(w))
    a = jax.nn.sigmoid(a0 + ad @ a_up)
    g = jax.nn.sigmoid(gd) @ g_up
    kk = _heads(k * k_k, N_HEADS_G)
    kk = kk / jnp.maximum(jnp.linalg.norm(kk, axis=-1, keepdims=True), 1e-12)
    k = k * (1.0 + (a - 1.0) * k_a)
    rh, wh, kh, vh, ah = (_heads(t, N_HEADS_G) for t in (r, decay, k, v, a))
    seq_major = [jnp.moveaxis(t, 1, 0) for t in (rh, wh, kh, vh, -kk, kk * ah)]

    def step(state, inp):
        r_t, w_t, k_t, v_t, a_t, b_t = inp
        sa = jnp.einsum("bhvk,bhk->bhv", state, a_t)
        state = (state * w_t[:, :, None, :] + sa[..., None] * b_t[:, :, None, :]
                 + v_t[..., None] * k_t[:, :, None, :])
        return state, jnp.einsum("bhvk,bhk->bhv", state, r_t)

    s0 = jnp.zeros((bsz, N_HEADS_G, HEAD_DIM, HEAD_DIM), rh.dtype)
    _, o = lax.scan(step, s0, tuple(seq_major))
    o = jnp.moveaxis(o, 0, 1).reshape(bsz, seq, GROUP_W)
    o = _group_norm(o, N_HEADS_G, ln_g, ln_b, RWKV_GN_EPS, center=True)
    bonus = jnp.sum(rh * kh * r_k, -1, keepdims=True) * vh
    return (o + bonus.reshape(bsz, seq, GROUP_W)) * g

def _gla_mixer(u, gate_up, gate_b, norm_g):
    bsz, seq, _ = u.shape
    q, k, v, gd, og = _split(u, GLA_SPLITS)
    log_a = jax.nn.log_sigmoid(gd @ gate_up + gate_b) / GLA_GATE_TAU
    qc = _to_chunks(_heads(q, N_HEADS_G), GLA_CHUNK) * GLA_HEAD_K ** -0.5
    kc = _to_chunks(_heads(k, N_HEADS_G), GLA_CHUNK)
    vc = _to_chunks(_heads(v, N_HEADS_G), GLA_CHUNK)
    bcum = jnp.cumsum(_to_chunks(_heads(log_a, N_HEADS_G), GLA_CHUNK), axis=3)
    q_dec = qc * jnp.exp(bcum)
    k_inv = kc * jnp.exp(-bcum)
    attn = jnp.where(_causal_mask(GLA_CHUNK), jnp.einsum("bhctd,bhcsd->bhcts", q_dec, k_inv), 0.0)
    o_intra = jnp.einsum("bhcts,bhcsv->bhctv", attn, vc)
    b_last = bcum[..., -1, :]
    contrib = jnp.einsum("bhcsd,bhcsv->bhcdv", kc * jnp.exp(b_last[..., None, :] - bcum), vc)
    prev = _chunk_states(jnp.exp(b_last)[..., None], contrib)
    o_inter = jnp.einsum("bhctd,bhcdv->bhctv", q_dec, prev)
    o = _from_chunks(o_intra + o_inter).reshape(bsz, seq, GROUP_W)
    return _group_norm(o, N_HEADS_G, norm_g, None, NORM_EPS, center=False) * jax.nn.silu(og)

def _mlstm_mixer(u, conv_w, conv_b, i_b, f_b, norm_g):
    bsz, seq, _ = u.shape
    q, k, v, ig, fg, og = _split(u, MLSTM_SPLITS)
    q, k = _split(jax.nn.silu(_causal_dwconv(jnp.concatenate([q, k], -1), conv_w, conv_b)), (GROUP_W, GROUP_W))
    qc = _to_chunks(_heads(q, N_HEADS_G), MLSTM_CHUNK) * HEAD_DIM ** -0.5
    kc = _to_chunks(_heads(k, N_HEADS_G), MLSTM_CHUNK)
    vc = _to_chunks(_heads(v, N_HEADS_G), MLSTM_CHUNK)
    i_pre = _to_chunks(ig + i_b, MLSTM_CHUNK)
    b = jnp.cumsum(_to_chunks(jax.nn.log_sigmoid(fg + f_b), MLSTM_CHUNK), axis=-1)
    b_last = b[..., -1]
    dmat = jnp.where(_causal_mask(MLSTM_CHUNK), b[..., :, None] - b[..., None, :] + i_pre[..., None, :], -jnp.inf)
    a_st = b_last[..., None] - b + i_pre
    m_loc = jnp.max(a_st, -1)
    w_st = jnp.exp(a_st - m_loc[..., None])
    c_contrib = jnp.einsum("bhcs,bhcsv,bhcsk->bhcvk", w_st, vc, kc)
    n_contrib = jnp.einsum("bhcs,bhcsk->bhck", w_st, kc)

    def step(carry, inp):
        c_s, n_s, m_s = carry
        bl, ml, cu, nu = inp
        m_new = jnp.maximum(bl + m_s, ml)
        s_old = jnp.exp(bl + m_s - m_new)
        s_new = jnp.exp(ml - m_new)
        c_new = s_old[..., None, None] * c_s + s_new[..., None, None] * cu
        n_new = s_old[..., None] * n_s + s_new[..., None] * nu
        return (c_new, n_new, m_new), (c_s, n_s, m_s)

    init = (jnp.zeros_like(c_contrib[:, :, 0]), jnp.zeros_like(n_contrib[:, :, 0]), jnp.zeros_like(b_last[:, :, 0]))
    xs = tuple(jnp.moveaxis(t, 2, 0) for t in (b_last, m_loc, c_contrib, n_contrib))
    _, (c_prev, n_prev, m_prev) = lax.scan(step, init, xs)
    c_prev, n_prev, m_prev = (jnp.moveaxis(t, 0, 2) for t in (c_prev, n_prev, m_prev))
    m_inter = b + m_prev[..., None]
    m_row = jnp.maximum(m_inter, jnp.max(dmat, -1))
    w_inter = jnp.exp(m_inter - m_row)
    scores = jnp.einsum("bhctk,bhcsk->bhcts", qc, kc) * jnp.exp(dmat - m_row[..., None])
    num = (w_inter[..., None] * jnp.einsum("bhcvk,bhctk->bhctv", c_prev, qc)
           + jnp.einsum("bhcts,bhcsv->bhctv", scores, vc))
    den = w_inter * jnp.einsum("bhck,bhctk->bhct", n_prev, qc) + jnp.sum(scores, -1)
    h = num / jnp.maximum(jnp.abs(den), jnp.exp(-m_row))[..., None]
    h = _from_chunks(h).reshape(bsz, seq, GROUP_W) * jax.nn.sigmoid(og)
    return _group_norm(h, N_HEADS_G, norm_g, None, NORM_EPS, center=True)

def _moe_ffn(x2d, router_w, router_b, w_gu, b_gu, w_down, b_down):
    t, d = x2d.shape
    n_assign = t * TOP_K
    logits = (x2d @ router_w + router_b).astype(jnp.float32)
    top_val, top_idx = lax.top_k(logits, TOP_K)
    gate = jax.nn.softmax(top_val, axis=-1)
    flat_e = top_idx.reshape(-1)
    flat_tok = jnp.arange(n_assign, dtype=jnp.int32) // TOP_K
    order = jnp.argsort(flat_e)
    e_s, tok_s, g_s = flat_e[order], flat_tok[order], gate.reshape(-1)[order]
    counts = jnp.zeros((N_EXPERTS,), jnp.int32).at[flat_e].add(1)
    padded = (counts + EXPERT_BLOCK - 1) // EXPERT_BLOCK * EXPERT_BLOCK
    start = jnp.cumsum(counts) - counts
    pend = jnp.cumsum(padded)
    pstart = pend - padded
    dest = pstart[e_s] + (jnp.arange(n_assign, dtype=jnp.int32) - start[e_s])
    n_blocks = (n_assign + N_EXPERTS * (EXPERT_BLOCK - 1) + EXPERT_BLOCK - 1) // EXPERT_BLOCK
    n_rows = n_blocks * EXPERT_BLOCK
    row_tok = jnp.full((n_rows,), t, jnp.int32).at[dest].set(tok_s)
    row_gate = jnp.zeros((n_rows,), jnp.float32).at[dest].set(g_s)
    block_expert = jnp.minimum(jnp.searchsorted(pend, jnp.arange(n_blocks) * EXPERT_BLOCK, side="right"),
                               N_EXPERTS - 1)
    x_pad = jnp.concatenate([x2d, jnp.zeros((1, d), x2d.dtype)], 0)
    xb = x_pad[row_tok].reshape(n_blocks, EXPERT_BLOCK, d)

    def expert_block(args):
        xblk, e = args
        hg, hl = jnp.split(xblk @ w_gu[e] + b_gu[e], 2, axis=-1)
        hg = jnp.minimum(hg, SWIGLU_LIMIT)
        hl = jnp.clip(hl, -SWIGLU_LIMIT, SWIGLU_LIMIT)
        glu = hg * jax.nn.sigmoid(hg * SWIGLU_ALPHA)
        return ((hl + 1.0) * glu) @ w_down[e] + b_down[e]

    yb = lax.map(expert_block, (xb, block_expert)).reshape(n_rows, d)
    y = (yb * row_gate[:, None]).astype(x2d.dtype)
    return jnp.zeros((t + 1, d), x2d.dtype).at[row_tok].add(y)[:t]

def first_inputs(seed: int = 0) -> dict:
    key = jax.random.key(seed)
    ks = iter(jax.random.split(key, 64))
    f32 = jnp.float32
    L, W, H = DEPTH, GROUP_W, N_HEADS_G

    def nrm(shape, scale):
        return scale * jax.random.normal(next(ks), shape, f32)

    def uni(shape, lo, hi):
        return jax.random.uniform(next(ks), shape, f32, lo, hi)

    dt0 = jnp.exp(uni((L, H), math.log(1e-3), math.log(1e-1)))
    return {
        "x": nrm((BATCH, SEQ, D_MODEL), 1.0),
        "p": nrm((DEPTH, BATCH, SEQ, PLE_DIM), 1.0),
        "w_in": nrm((L, D_MODEL, D_IN_PROJ), D_MODEL ** -0.5),
        "w_out": nrm((L, D_MIX, D_MODEL), DEEPNORM_BETA * D_MIX ** -0.5),
        "ln1_g": 1.0 + nrm((L, D_MODEL), 0.02),
        "ln1_b": nrm((L, D_MODEL), 0.02),
        "ssd_conv_w": nrm((L, SSD_CONV, W + 2 * SSD_STATE), SSD_CONV ** -0.5),
        "ssd_conv_b": nrm((L, W + 2 * SSD_STATE), 0.02),
        "ssd_a_log": jnp.log(uni((L, H), 1.0, 16.0)),
        "ssd_dt_bias": dt0 + jnp.log(-jnp.expm1(-dt0)),
        "ssd_d": 1.0 + nrm((L, H), 0.1),
        "ssd_norm_g": 1.0 + nrm((L, W), 0.02),
        "rwkv_mu": uni((L, RWKV_W), 0.0, 1.0),
        "rwkv_w0": uni((L, W), -6.0, -1.0),
        "rwkv_w_up": nrm((L, RWKV_DECAY_LORA, W), 0.5 * RWKV_DECAY_LORA ** -0.5),
        "rwkv_a0": nrm((L, W), 0.1),
        "rwkv_a_up": nrm((L, RWKV_A_LORA, W), RWKV_A_LORA ** -0.5),
        "rwkv_g_up": nrm((L, RWKV_GATE_LORA, W), RWKV_GATE_LORA ** -0.5),
        "rwkv_k_k": 0.85 + nrm((L, W), 0.02),
        "rwkv_k_a": 1.0 + nrm((L, W), 0.02),
        "rwkv_r_k": nrm((L, H, HEAD_DIM), 0.1),
        "rwkv_ln_g": 1.0 + nrm((L, W), 0.02),
        "rwkv_ln_b": nrm((L, W), 0.02),
        "gla_gate_up": nrm((L, GLA_GATE_LORA, GLA_DK), GLA_GATE_LORA ** -0.5),
        "gla_gate_b": nrm((L, GLA_DK), 0.1),
        "gla_norm_g": 1.0 + nrm((L, W), 0.02),
        "mlstm_conv_w": nrm((L, MLSTM_CONV, 2 * W), MLSTM_CONV ** -0.5),
        "mlstm_conv_b": nrm((L, 2 * W), 0.02),
        "mlstm_i_b": nrm((L, H), 0.1),
        "mlstm_f_b": uni((L, H), 3.0, 6.0),
        "mlstm_norm_g": 1.0 + nrm((L, W), 0.02),
        "router_w": nrm((L, D_MODEL, N_EXPERTS), D_MODEL ** -0.5),
        "router_b": nrm((L, N_EXPERTS), 0.01),
        "exp_w_gu": nrm((L, N_EXPERTS, D_MODEL, 2 * D_EXPERT), D_MODEL ** -0.5),
        "exp_b_gu": nrm((L, N_EXPERTS, 2 * D_EXPERT), 0.01),
        "exp_w_down": nrm((L, N_EXPERTS, D_EXPERT, D_MODEL), DEEPNORM_BETA * D_EXPERT ** -0.5),
        "exp_b_down": nrm((L, N_EXPERTS, D_MODEL), 0.01),
        "ple_gate_w": nrm((L, D_MODEL, D_MODEL), D_MODEL ** -0.5),
        "ple_proj": nrm((L, PLE_DIM, D_MODEL), DEEPNORM_BETA * PLE_DIM ** -0.5),
        "ln2_g": 1.0 + nrm((L, D_MODEL), 0.02),
        "ln2_b": nrm((L, D_MODEL), 0.02),
    }

def first_block(x, p, w_in, w_out, ln1_g, ln1_b,
              ssd_conv_w, ssd_conv_b, ssd_a_log, ssd_dt_bias, ssd_d, ssd_norm_g,
              rwkv_mu, rwkv_w0, rwkv_w_up, rwkv_a0, rwkv_a_up, rwkv_g_up, rwkv_k_k, rwkv_k_a,
              rwkv_r_k, rwkv_ln_g, rwkv_ln_b,
              gla_gate_up, gla_gate_b, gla_norm_g,
              mlstm_conv_w, mlstm_conv_b, mlstm_i_b, mlstm_f_b, mlstm_norm_g,
              router_w, router_b, exp_w_gu, exp_b_gu, exp_w_down, exp_b_down,
              ple_gate_w, ple_proj, ln2_g, ln2_b):
    bsz, seq, d = x.shape
    for i in range(DEPTH):
        u = (x @ w_in[i]).astype(jnp.float32)
        u_ssd, u_rwkv, u_gla, u_mlstm = _split(u, (SSD_W, RWKV_W, GLA_W, MLSTM_W))
        y_ssd = _ssd_mixer(u_ssd, ssd_conv_w[i], ssd_conv_b[i], ssd_a_log[i], ssd_dt_bias[i],
                           ssd_d[i], ssd_norm_g[i])
        y_rwkv = _rwkv7_mixer(u_rwkv, rwkv_mu[i], rwkv_w0[i], rwkv_w_up[i], rwkv_a0[i], rwkv_a_up[i],
                              rwkv_g_up[i], rwkv_k_k[i], rwkv_k_a[i], rwkv_r_k[i], rwkv_ln_g[i], rwkv_ln_b[i])
        y_gla = _gla_mixer(u_gla, gla_gate_up[i], gla_gate_b[i], gla_norm_g[i])
        y_mlstm = _mlstm_mixer(u_mlstm, mlstm_conv_w[i], mlstm_conv_b[i], mlstm_i_b[i], mlstm_f_b[i],
                               mlstm_norm_g[i])
        mix = jnp.concatenate([y_ssd, y_rwkv, y_gla, y_mlstm], -1).astype(x.dtype) @ w_out[i]
        x = _layer_norm(DEEPNORM_ALPHA * x + mix, ln1_g[i], ln1_b[i])
        ffn = _moe_ffn(x.reshape(bsz * seq, d), router_w[i], router_b[i], exp_w_gu[i], exp_b_gu[i],
                       exp_w_down[i], exp_b_down[i]).reshape(bsz, seq, d)
        h = DEEPNORM_ALPHA * x + ffn
        h = h + jax.nn.sigmoid(h @ ple_gate_w[i]) * (p[i] @ ple_proj[i])
        x = _layer_norm(h, ln2_g[i], ln2_b[i])
    return x


_first_inputs = first_inputs


def first_inputs(seed=0):
    import zlib

    import numpy as np

    out = dict(_first_inputs(seed))
    spreads = {}
    factors = {'ssd_conv_b': 4.119,
     'ssd_norm_g': 38.958,
     'rwkv_w_up': 7.026,
     'rwkv_a0': 5.308,
     'rwkv_k_k': 200.0,
     'rwkv_k_a': 74.503,
     'rwkv_ln_g': 84.375,
     'rwkv_ln_b': 101.95,
     'gla_gate_b': 3.936,
     'gla_norm_g': 74.663,
     'mlstm_conv_b': 4.018,
     'mlstm_i_b': 200.0,
     'mlstm_norm_g': 16.851,
     'router_b': 3.315,
     'exp_b_gu': 8.0,
     'exp_b_down': 8.0,
     'ln2_g': 20.412,
     'ln2_b': 19.305}
    for name, (base, spread) in spreads.items():
        noise = np.random.default_rng([zlib.crc32(name.encode()), seed]).standard_normal(out[name].shape)
        drawn = base * np.exp(spread * noise) if base else spread * noise
        out[name] = __import__('jax').numpy.asarray(drawn.astype(out[name].dtype))
    for name, factor in factors.items():
        out[name] = (out[name] * factor).astype(out[name].dtype)
    return out


_narrow_inputs = first_inputs


def first_inputs(seed=0):

    out = dict(_narrow_inputs(seed))
    wider = {'ssd_norm_g': 3.26,
     'rwkv_k_k': 4.65,
     'gla_norm_g': 3.2,
     'mlstm_i_b': 12.0,
     'mlstm_norm_g': 8.43,
     'ln2_g': 3.07,
     'ln2_b': 3.07}
    for name, times in wider.items():
        mean = out[name].mean()
        out[name] = (mean + times * (out[name] - mean)).astype(out[name].dtype)
    return out


DEPTH_2 = 2

N_META = 16
CHUNK = 128
PAD = (-N_META) % CHUNK
RET_HEADS = 4
RET_DK = 48
RET_DV = 96
RET_QK = RET_HEADS * RET_DK
RET_W = RET_HEADS * RET_DV
POOL_WINDOWS = (2, 4, 8, 16)
POOL_GROUP = 64
POOL_W = len(POOL_WINDOWS) * POOL_GROUP
FOX_HEADS = 6
FOX_DH = 64
FOX_W = FOX_HEADS * FOX_DH
D_MIX_2 = RET_W + POOL_W + FOX_W
IN_SPLITS = (RET_QK, RET_QK, RET_W, RET_W, POOL_W, FOX_W, FOX_W, FOX_W, FOX_HEADS)
D_IN = sum(IN_SPLITS)
D_FF = -(-8 * D_MODEL // (3 * 256)) * 256
ROPE_BASE = 10000.0
NEG_INF = -1e30
ALPHA = (2.0 * DEPTH_2) ** 0.25
BETA = (8.0 * DEPTH_2) ** -0.25


def layer_norm(x, g, b):
    xf = x.astype(jnp.float32)
    mu = jnp.mean(xf, axis=-1, keepdims=True)
    var = jnp.mean(jnp.square(xf - mu), axis=-1, keepdims=True)
    y = (xf - mu) * lax.rsqrt(var + LN_EPS)
    return (y * g + b).astype(x.dtype)

def pad_front(a):
    widths = [(0, 0), (PAD, 0)] + [(0, 0)] * (a.ndim - 2)
    return jnp.pad(a, widths)

def rotary(x, cos, sin):
    half = x.shape[-1] // 2
    x1, x2 = x[..., :half], x[..., half:]
    return jnp.concatenate([x1 * cos - x2 * sin, x1 * sin + x2 * cos], axis=-1)

def retention_chunkwise(q, k, v):
    Bsz, Lp, H, dk = q.shape
    dv = v.shape[-1]
    n = Lp // CHUNK
    gamma = 1.0 - 2.0 ** (-5.0 - jnp.arange(H, dtype=jnp.float32))
    lg = jnp.log(gamma)
    i = jnp.arange(CHUNK, dtype=jnp.float32)
    diff = i[:, None] - i[None, :]
    dmask = jnp.where(diff >= 0, jnp.exp(lg[:, None, None] * jnp.maximum(diff, 0.0)), 0.0)
    xi = jnp.exp(lg[:, None] * (i + 1.0))
    zeta = jnp.exp(lg[:, None] * (CHUNK - 1.0 - i))
    chunk_decay = jnp.exp(lg * CHUNK)
    qc = q.astype(jnp.float32).reshape(Bsz, n, CHUNK, H, dk)
    kc = k.astype(jnp.float32).reshape(Bsz, n, CHUNK, H, dk) * (dk ** -0.5)
    vc = v.astype(jnp.float32).reshape(Bsz, n, CHUNK, H, dv)
    scores = jnp.einsum('bnihd,bnjhd->bnhij', qc, kc) * dmask
    inner = jnp.einsum('bnhij,bnjhe->bnihe', scores, vc)
    kv = jnp.einsum('bnjhd,hj,bnjhe->nbhde', kc, zeta, vc)

    def step(state, kv_n):
        return state * chunk_decay[None, :, None, None] + kv_n, state

    _, prev = lax.scan(step, jnp.zeros_like(kv[0]), kv)
    cross = jnp.einsum('bnihd,nbhde,hi->bnihe', qc, prev, xi)
    return (inner + cross).reshape(Bsz, Lp, H, dv)

def multiscale_pool(u, pool_w, pool_scale):
    Bsz, L, _ = u.shape
    G = len(POOL_WINDOWS)
    uf = u.astype(jnp.float32).reshape(Bsz, L, G, POOL_GROUP)
    cs = jnp.concatenate([jnp.zeros((Bsz, 1, G, POOL_GROUP), jnp.float32),
                          jnp.cumsum(uf, axis=1)], axis=1)
    t = jnp.arange(L)
    outs = []
    for g, w in enumerate(POOL_WINDOWS):
        lo = jnp.maximum(t + 1 - w, 0)
        cnt = (t + 1 - lo).astype(jnp.float32)
        window_sum = cs[:, t + 1, g] - cs[:, lo, g]
        outs.append(window_sum / cnt[None, :, None] - uf[:, :, g])
    pooled = jnp.stack(outs, axis=2)
    y = jnp.einsum('blgc,gcd->blgd', pooled, pool_w.astype(jnp.float32)).reshape(Bsz, L, POOL_W)
    return y * pool_scale

def forgetting_attention(q, k, v, logf):
    Bsz, Lp, H, d = q.shape
    c = jnp.cumsum(logf.astype(jnp.float32), axis=1).transpose(0, 2, 1)
    qf = q.astype(jnp.float32) * (d ** -0.5)
    kf = k.astype(jnp.float32)
    vf = v.astype(jnp.float32)
    kpos = jnp.arange(Lp)
    key_ok = kpos >= PAD
    nb = Lp // CHUNK

    def block(ib):
        start = ib * CHUNK
        qb = lax.dynamic_slice_in_dim(qf, start, CHUNK, axis=1)
        cb = lax.dynamic_slice_in_dim(c, start, CHUNK, axis=2)
        qpos = start + jnp.arange(CHUNK)
        s = jnp.einsum('bihd,bjhd->bhij', qb, kf)
        s = s + cb[..., :, None] - c[..., None, :]
        mask = (kpos[None, :] <= qpos[:, None]) & key_ok[None, :]
        s = jnp.where(mask, s, NEG_INF)
        p = jax.nn.softmax(s, axis=-1)
        return jnp.einsum('bhij,bjhd->bihd', p, vf)

    out = lax.map(block, jnp.arange(nb))
    return out.transpose(1, 0, 2, 3, 4).reshape(Bsz, Lp, H, d)

def head_group_norm(o, g):
    of = o.astype(jnp.float32)
    mu = jnp.mean(of, axis=-1, keepdims=True)
    var = jnp.mean(jnp.square(of - mu), axis=-1, keepdims=True)
    y = ((of - mu) * lax.rsqrt(var + LN_EPS)).reshape(o.shape[0], o.shape[1], -1)
    return y * g

def hybrid_layer(h, w_in, b_f, ret_gn_g, pool_w, pool_scale, w_out,
                 ln1_g, ln1_b, w1, w3, w2, ln2_g, ln2_b, cos, sin):
    Bsz, L, _ = h.shape
    proj = jnp.einsum('bld,de->ble', h, w_in)
    parts = []
    off = 0
    for sz in IN_SPLITS:
        parts.append(proj[..., off:off + sz])
        off += sz
    q_r, k_r, v_r, g_r, u_p, q_f, k_f, v_f, f_logit = parts

    qr = rotary(pad_front(q_r.reshape(Bsz, L, RET_HEADS, RET_DK)), cos, sin)
    kr = rotary(pad_front(k_r.reshape(Bsz, L, RET_HEADS, RET_DK)), cos, sin)
    vr = pad_front(v_r.reshape(Bsz, L, RET_HEADS, RET_DV))
    o_r = retention_chunkwise(qr, kr, vr)[:, PAD:]
    o_r = jax.nn.silu(g_r.astype(jnp.float32)) * head_group_norm(o_r, ret_gn_g)

    o_p = multiscale_pool(u_p, pool_w, pool_scale)

    logf = jax.nn.log_sigmoid(f_logit.astype(jnp.float32) + b_f)
    o_f = forgetting_attention(pad_front(q_f.reshape(Bsz, L, FOX_HEADS, FOX_DH)),
                               pad_front(k_f.reshape(Bsz, L, FOX_HEADS, FOX_DH)),
                               pad_front(v_f.reshape(Bsz, L, FOX_HEADS, FOX_DH)),
                               pad_front(logf))[:, PAD:].reshape(Bsz, L, FOX_W)

    mix = jnp.concatenate([o_r, o_p, o_f], axis=-1)
    mix = jnp.einsum('ble,ed->bld', mix, w_out)
    h = layer_norm(ALPHA * h + mix, ln1_g, ln1_b)

    a = jnp.einsum('bld,df->blf', h, w1)
    b = jnp.einsum('bld,df->blf', h, w3)
    y = jnp.einsum('blf,fd->bld', jax.nn.silu(a) * b, w2)
    return layer_norm(ALPHA * h + y, ln2_g, ln2_b)

def second_inputs(seed: int = 0) -> dict:
    key = jax.random.key(seed)
    ks = jax.random.split(key, 20)
    f32 = jnp.float32
    x = jax.random.normal(ks[0], (BATCH, SEQ, D_MODEL), f32)
    meta = jax.random.normal(ks[1], (N_META, D_MODEL), f32)
    ln_emb_g = 1.0 + 0.01 * jax.random.normal(ks[2], (D_MODEL,), f32)
    ln_emb_b = 0.01 * jax.random.normal(ks[3], (D_MODEL,), f32)
    w_in = jax.random.normal(ks[4], (DEPTH_2, D_MODEL, D_IN), f32) * D_MODEL ** -0.5
    b_f = jax.random.uniform(ks[5], (DEPTH_2, FOX_HEADS), f32, 1.0, 4.0)
    ret_gn_g = 1.0 + 0.01 * jax.random.normal(ks[6], (DEPTH_2, RET_W), f32)
    pool_w = jax.random.normal(ks[7], (DEPTH_2, len(POOL_WINDOWS), POOL_GROUP, POOL_GROUP), f32) * POOL_GROUP ** -0.5
    pool_scale = 1.0 + 0.1 * jax.random.normal(ks[8], (DEPTH_2, POOL_W), f32)
    w_out = jax.random.normal(ks[9], (DEPTH_2, D_MIX_2, D_MODEL), f32) * (D_MIX_2 ** -0.5) * BETA
    ln1_g = 1.0 + 0.01 * jax.random.normal(ks[10], (DEPTH_2, D_MODEL), f32)
    ln1_b = 0.01 * jax.random.normal(ks[11], (DEPTH_2, D_MODEL), f32)
    w_ffn1 = jax.random.normal(ks[12], (DEPTH_2, D_MODEL, D_FF), f32) * D_MODEL ** -0.5
    w_ffn3 = jax.random.normal(ks[13], (DEPTH_2, D_MODEL, D_FF), f32) * D_MODEL ** -0.5
    w_ffn2 = jax.random.normal(ks[14], (DEPTH_2, D_FF, D_MODEL), f32) * (D_FF ** -0.5) * BETA
    ln2_g = 1.0 + 0.01 * jax.random.normal(ks[15], (DEPTH_2, D_MODEL), f32)
    ln2_b = 0.01 * jax.random.normal(ks[16], (DEPTH_2, D_MODEL), f32)
    return {'x': x, 'meta': meta, 'ln_emb_g': ln_emb_g, 'ln_emb_b': ln_emb_b,
            'w_in': w_in, 'b_f': b_f, 'ret_gn_g': ret_gn_g, 'pool_w': pool_w,
            'pool_scale': pool_scale, 'w_out': w_out, 'ln1_g': ln1_g, 'ln1_b': ln1_b,
            'w_ffn1': w_ffn1, 'w_ffn3': w_ffn3, 'w_ffn2': w_ffn2,
            'ln2_g': ln2_g, 'ln2_b': ln2_b}

def second_block(x, meta, ln_emb_g, ln_emb_b, w_in, b_f, ret_gn_g, pool_w, pool_scale,
              w_out, ln1_g, ln1_b, w_ffn1, w_ffn3, w_ffn2, ln2_g, ln2_b):
    Bsz = x.shape[0]
    h = jnp.concatenate([jnp.broadcast_to(meta[None].astype(x.dtype), (Bsz, N_META, D_MODEL)), x], axis=1)
    h = layer_norm(h, ln_emb_g, ln_emb_b)
    L = h.shape[1]
    Lp = L + PAD
    pos = jnp.arange(Lp, dtype=jnp.float32) - PAD
    inv_freq = ROPE_BASE ** (-jnp.arange(RET_DK // 2, dtype=jnp.float32) / (RET_DK // 2))
    ang = pos[:, None] * inv_freq[None, :]
    cos = jnp.cos(ang)[:, None, :]
    sin = jnp.sin(ang)[:, None, :]
    for l in range(DEPTH_2):
        h = hybrid_layer(h, w_in[l], b_f[l], ret_gn_g[l], pool_w[l], pool_scale[l], w_out[l],
                         ln1_g[l], ln1_b[l], w_ffn1[l], w_ffn3[l], w_ffn2[l], ln2_g[l], ln2_b[l],
                         cos, sin)
    return h[:, N_META:]


def setup_inputs(seed=0):
    out = dict(first_inputs(seed))
    for name, value in second_inputs(seed + 1).items():
        if name != "x":
            out[name + "_2"] = value
    return out


def reference(
    x, p, w_in, w_out, ln1_g, ln1_b, ssd_conv_w, ssd_conv_b, ssd_a_log, ssd_dt_bias, ssd_d,
    ssd_norm_g, rwkv_mu, rwkv_w0, rwkv_w_up, rwkv_a0, rwkv_a_up, rwkv_g_up, rwkv_k_k, rwkv_k_a,
    rwkv_r_k, rwkv_ln_g, rwkv_ln_b, gla_gate_up, gla_gate_b, gla_norm_g, mlstm_conv_w,
    mlstm_conv_b, mlstm_i_b, mlstm_f_b, mlstm_norm_g, router_w, router_b, exp_w_gu, exp_b_gu,
    exp_w_down, exp_b_down, ple_gate_w, ple_proj, ln2_g, ln2_b, meta_2, ln_emb_g_2, ln_emb_b_2,
    w_in_2, b_f_2, ret_gn_g_2, pool_w_2, pool_scale_2, w_out_2, ln1_g_2, ln1_b_2, w_ffn1_2,
    w_ffn3_2, w_ffn2_2, ln2_g_2, ln2_b_2,
):
    x = first_block(
        x, p, w_in, w_out, ln1_g, ln1_b, ssd_conv_w, ssd_conv_b, ssd_a_log, ssd_dt_bias, ssd_d,
        ssd_norm_g, rwkv_mu, rwkv_w0, rwkv_w_up, rwkv_a0, rwkv_a_up, rwkv_g_up, rwkv_k_k,
        rwkv_k_a, rwkv_r_k, rwkv_ln_g, rwkv_ln_b, gla_gate_up, gla_gate_b, gla_norm_g,
        mlstm_conv_w, mlstm_conv_b, mlstm_i_b, mlstm_f_b, mlstm_norm_g, router_w, router_b,
        exp_w_gu, exp_b_gu, exp_w_down, exp_b_down, ple_gate_w, ple_proj, ln2_g, ln2_b,
    )
    return second_block(
        x, meta_2, ln_emb_g_2, ln_emb_b_2, w_in_2, b_f_2, ret_gn_g_2, pool_w_2, pool_scale_2,
        w_out_2, ln1_g_2, ln1_b_2, w_ffn1_2, w_ffn3_2, w_ffn2_2, ln2_g_2, ln2_b_2,
    )


_drawn_inputs = setup_inputs


def setup_inputs(seed=0):
    import zlib

    import numpy as np

    out = dict(_drawn_inputs(seed))
    spreads = {}
    factors = {'mlstm_i_b': 8.0,
     'ln_emb_g_2': 5.235,
     'ln_emb_b_2': 4.945,
     'ret_gn_g_2': 8.0,
     'ln1_g_2': 3.838,
     'ln1_b_2': 3.746,
     'ln2_g_2': 4.088,
     'ln2_b_2': 3.875}
    for name, (base, spread) in spreads.items():
        noise = np.random.default_rng([zlib.crc32(name.encode()), seed]).standard_normal(out[name].shape)
        drawn = base * np.exp(spread * noise) if base else spread * noise
        out[name] = __import__('jax').numpy.asarray(drawn.astype(out[name].dtype))
    for name, factor in factors.items():
        out[name] = (out[name] * factor).astype(out[name].dtype)
    return out
```

```python
from contextlib import ExitStack

import concourse.bass as bass
import numpy as np
from concourse import mybir

F32 = mybir.dt.float32
ALU = mybir.AluOpType
ACT = mybir.ActivationFunctionType
AX = mybir.AxisListType

P = 128
D = 1024
KT = D // P
SEQ = 512
TT = SEQ // P
H = 4
HD = 64
W = H * HD
CH = 64
E = 32
TOP = 4
SWIGLU_ALPHA, SWIGLU_LIMIT = 1.702, 7.0
EXTRA = SEQ * TOP // P - 1
NB = E + EXTRA + 1
ALPHA1 = 2 ** 0.25
ALPHA2 = 4 ** 0.25
LN_EPS = 1e-5
GN_EPS_RWKV = 64e-5
NEG = -1e30

SLOTS = 6
PIECE = KT * 512
PAD = 3

F_SSD, F_MQK, F_GLA, F_RWKV, F_ROWS = 0, 4, 8, 10, 17
NF = 18
T_Z, T_MV, T_MOG, T_GV, T_GOG = 0, 256, 512, 768, 1024
NT = 1280


META = 16
LEN = META + SEQ
NT2 = TT + 1
OFF = [0] + [META + P * t for t in range(TT)]
SIZE = [META] + [P] * TT
LAYERS = 2
RH, RK, RV = 4, 48, 96
WINDOWS = (2, 4, 8, 16)
FH = 6
FF = 2816
FT = FF // P
HALF = LEN // 2
U_QK, U_V, U_G, U_U, U_VF = 0, 384, 768, 1152, 1408
NU = 1792
W_OUT, W_FFN, W_DOWN, LAYER_PIECES = 5, 7, 18, 24

LAYER_SIGNALS = dict(
    forget_asked=1, forget_given=1, fox_max=30, fox_out=30, fox_out_drained=30, fox_scores=30, fox_scores_drained=30,
    fox_turned=36, fox_turned_drained=36, fox_weights_ready=30, layer_ln_asked=4, layer_ln_given=4,
    layer_scalar_drained=93, layer_scalar_filled=93, layer_scalar_step=26, layer_start=1, layer_vector_drained=135,
    layer_vector_filled=135, layer_vector_step=198, mid_ready=1, mix2_ready=1, ret_gate_ready=2, ret_root=2,
    ret_stat=2, retained_drained=4, retention_done=24, rotated_ready=5,
    layer_params_landed=16 * 5, retention_decay_landed=16, layer_ln_landed=16 * 2,
    **{f"layer_weights_landed_{s}": 16 * LAYER_PIECES // SLOTS for s in range(SLOTS)})


class Layout:

    def __init__(self, **widths):
        self.at, self.width = {}, 0
        for name, w in widths.items():
            self.at[name] = (self.width, w)
            self.width += w

    def __call__(self, tensor, name, a=0, b=None):
        at, w = self.at[name]
        return tensor[:, at + a:at + (w if b is None else b)]


CONST1 = Layout(ident=P, causal=SEQ, select=H * P, eps=2, ones=P)
CONST2 = Layout(mask4=4 * P, lower=P, level=12 * P, headones=P, headsum=2, reset=SEQ, glamask=W)
CONST3 = Layout(before=P, iota=P, expert=P)
CONST4 = Layout(pool=4 * P, pool_before=4 * P, pool_meta=4 * P, pool_first=4 * META, cos=NT2 * 24, sin=NT2 * 24, row_causal=P)
ROWS2 = Layout(ret_g=RH * RV, pool_scale=4 * HD)
COLS = Layout(ssd_cw=16, ssd_cb=4, m_cw=16, m_cb=4, mu=7, w0=2, a0=2, k_k=2, k_a=2, r_k=2, gate_b=1,
              rows_b=1, a_log=1)
ROWS = Layout(ssd_d=H, ssd_g=W, rwkv_g=W, rwkv_b=W, gla_g=W, m_g=W)


def const1():
    c = np.zeros((P, CONST1.width), np.float32)
    s = np.arange(P)[:, None]
    CONST1(c, "ident")[:] = np.eye(P)
    CONST1(c, "causal")[:] = np.where(np.arange(SEQ)[None] >= s, 0.0, NEG)
    CONST1(c, "select")[:] = (np.arange(H * P)[None] // P == s)
    CONST1(c, "eps")[:] = [LN_EPS, GN_EPS_RWKV]
    CONST1(c, "ones")[:] = 1.0
    return c


def const2():
    c = np.zeros((P, CONST2.width), np.float32)
    s, t = np.arange(P)[:, None], np.arange(P)[None]
    same = s // CH == t // CH
    strict, incl = same & (s < t), same & (s <= t)
    CONST2(c, "mask4")[:] = np.concatenate([strict, incl, strict, incl], 1)
    CONST2(c, "lower")[:] = same & (s > t)
    levels = []
    for n in (1, 2, 4, 8, 16, 32):
        off = (s // (2 * n) == t // (2 * n)) & (s % (2 * n) >= n) & (t % (2 * n) < n)
        levels += [off, off.T]
    CONST2(c, "level")[:] = np.concatenate(levels, 1)
    CONST2(c, "headones")[:] = s // HD == t // HD
    CONST2(c, "headsum")[:] = s // HD == np.arange(2)[None]
    CONST2(c, "reset")[:] = (np.arange(SEQ)[None] % CH != 0)
    CONST2(c, "glamask")[:] = s // (P // H) == np.arange(W)[None] // HD
    return c


def const3():
    c = np.zeros((P, CONST3.width), np.float32)
    s, t = np.arange(P)[:, None], np.arange(P)[None]
    CONST3(c, "before")[:] = s < t
    CONST3(c, "iota")[:] = t
    CONST3(c, "expert")[:] = s
    return c


def const4():
    c = np.zeros((P, CONST4.width), np.float32)
    s, t = np.arange(P)[:, None], np.arange(P)[None]

    def pool(w, s, t, first=False):
        count = np.minimum(t + 1, w) if first else w
        return ((s <= t) & (s > t - w)) / count - (s == t)

    for g, w in enumerate(WINDOWS):
        CONST4(c, "pool", g * P, (g + 1) * P)[:] = pool(w, s, t)
        CONST4(c, "pool_before", g * P, (g + 1) * P)[:] = pool(w, s - P, t)
        CONST4(c, "pool_meta", g * P, (g + 1) * P)[0:META] = pool(w, s[0:META] - META, t)
        CONST4(c, "pool_first", g * META, (g + 1) * META)[0:META] = pool(w, s[0:META], t[:, 0:META], True)
    freq = 10000.0 ** (-np.arange(24) / 24)
    for i in range(NT2):
        angle = (OFF[i] + np.arange(SIZE[i]))[:, None] * freq[None]
        CONST4(c, "cos", i * 24, (i + 1) * 24)[0:SIZE[i]] = np.cos(angle)
        CONST4(c, "sin", i * 24, (i + 1) * 24)[0:SIZE[i]] = np.sin(angle)
    CONST4(c, "row_causal")[:] = np.where(t <= s, 0.0, NEG)
    return c


def retention_decay():
    s, t = np.arange(P)[:, None], np.arange(LEN)[None]
    gamma = 1.0 - 2.0 ** (-5.0 - np.arange(RH))
    return np.concatenate([np.where(t >= s, g ** np.maximum(t - s, 0) * RK ** -0.5, 0.0) for g in gamma], 1).astype(np.float32)


class Steps:

    def __init__(self, engine, own):
        self.engine, self.own, self.count, self.last = engine, own, {}, None

    def did(self, instruction, sem=None):
        sem = self.own if sem is None else sem
        instruction.then_inc(sem, 1)
        self.count[sem.name] = self.count.get(sem.name, 0) + 1
        self.last = (sem, self.count[sem.name])
        return self.count[sem.name]

    def settle(self):
        self.engine.wait_ge(*self.last)


class Turn:

    def __init__(self, engine, i, own, per, credit, passed=None):
        self.engine, self.i, self.own, self.per, self.credit, self.passed = engine, i, own, per, credit, passed
        self.count, self.last = {}, None

    def value(self, sem, n):
        return self.i * self.per[sem.name] + (self.credit.get(sem.name, 0) + n)

    def wait(self, sem, n):
        self.engine.wait_ge(sem, self.value(sem, n))

    def did(self, instruction, sem=None):
        sem = self.own if sem is None else sem
        instruction.then_inc(sem, 1)
        self.count[sem.name] = self.count.get(sem.name, 0) + 1
        assert self.count[sem.name] <= self.per[sem.name]
        self.last = (sem, self.count[sem.name])

    def settle(self):
        self.wait(*self.last)

    def hold(self):
        self.engine.sem_inc(self.passed, 1)

    def check(self):
        for name, n in self.count.items():
            assert n == self.per[name], (name, n)


class TurnRing:

    def __init__(self, psum, first, filled, drained, banks=3):
        self.psum, self.first, self.filled, self.drained, self.banks = psum, first, filled, drained, banks
        self.sent = self.taken = 0

    def bank(self, turn):
        turn.wait(self.drained, self.sent + 1 - self.banks)
        return self.psum[:, self.first + self.sent % self.banks, :]

    def ship(self, turn, matmul):
        turn.did(matmul, self.filled)
        self.sent += 1
        return self.sent

    def take(self, turn):
        self.taken += 1
        turn.wait(self.filled, self.taken)
        return self.psum[:, self.first + (self.taken - 1) % self.banks, :]


class BankRing:

    def __init__(self, psum, first, filled, drained, banks=3):
        self.psum, self.first, self.filled, self.drained, self.banks = psum, first, filled, drained, banks
        self.sent = self.taken = 0

    def bank(self, pe):
        if self.sent >= self.banks:
            pe.wait_ge(self.drained, self.sent - self.banks + 1)
        return self.psum[:, self.first + self.sent % self.banks, :]

    def ship(self, matmul):
        matmul.then_inc(self.filled, 1)
        self.sent += 1
        return self.sent

    def take(self, engine):
        self.taken += 1
        engine.wait_ge(self.filled, self.taken)
        return self.psum[:, self.first + (self.taken - 1) % self.banks, :]


def build(nc, io):
    with ExitStack() as ctx:
        sems = {}

        def sem(name):
            if name not in sems:
                sems[name] = ctx.enter_context(nc.semaphore(name))
            return sems[name]

        def sb(name, words):
            return ctx.enter_context(nc.sbuf_tensor(name, [P, words], F32))

        ring = sb("weight_ring", SLOTS * PIECE)
        arena_words = 28600
        arena = sb("arena", arena_words)
        psum = ctx.enter_context(nc.psum_tensor("psum", [P, 8, 512], F32))
        used = [0]

        def take(words):
            at = used[0]
            used[0] += words
            assert used[0] <= arena_words, (used[0], arena_words)
            return arena[:, at:at + words]

        slot = [ring[:, s * PIECE:(s + 1) * PIECE].rearrange("p (k n) -> p k n", k=KT) for s in range(SLOTS)]

        c1 = take(CONST1.width)
        cols = take(COLS.width)
        rows = take(ROWS.width)
        lora_up = take(W)
        gate_up = take(P)
        y = take(TT * D).rearrange("p (t d) -> p t d", t=TT)
        small = take(256)
        u_tok = take(TT * NT).rearrange("p (t n) -> p t n", t=TT)
        u_feat = take(NF * (PAD + SEQ)).rearrange("p (i s) -> p i s", i=NF)
        mixer_base = used[0]
        ident = CONST1(c1, "ident")
        ones = CONST1(c1, "ones")
        x_t = take(KT * SEQ).rearrange("p (k s) -> p k s", k=KT)
        used[0] = mixer_base
        hrow = take(6 * SEQ).rearrange("p (r s) -> p r s", r=6)
        row_cast = take(2 * SEQ).rearrange("p (r s) -> p r s", r=2)
        decay = take(2 * SEQ).rearrange("p (r s) -> p r s", r=2)
        weigh = take(2 * SEQ).rearrange("p (r s) -> p r s", r=2)
        xs_tok = y[:, :, 256:512]
        feat_flat = u_feat.rearrange("p i s -> p (i s)")
        norm_tmp = feat_flat[:, 0:TT * W]
        used[0] = mixer_base
        c2 = take(CONST2.width)
        spare = take(3600)
        gla_la, gla_cum, gla_tmp = (spare[:, i * SEQ:(i + 1) * SEQ] for i in range(3))
        gla_kdec = spare[:, 3 * SEQ:4 * SEQ].rearrange("p (t c) -> p t c", t=TT)
        gla_st = spare[:, 4 * SEQ:6 * SEQ].rearrange("p (b h s) -> p b h s", b=2, h=H)
        gla_state = feat_flat[:, 1024:1024 + 8 * W].rearrange("p (c d) -> p c d", c=8)
        gla_eb = small[:, 96:104]
        r_at = feat_flat[:, 0:2048].rearrange("p (t f k s) -> p t f k s", t=TT, f=2, k=2)
        r_bk = feat_flat[:, 2048:4096].rearrange("p (k t f s) -> p k t f s", k=2, t=TT, f=2)
        r_tmp = feat_flat[:, 4096:5120].rearrange("p (t f s) -> p t f s", t=TT, f=2)
        r_dec = spare[:, 0:2048].rearrange("p (k t f s) -> p k t f s", k=2, t=TT, f=2)
        r_lw, r_cw = r_dec[:, 0], r_dec[:, 1]
        r_kk = spare[:, 2048:3072].rearrange("p (t f s) -> p t f s", t=TT, f=2)
        r_a, r_t1, r_t2 = (u_tok[:, :, c:c + W].rearrange("p t (f s) -> p t f s", f=2) for c in (512, 768, 1024))
        g_tok, v_tok = u_tok[:, :, 0:W], u_tok[:, :, W:2 * W]
        r_wl = small[:, 104:120].rearrange("p (t f c) -> p t f c", t=TT, f=2)
        r_bonus = small[:, 120:136].rearrange("p (t h) -> p t h", t=TT)
        r_omka = small[:, 136:138]
        c_area = feat_flat[:, F_RWKV * (PAD + SEQ):(F_RWKV + 7) * (PAD + SEQ)]
        r_mt = c_area[:, 0:2048].rearrange("p (f k g q s) -> p f k g q s", f=2, k=2, g=2, q=2)
        r_x, r_xt, r_prod = (c_area[:, 2048 + i * 512:2560 + i * 512].rearrange("p (h s) -> p h s", h=H) for i in range(3))
        r_anv, r_xau, r_mot, r_mlo = (u_tok[:, :, 512 + i * P:512 + (i + 1) * P] for i in range(4))
        r_dtok = u_tok[:, :, 1024:1024 + P]
        r_rot = spare[:, 2048:2304].rearrange("p (f s) -> p f s", f=2)
        r_gt = spare[:, 2304:2816].rearrange("p (c f v) -> p c f v", c=2, f=2)
        r_state = spare[:, 2816:3584].rearrange("p (n f v) -> p n f v", n=3, f=2)
        r_atm = feat_flat[:, 4096:5120].rearrange("p (f g k s) -> p f g k s", f=2, g=2, k=2)
        gla_qm = y[:, :, W:2 * W].rearrange("p b (h s) -> p b h s", h=2)
        R_DT, R_NF, R_M, R_F, R_G, R_A = range(6)
        hcol = small[:, 0:64].rearrange("p (k t h) -> p k t h", k=4, t=TT)
        expa = small[:, 64:65]
        den = small[:, 68:72]
        stat = small[:, 80:96]

        at_y = CONST1.width + COLS.width + ROWS.width + W + P
        at_tok = at_y + TT * D + 256
        at_feat = at_tok + TT * NT
        at_mix = at_feat + NF * (PAD + SEQ)
        ffn = y
        x1 = arena[:, at_tok:at_tok + TT * D].rearrange("p (t d) -> p t d", t=TT)
        y_t = arena[:, at_feat:at_feat + KT * SEQ].rearrange("p (k s) -> p k s", k=KT)
        x1_t = arena[:, at_mix:at_mix + KT * SEQ].rearrange("p (k s) -> p k s", k=KT)
        ln_par = arena[:, at_mix + KT * SEQ:at_mix + KT * SEQ + 2 * D].rearrange("p (k d) -> p k d", k=2)
        used[0] = at_mix + KT * SEQ + 2 * D
        router_w = take(KT * E).rearrange("p (k e) -> p k e", k=KT)
        router_b = take(E)
        block_expert = take(NB).bitcast(mybir.dt.int32)
        block_count = take(1).bitcast(mybir.dt.int32)
        ln_stats = take(5 * 12).rearrange("p (t s) -> p t s", t=5)
        ln_mean = take(5 * 2).rearrange("p (t s) -> p t s", t=5)
        used[0] = at_feat + KT * SEQ
        c3 = take(CONST3.width)
        b_down = take(D)
        to_block, from_block = (take(TT * P).rearrange("p (t r) -> p t r", t=TT) for _ in range(2))
        from_t = take(TT * P)
        gates, assigned, logits, pos = (take(TT * E).rearrange("p (t e) -> p t e", t=TT) for _ in range(4))
        gates_t = take(SEQ)
        pos_t = take(SEQ)
        top, top_i, gate4 = (take(TT * 8).rearrange("p (t e) -> p t e", t=TT) for _ in range(3))
        rank = take(16)
        hot, base_w = take(NB), take(NB)
        block_pos, block_gate = (take(TT * NB).rearrange("p (t n) -> p t n", t=TT) for _ in range(2))
        used[0] = at_feat
        xg = take(KT * P).rearrange("p (k r) -> p k r", k=KT)
        hid = take(D)
        hid_t = take(KT * P).rearrange("p (k r) -> p k r", k=KT)
        y_blk = take(D)
        b_gu = arena[:, at_mix:at_mix + 2 * D]
        swi = arena[:, at_mix + 2 * D:at_mix + 2 * D + 1024]
        h_t = y_t
        p_t = arena[:, at_mix + 2 * D:at_mix + 2 * D + 2 * SEQ].rearrange("p (k s) -> p k s", k=2)
        ple_gate = arena[:, at_mix:at_mix + TT * 512].rearrange("p (b s) -> p b s", b=TT)
        ev_ring = TurnRing(psum, 0, sem("expert_vector_filled"), sem("expert_vector_drained"))
        ea_ring = TurnRing(psum, 3, sem("expert_scalar_filled"), sem("expert_scalar_drained"))
        expert_landed = [sem(f"expert_landed_{k}") for k in range(6)]
        landed2 = [sem(f"late_weights_landed_{k}") for k in range(SLOTS)]
        slot_free2 = {}
        hidden_ready, swish_asked, swish_given = sem("hidden_ready"), sem("swish_asked"), sem("swish_given")
        to_ready, from_ready, bias_landed = sem("to_block_ready"), sem("from_block_ready"), sem("bias_landed")
        PER = {ev_ring.filled.name: 12, ev_ring.drained.name: 12, ea_ring.filled.name: 9, ea_ring.drained.name: 9,
               hidden_ready.name: 4, swish_asked.name: 4, swish_given.name: 4, to_ready.name: 1, from_ready.name: 1,
               bias_landed.name: 16, **{x.name: 16 for x in expert_landed}}
        CREDIT = {ev_ring.drained.name: 3, ea_ring.drained.name: 3}

        used[0] = CONST1.width
        rows2 = take(ROWS2.width)
        assert used[0] <= at_y - D
        h2 = arena[:, at_y - D:at_y + TT * D].rearrange("p (t d) -> p t d", t=NT2)
        used[0] = at_y + TT * D
        small2 = take(200)
        h2_t = take(KT * LEN)
        retained = h2_t[:, 0:4 * LEN].rearrange("p (h s) -> p h s", h=4)
        rotated = h2_t[:, 4 * LEN:8 * LEN].rearrange("p (u s) -> p u s", u=4)
        fox_c = h2_t[:, 0:2 * LEN].rearrange("p (b s) -> p b s", b=2)
        fox_p = h2_t[:, 2 * LEN:4 * LEN].rearrange("p (b s) -> p b s", b=2)
        fox_pt = h2_t[:, 4 * LEN:4 * LEN + 2 * NT2 * P].rearrange("p (b j s) -> p b j s", b=2, j=NT2)
        h2_t = h2_t.rearrange("p (k s) -> p k s", k=KT)
        at_qk = used[0]
        qk_f = take(6 * LEN).rearrange("p (u s) -> p u s", u=6)
        u2 = take(NT2 * NU).rearrange("p (t n) -> p t n", t=NT2)
        ff_t = arena[:, at_qk:at_qk + FT * LEN].rearrange("p (f s) -> p f s", f=FT)
        assert at_qk + FT * LEN <= used[0]
        c4 = take(CONST4.width)
        pool_w = take(4 * HD).rearrange("p (u d) -> p u d", u=2)
        f_w = take(KT * FH).rearrange("p (k h) -> p k h", k=KT)
        f_b = take(1)
        ln_par2 = arena[:, used[0]:used[0] + 2 * D].rearrange("p (k d) -> p k d", k=2)
        f_row = take(2 * LEN).rearrange("p (r s) -> p r s", r=2)
        work = take(2 * 512).rearrange("p (b s) -> p b s", b=2)
        c_col = small2[:, 0:NT2 * FH].rearrange("p (t h) -> p t h", t=NT2)
        stat2 = small2[:, 32:52]
        row_max, row_sum = small2[:, 52:54], small2[:, 54:56]
        lv_ring = TurnRing(psum, 0, sem("layer_vector_filled"), sem("layer_vector_drained"))
        la_ring = TurnRing(psum, 3, sem("layer_scalar_filled"), sem("layer_scalar_drained"))

        layer_landed = [sem(f"layer_weights_landed_{s}") for s in range(SLOTS)]
        layer_free, layer_mark = {}, {}
        LATE = (3 + 3) % SLOTS
        PARTS = ((META, slice(0, 1)), (P, slice(1, NT2)))
        SEGMENTS = [(0, 0, OFF[3]), (0, OFF[3], LEN)] + [(i, OFF[i], LEN) for i in range(1, NT2)]
        FOX_TURNED = []
        for n in range(FH * NT2):
            FOX_TURNED.append((FOX_TURNED[-1] if n else 0) + (2 if n % NT2 == NT2 - 1 else 1))
        LAYER_PER = LAYER_SIGNALS
        LAYER_CREDIT = {lv_ring.drained.name: 3, la_ring.drained.name: 3, "retained_drained": 2, "fox_turned_drained": 2,
                        "fox_out_drained": 2}

        v_ring = BankRing(psum, 0, sem("vector_bank_filled"), sem("vector_bank_drained"))
        a_ring = BankRing(psum, 3, sem("scalar_bank_filled"), sem("scalar_bank_drained"))
        x_landed, setup_landed = sem("x_landed"), sem("setup_landed")
        landed = [sem(f"weights_landed_{s}") for s in range(SLOTS)]
        dve_step, act_step = sem("vector_step"), sem("scalar_step")
        conv_summed, conv_ready = sem("conv_summed"), sem("conv_ready")
        rows_biased, rows_softplus, hrow_ready, hcol_ready = sem("rows_biased"), sem("rows_softplus"), sem("hrow_ready"), sem("hcol_ready")
        decay_arg, decay_ready, pv_done = sem("decay_arg"), sem("decay_ready"), sem("pv_done")
        sums_drained = sem("sums_drained")
        z_ready, stat_sum, stat_root = sem("z_ready"), sem("stat_sum"), sem("stat_root")
        out_landed = sem("out_landed")

        SETUP = [(c1, "const1"), (cols, "cols"), (rows, "rows"), (lora_up, "lora_up"), (gate_up, "gate_up")]
        slot_free = {}
        mark = {}

        def heads_of(view, n):
            return view.rearrange("p t (h d) -> p t h d", h=n)

        block = ctx.enter_context(nc.Block())

        @block.tensor
        def _(pe):
            def piece(n):
                pe.wait_ge(landed[n % SLOTS], 16 * (n // SLOTS + 1))
                return slot[n % SLOTS]

            def transpose(out, in_, parts=P):
                return pe.transpose(out, in_, ident[0:parts, 0:parts] if parts < P else ident)

            def project_block1():
                pe.wait_ge(x_landed, 16)
                for i in range(NF):
                    w = piece(i // 4)
                    bank = v_ring.bank(pe)
                    for k in range(KT):
                        mm = pe.matmul(bank, w[:, k, i % 4 * P:(i % 4 + 1) * P], x_t[:, k, :],
                                       start=(k == 0), stop=(k == KT - 1))
                    slot_free[i // 4] = (v_ring.filled, v_ring.ship(mm))
                for n, a, width in ((4, 256, 256), (5, 0, 512), (6, 0, 512)):
                    w = piece(n)
                    for t in range(TT):
                        bank = a_ring.bank(pe)
                        for k in range(KT):
                            mm = pe.matmul(bank[:, 0:width], x_t[:, k, t * P:(t + 1) * P], w[:, k, a:a + width],
                                           start=(k == 0), stop=(k == KT - 1))
                        slot_free[n] = (a_ring.filled, a_ring.ship(mm))
                mark["projected"] = a_ring.sent

            def head_columns():
                pe.wait_ge(setup_landed, 16 * len(SETUP))
                pe.wait_ge(hrow_ready, 1)
                bank = v_ring.bank(pe)
                for kind, r in enumerate((R_DT, R_A, R_G, R_F)):
                    for t in range(TT):
                        mm = transpose(bank[:, kind * 16 + t * 4:kind * 16 + t * 4 + 4],
                                       hrow[0:4, r, t * P:(t + 1) * P], 4)
                v_ring.ship(mm)

            def ssd_values():
                pe.wait_ge(conv_ready, 2)
                for t in range(TT):
                    bank = v_ring.bank(pe)
                    for i in range(2):
                        mm = transpose(bank[:, i * P:(i + 1) * P], u_feat[:, F_SSD + i, PAD + t * P:PAD + (t + 1) * P])
                    v_ring.ship(mm)
                mark["ssd_values"] = v_ring.sent

            def decayed_attention():
                waiting = []

                def weigh_values():
                    n, job = waiting.pop(0)
                    g, i = n // TT, n % TT
                    m, h = g // H, g % H
                    sums = psum[:, 6 + g % 2, :]
                    pe.wait_ge(v_ring.drained, job)
                    if i == 0 and g >= 2:
                        pe.wait_ge(sums_drained, g - 1)
                    for j in range(i, TT):
                        keys = weigh[:, n % 2, (j - i) * P:(j - i + 1) * P]
                        values = (xs_tok[:, i, h * HD:(h + 1) * HD] if m == 0
                                  else u_tok[:, i, T_MV + h * HD:T_MV + (h + 1) * HD])
                        mm = pe.matmul(sums[:, j * HD:(j + 1) * HD], keys, values, start=(i == 0 and j == 0),
                                       stop=(i == TT - 1), skip_group_check=True)
                        if m == 1:
                            mm = pe.matmul(sums[:, TT * HD + j:TT * HD + j + 1], keys, ones[:, 0:1], start=False,
                                           stop=(i == TT - 1), skip_group_check=True)
                    mm.then_inc(pv_done, 1)

                for g in range(2 * H):
                    m, h = g // H, g % H
                    bank = v_ring.bank(pe)
                    v_ring.ship(pe.matmul(bank, CONST1(c1, "select", h * P, (h + 1) * P)[0:4, :],
                                          hrow[0:4, R_A if m == 0 else R_M, :], start=True, stop=True))
                    for i in range(TT):
                        if m == 0:
                            keys, queries = u_feat[:, F_SSD + 2, :], u_feat[:, F_SSD + 3, :]
                        else:
                            half = slice(h % 2 * HD, h % 2 * HD + HD)
                            keys, queries = u_feat[half, F_MQK + 2 + h // 2, :], u_feat[half, F_MQK + h // 2, :]
                        pe.wait_ge(conv_ready, 4 if m == 0 else 8)
                        bank = v_ring.bank(pe)
                        mm = pe.matmul(bank[:, 0:SEQ - i * P], keys[:, PAD + i * P:PAD + (i + 1) * P],
                                       queries[:, PAD + i * P:PAD + SEQ], start=True, stop=True)
                        waiting.append((g * TT + i, v_ring.ship(mm)))
                        if len(waiting) > 1:
                            weigh_values()
                weigh_values()

            project_block1()
            head_columns()
            ssd_values()
            decayed_attention()

            def gla():
                pe.wait_ge(sem("const2_landed"), 16)
                ready = sem("gla_ready")
                bank = v_ring.bank(pe)
                v_ring.ship(pe.matmul(bank, gate_up[96:112, :], u_feat[96:112, F_ROWS, PAD:], start=True, stop=True))
                q, k = u_feat[:, F_GLA, PAD:], u_feat[:, F_GLA + 1, PAD:]
                pe.wait_ge(ready, 2)
                bank = v_ring.bank(pe)
                for t in range(TT):
                    mm = transpose(bank[:, t * P:(t + 1) * P], gla_tmp[:, t * P:(t + 1) * P])
                kdec_job = v_ring.ship(mm)
                scored = []

                def scores(t):
                    bank = v_ring.bank(pe)
                    pe.wait_ge(sem("gla_masked"), t + 1)
                    scored.append(v_ring.ship(pe.matmul(bank, k[:, t * P:(t + 1) * P], gla_qm[:, t % 2 * 2:t % 2 * 2 + 2],
                                                        start=True, stop=True)))

                pe.wait_ge(v_ring.drained, kdec_job)
                for c in range(7):
                    half = slice(c % 2 * CH, c % 2 * CH + CH)
                    bank = v_ring.bank(pe)
                    job = v_ring.ship(pe.matmul(bank[:, 0:W], gla_kdec[half, c // 2, :],
                                                u_tok[half, c // 2, T_GV:T_GV + W], start=True, stop=True))
                scores(0)
                pe.wait_ge(ready, 3)
                for t in range(TT):
                    if t + 1 < TT:
                        scores(t + 1)
                    pe.wait_ge(v_ring.drained, scored[t])
                    bank = v_ring.bank(pe)
                    for h in range(H):
                        pe.matmul(bank[:, h * HD:(h + 1) * HD], gla_st[:, t % 2, h, :], u_tok[:, t, T_GV + h * HD:T_GV + (h + 1) * HD],
                                  start=(h == 0), stop=False, skip_group_check=True)
                    for c in range(2):
                        at = t * P + c * CH
                        mm = pe.matmul(bank[c * CH:(c + 1) * CH, 0:W], q[:, at:at + CH], gla_state[:, 2 * t + c, :],
                                       start=False, stop=True, skip_group_check=True)
                    v_ring.ship(mm)

            def rwkv_features():
                lora = u_feat[:, F_RWKV + 6, PAD:]
                pe.wait_ge(sem("lora_ready"), 2)
                for part in (slice(0, 32), slice(32, 64)):
                    for f in range(2):
                        bank = a_ring.bank(pe)
                        a_ring.ship(pe.matmul(bank, lora_up[part, f * P:(f + 1) * P], lora[part, :], start=True, stop=True))
                for t in range(TT):
                    bank = a_ring.bank(pe)
                    a_ring.ship(pe.matmul(bank[:, 0:W], lora[64:128, t * P:(t + 1) * P], lora_up[64:128, :], start=True, stop=True))
                for t in range(TT):
                    bank = v_ring.bank(pe)
                    for f in range(2):
                        mm = transpose(bank[:, f * P:(f + 1) * P], u_feat[:, F_RWKV + 4 + f, PAD + t * P:PAD + (t + 1) * P])
                    v_ring.ship(mm)
                ready = sem("rwkv_ready")
                pe.wait_ge(ready, 1)
                for t in range(TT // 2):
                    bank = a_ring.bank(pe)
                    a_ring.ship(pe.matmul(bank, CONST2(c2, "headones"), r_tmp[:, 2 * t:2 * t + 2, :, :], start=True, stop=True))
                pe.wait_ge(ready, 2)
                bank = v_ring.bank(pe)
                for t in range(TT):
                    for f in range(2):
                        mm = pe.matmul(bank[:, t * H + 2 * f:t * H + 2 * f + 2], r_tmp[:, t, f, :], CONST2(c2, "headsum"), start=True, stop=True)
                v_ring.ship(mm)
                pe.wait_ge(ready, 3)

            def rwkv_tile(t):
                half = [slice(h % 2 * HD, h % 2 * HD + HD) for h in range(H)]
                pe.wait_ge(sem("rwkv_masked"), t + 1)
                for f in range(2):
                    for kind in range(2):
                        bank = v_ring.bank(pe)
                        inner = v_ring.ship(pe.matmul(bank, r_bk[:, kind, t, f, :], r_atm[:, f], start=True, stop=True))
                bank = v_ring.bank(pe)
                for h in range(H):
                    mm = pe.matmul(bank[:, h * P:(h + 1) * P], r_atm[:, h // 2, h % 2, 0, :], r_bk[:, 0, t, h // 2, :],
                                   start=True, stop=True)
                v_ring.ship(mm)
                bank = v_ring.bank(pe)
                for f in range(2):
                    mm = transpose(bank[:, f * P:(f + 1) * P], r_at[:, t, f, 0, :])
                v_ring.ship(mm)
                bank = v_ring.bank(pe)
                for kind in range(2):
                    for f in range(2):
                        n = 2 * kind + f
                        mm = transpose(bank[:, n * P:(n + 1) * P], r_dec[:, kind, t, f, :])
                v_ring.ship(mm)
                pe.wait_ge(v_ring.drained, inner)
                bank = v_ring.bank(pe)
                for h in range(H):
                    mm = pe.matmul(bank[:, h * HD:(h + 1) * HD], r_mt[:, h // 2, 1, h % 2, 0, :], v_tok[:, t, h * HD:(h + 1) * HD], start=True, stop=True)
                nv = v_ring.ship(mm)
                levels = sem("level_ready")
                for n in range(1, 6):
                    pe.wait_ge(levels, 5 * t + n)
                    bank = v_ring.bank(pe)
                    for h in range(H):
                        mm = pe.matmul(bank[:, h * P:(h + 1) * P], r_mot[:, h, :], r_x[:, h, :], start=True, stop=True)
                    job = v_ring.ship(mm)
                    pe.wait_ge(v_ring.drained, job)
                    if n < 5:
                        bank = v_ring.bank(pe)
                        for h in range(H):
                            mm = pe.matmul(bank[:, h * P:(h + 1) * P], r_xt[:, h, :], r_prod[:, h, :], start=True, stop=True)
                        v_ring.ship(mm)
                    bank = v_ring.bank(pe)
                    for h in range(H):
                        mm = pe.matmul(bank[:, h * P:(h + 1) * P], r_prod[:, h, :], r_xt[:, h, :], start=True, stop=True)
                    job = v_ring.ship(mm)
                pe.wait_ge(v_ring.drained, job)
                bank = v_ring.bank(pe)
                for h in range(H):
                    mm = pe.matmul(bank[:, h * P:(h + 1) * P], r_xt[:, h, :], r_anv[:, h, :], start=True, stop=True)
                job = v_ring.ship(mm)
                pe.wait_ge(v_ring.drained, job)
                bank = v_ring.bank(pe)
                for h in range(H):
                    mm = pe.matmul(bank[half[h], h // 2 * P:(h // 2 + 1) * P], r_xau[:, h, 0:HD], r_mt[:, h // 2, 0, h % 2, 1, :], start=True, stop=True,
                                   skip_group_check=True)
                v_ring.ship(mm)
                for c in range(2):
                    bank = v_ring.bank(pe)
                    chunk = slice(c * CH, (c + 1) * CH)
                    for h in range(H):
                        at = h // 2 * HD
                        mm = pe.matmul(bank[half[h], at:at + HD], r_xau[chunk, h, 0:HD], r_dtok[chunk, h // 2, h % 2 * HD:(h % 2 + 1) * HD],
                                       start=True, stop=True, skip_group_check=True)
                    gt_job = v_ring.ship(mm)
                out = psum[:, 6 + t % 2, :]
                if t >= 2:
                    pe.wait_ge(sem("rwkv_out_drained"), t - 1)
                for h in range(H):
                    o = out[:, h * HD:(h + 1) * HD]
                    pe.matmul(o, r_mt[:, h // 2, 0, h % 2, 1, :], r_xau[:, h, HD:P], start=(h == 0), stop=False, skip_group_check=True)
                    pe.matmul(o, r_mt[:, h // 2, 1, h % 2, 1, :], v_tok[:, t, h * HD:(h + 1) * HD], start=False, stop=False, skip_group_check=True)
                for c in range(2):
                    chunk = slice(c * CH, (c + 1) * CH)
                    bank = v_ring.bank(pe)
                    pe.wait_ge(v_ring.drained, gt_job)
                    pe.wait_ge(sem("state_ready"), 2 * t + c + 1)
                    state = r_state[:, (2 * t + c) % 3]
                    for f in range(2):
                        pe.matmul(bank[:, f * P:(f + 1) * P], r_gt[:, c, f, :], state[:, f, :], start=(f == 0), stop=False,
                                  skip_group_check=True)
                    for h in range(H):
                        at = h * HD
                        cols_of = slice(h % 2 * HD, (h % 2 + 1) * HD)
                        pe.matmul(bank[half[h], at:at + HD], r_dtok[chunk, h // 2, cols_of], r_xau[chunk, h, HD:P],
                                  start=False, stop=False, skip_group_check=True)
                        mm = pe.matmul(bank[half[h], at:at + HD], r_dtok[chunk, 2 + h // 2, cols_of], v_tok[chunk, t, h * HD:(h + 1) * HD],
                                       start=False, stop=True, skip_group_check=True)
                    v_ring.ship(mm)
                    for f in range(2):
                        mm = pe.matmul(out[chunk, f * P:(f + 1) * P], r_rot[:, f, chunk], state[:, f, :],
                                       start=False, stop=True, skip_group_check=True)
                mm.then_inc(sem("rwkv_out_filled"), 1)

            gla()
            rwkv_features()
            for t in range(TT):
                rwkv_tile(t)

            def transposed_rows(source, ready):
                for t in range(TT):
                    if ready is not None:
                        pe.wait_ge(ready, t + 1)
                    for half in range(2):
                        bank = a_ring.bank(pe)
                        for k in range(4):
                            mm = transpose(bank[:, k * P:(k + 1) * P], source[:, t, (4 * half + k) * P:(4 * half + k + 1) * P])
                        job = a_ring.ship(mm)
                return job

            def mix_out():
                pe.wait_ge(sem("mixed"), 1)
                pe.wait_ge(a_ring.drained, transposed_rows(y, None))
                for half in range(2):
                    w = piece(7 + half)
                    for t in range(TT):
                        bank = v_ring.bank(pe)
                        for k in range(KT):
                            mm = pe.matmul(bank, y_t[:, k, t * P:(t + 1) * P], w[:, k, :], start=(k == 0), stop=(k == KT - 1))
                        slot_free[7 + half] = (v_ring.filled, v_ring.ship(mm))

            def route():
                before, iota, expert = (CONST3(c3, n) for n in ("before", "iota", "expert"))
                routed = sem("routed")
                pe.wait_ge(sem("router_landed"), 16 * 4)
                pe.wait_ge(a_ring.drained, transposed_rows(x1, sem("x1_ready")))
                bank = v_ring.bank(pe)
                for t in range(TT):
                    for k in range(KT):
                        mm = pe.matmul(bank[:, t * E:(t + 1) * E], x1_t[:, k, t * P:(t + 1) * P], router_w[:, k, :],
                                       start=(k == 0), stop=(k == KT - 1), skip_group_check=True)
                v_ring.ship(mm)
                pe.wait_ge(routed, 1)
                bank = v_ring.bank(pe)
                for t in range(TT):
                    mm = transpose(bank[0:E, t * P:(t + 1) * P], gates[:, t, :])
                v_ring.ship(mm)
                bank = v_ring.bank(pe)
                for t in range(TT):
                    for u in range(t + 1):
                        mm = pe.matmul(bank[:, t * E:(t + 1) * E], before if u == t else ones, assigned[:, u, :],
                                       start=(u == 0), stop=(u == t), skip_group_check=True)
                v_ring.ship(mm)
                bank = v_ring.bank(pe)
                for t in range(TT):
                    mm = pe.matmul(bank[0:E, 0:1], assigned[:, t, :], ones[:, 0:1], start=(t == 0), stop=(t == TT - 1))
                v_ring.ship(mm)
                pe.wait_ge(routed, 2)
                bank = v_ring.bank(pe)
                for t in range(TT):
                    mm = transpose(bank[0:E, t * P:(t + 1) * P], pos[:, t, :])
                v_ring.ship(mm)
                bank = v_ring.bank(pe)
                pe.matmul(bank[0:E, 0:3], before[0:E, 0:E], rank[0:E, 0:3], start=True, stop=False, skip_group_check=True)
                mm = pe.matmul(bank[0:E, 0:3], ones[0:E, 0:E], rank[0:E, 3:6], start=False, stop=True, skip_group_check=True)
                v_ring.ship(mm)
                bank = v_ring.bank(pe)
                v_ring.ship(pe.matmul(bank[:, 0:1], ones[0:E, :], rank[0:E, 6:7], start=True, stop=True))
                pe.wait_ge(routed, 3)
                bank = v_ring.bank(pe)
                pe.matmul(bank[:, 0:NB], expert[0:E, :], hot[0:E, :], start=True, stop=True, skip_group_check=True)
                mm = pe.matmul(bank[:, 64:64 + NB], ones[0:E, :], base_w[0:E, :], start=True, stop=True, skip_group_check=True)
                v_ring.ship(mm)
                for rows_t in (pos_t, gates_t):
                    bank = v_ring.bank(pe)
                    for t in range(TT):
                        mm = pe.matmul(bank[:, t * NB:(t + 1) * NB], rows_t[0:E, t * P:(t + 1) * P], hot[0:E, :], start=True, stop=True,
                                       skip_group_check=True)
                    v_ring.ship(mm)
                for t in range(TT):
                    for half in range(2):
                        bank = v_ring.bank(pe)
                        v_ring.ship(pe.matmul(bank, gates_t[0:E, t * P:(t + 1) * P], b_down[0:E, half * 512:(half + 1) * 512],
                                              start=True, stop=True))

            def gather(half, bank):
                for k in range(4 * half, 4 * half + 4):
                    for t in range(TT):
                        mm = pe.matmul(bank[:, k % 4 * P:(k % 4 + 1) * P], x1[:, t, k * P:(k + 1) * P], to_block[:, t, :],
                                       start=(t == 0), stop=(t == TT - 1), skip_group_check=True)
                return mm

            def experts():
                pe.wait_ge(sem("first_block_ready"), 1)
                for half in range(2):
                    bank = a_ring.bank(pe)
                    job = a_ring.ship(gather(half, bank))
                pe.wait_ge(a_ring.drained, job)
                pe.wait_ge(v_ring.drained, v_ring.sent)
                blocks = pe.value_load(block_count[0:1, 0:1], min_val=E, max_val=NB - 1)
                with pe.Fori(0, blocks) as i:
                    T = Turn(pe, i, None, PER, CREDIT)
                    ev_ring.sent = ea_ring.sent = 0

                    def gate_up(c):
                        T.wait(expert_landed[c], 16)
                        bank = ev_ring.bank(T)
                        w = slot[(3 + c) % SLOTS]
                        for k in range(KT):
                            mm = pe.matmul(bank, xg[:, k, :], w[:, k, :], start=(k == 0), stop=(k == KT - 1))
                        ev_ring.ship(T, mm)

                    def turn_hidden(c):
                        T.wait(hidden_ready, c + 1)
                        bank = ea_ring.bank(T)
                        for k in range(2):
                            mm = transpose(bank[:, k * P:(k + 1) * P], hid[:, (2 * c + k) * P:(2 * c + k + 1) * P])
                        return ea_ring.ship(T, mm)

                    def down(half):
                        T.wait(expert_landed[4 + half], 16)
                        bank = ea_ring.bank(T)
                        w = slot[(7 + half) % SLOTS]
                        for k in range(KT):
                            mm = pe.matmul(bank, hid_t[:, k, :], w[:, k, :], start=(k == 0), stop=(k == KT - 1))
                        return ea_ring.ship(T, mm)

                    T.wait(ea_ring.drained, 0)
                    gate_up(0)
                    gate_up(1)
                    turn_hidden(0)
                    gate_up(2)
                    turn_hidden(1)
                    gate_up(3)
                    turn_hidden(2)
                    T.wait(from_ready, 1)
                    bank = ea_ring.bank(T)
                    for t in range(TT):
                        mm = transpose(bank[:, t * P:(t + 1) * P], from_block[:, t, :])
                    ea_ring.ship(T, mm)
                    T.wait(to_ready, 1)
                    bank = ea_ring.bank(T)
                    ea_ring.ship(T, gather(0, bank))
                    T.wait(ea_ring.drained, turn_hidden(3))
                    down(0)
                    rows_done = down(1)
                    bank = ea_ring.bank(T)
                    ea_ring.ship(T, gather(1, bank))
                    T.wait(ea_ring.drained, rows_done)
                    for t in range(TT):
                        for half in range(2):
                            bank = ev_ring.bank(T)
                            ev_ring.ship(T, pe.matmul(bank, from_t[:, t * P:(t + 1) * P], y_blk[:, half * 512:(half + 1) * 512],
                                                      start=True, stop=True))
                pe.wait_ge(ev_ring.drained, blocks * 12 + 3)
                pe.wait_ge(ea_ring.drained, blocks * 9 + 3)

            def piece2(n):
                pe.wait_ge(landed2[(3 + n) % SLOTS], 16 * (n // SLOTS + 1))
                return slot[(3 + n) % SLOTS]

            def gated_embedding():
                pe.wait_ge(sem("ffn_ready"), 1)
                pe.wait_ge(a_ring.drained, transposed_rows(ffn, None))
                for half in range(2):
                    w = piece2(half)
                    w_proj = piece2(2)
                    for t in range(TT):
                        bank = a_ring.bank(pe)
                        for k in range(KT):
                            mm = pe.matmul(bank, h_t[:, k, t * P:(t + 1) * P], w[:, k, :], start=(k == 0), stop=(k == KT - 1))
                        slot_free2[half] = (a_ring.filled, a_ring.ship(mm))
                        bank = v_ring.bank(pe)
                        if t == 0 and half == 0:
                            pe.wait_ge(sem("p_landed"), 16)
                        for k in range(2):
                            mm = pe.matmul(bank, p_t[:, k, t * P:(t + 1) * P],
                                           w_proj.rearrange("p k n -> p (k n)")[:, k * D + half * 512:k * D + (half + 1) * 512],
                                           start=(k == 0), stop=(k == 1))
                        slot_free2[2] = (v_ring.filled, v_ring.ship(mm))

            mix_out()
            route()
            experts()
            gated_embedding()

            def layer(T):
                lv_ring.sent = la_ring.sent = 0

                def weights(n):
                    T.wait(layer_landed[n % SLOTS], 16 * (n // SLOTS + 1))
                    return slot[(n + LATE) % SLOTS]

                def products(n, half, lhs, w):
                    for k in range(KT):
                        mm = pe.matmul(n, lhs(k), w(k), start=(k == 0), stop=(k == KT - 1))
                    return mm

                def turned(source, parts, meta_banks=2):
                    for t in range(NT2):
                        n = SIZE[t]
                        banks = 2 if t else meta_banks
                        for b in range(banks):
                            bank = la_ring.bank(T)
                            if t == 0:
                                T.hold()
                            for k in range(KT // banks):
                                at = parts[KT // banks * b + k]
                                mm = transpose(bank[:, k * n:(k + 1) * n], source[0:n, t, at:at + P], n)
                            job = la_ring.ship(T, mm)
                    T.wait(la_ring.drained, job)

                def project():
                    turned(h2, range(0, D, P), 1)
                    for n in range(4):
                        w, width = weights(n), 512 if n < 3 else 256
                        for t in range(NT2):
                            bank = la_ring.bank(T)
                            for k in range(KT):
                                mm = pe.matmul(bank[0:SIZE[t], 0:width], h2_t[:, k, OFF[t]:OFF[t] + SIZE[t]], w[:, k, 0:width],
                                               start=(k == 0), stop=(k == KT - 1))
                            layer_free[n] = (la_ring.filled, la_ring.ship(T, mm))
                    for u in range(6):
                        n, at = (3, 256 + u * P) if u < 2 else (4, (u - 2) * P)
                        w = weights(n)
                        for c in range(2):
                            bank = lv_ring.bank(T)
                            for k in range(KT):
                                mm = pe.matmul(bank[:, 0:HALF], w[:, k, at:at + P], h2_t[:, k, c * HALF:(c + 1) * HALF],
                                               start=(k == 0), stop=(k == KT - 1))
                            layer_free[n] = (lv_ring.filled, lv_ring.ship(T, mm))
                    T.wait(sem("layer_params_landed"), 16 * 5)
                    for c in range(2):
                        bank = lv_ring.bank(T)
                        for k in range(KT):
                            mm = pe.matmul(bank[0:FH, 0:HALF], f_w[:, k, :], h2_t[:, k, c * HALF:(c + 1) * HALF],
                                           start=(k == 0), stop=(k == KT - 1))
                        lv_ring.ship(T, mm)
                    layer_mark["projected"] = lv_ring.sent

                def turn_rotated():
                    for t in range(NT2):
                        T.wait(sem("rotated_ready"), t + 1)
                        bank = lv_ring.bank(T)
                        n = SIZE[t]
                        if t == 0:
                            T.hold()
                        for u in range(4):
                            mm = transpose(bank[:, u * n:(u + 1) * n], work[0:n, t % 2, u * P:(u + 1) * P], n)
                        job = lv_ring.ship(T, mm)
                    T.wait(lv_ring.drained, job)

                def retention():
                    waiting = []

                    def weigh_values():
                        h, i, a, b, seg, job = waiting.pop(0)
                        sums = psum[:, 6 + h % 2, :]
                        T.wait(lv_ring.drained, job)
                        if seg == 0:
                            T.wait(sem("retained_drained"), h - 1)
                        if i == 0:
                            T.hold()
                        for j in range(NT2):
                            if not a <= OFF[j] < b:
                                continue
                            n = SIZE[j]
                            mm = pe.matmul(sums[0:n, j * RV:(j + 1) * RV], work[0:SIZE[i], seg % 2, OFF[j] - a:OFF[j] - a + n],
                                           u2[0:SIZE[i], i, U_V + h * RV:U_V + (h + 1) * RV], start=(i == 0 and j <= 1),
                                           stop=(i == j), skip_group_check=True)
                        T.did(mm, sem("retention_done"))

                    for h in range(RH):
                        half = slice(h % 2 * HD, h % 2 * HD + HD)
                        for seg, (i, a, b) in enumerate(SEGMENTS):
                            bank = lv_ring.bank(T)
                            if i == 0:
                                T.hold()
                            mm = pe.matmul(bank[0:SIZE[i], 0:b - a], rotated[half, 2 + h // 2, OFF[i]:OFF[i] + SIZE[i]],
                                           rotated[half, h // 2, a:b], start=True, stop=True)
                            waiting.append((h, i, a, b, seg, lv_ring.ship(T, mm)))
                            if len(waiting) > 1:
                                weigh_values()
                    weigh_values()

                def pool():
                    for t in reversed(range(NT2)):
                        n = SIZE[t]
                        bank = lv_ring.bank(T)
                        for g in range(4):
                            out = bank[g % 2 * HD:(g % 2 + 1) * HD, g // 2 * n:(g // 2 + 1) * n]
                            u = slice(U_U + g * HD, U_U + (g + 1) * HD)
                            here = CONST4(c4, "pool", g * P, (g + 1) * P) if t else CONST4(c4, "pool_first", g * META, (g + 1) * META)
                            mm = pe.matmul(out, u2[0:n, t, u], here[0:n, :], start=True, stop=(t == 0), skip_group_check=True)
                            if t:
                                m = SIZE[t - 1]
                                before = CONST4(c4, "pool_before" if t > 1 else "pool_meta", g * P, (g + 1) * P)
                                mm = pe.matmul(out, u2[0:m, t - 1, u], before[0:m, :], start=False, stop=True, skip_group_check=True)
                        T.wait(lv_ring.drained, lv_ring.ship(T, mm))
                        for g in range(2):
                            bank = lv_ring.bank(T)
                            lv_ring.ship(T, pe.matmul(bank[0:n, 0:P], work[:, t % 2, g * n:(g + 1) * n], pool_w[:, g, :],
                                                      start=True, stop=True))

                def forget():
                    bank = lv_ring.bank(T)
                    T.hold()
                    for t in range(NT2):
                        mm = transpose(bank[0:SIZE[t], t * FH:(t + 1) * FH], f_row[0:FH, 1, OFF[t]:OFF[t] + SIZE[t]], FH)
                    lv_ring.ship(T, mm)
                    waiting = []
                    turned_jobs = [0]

                    def attend():
                        h, i, n = waiting.pop(0)
                        m = SIZE[i]
                        T.wait(sem("fox_weights_ready"), n + 1)
                        for first, last in ([(0, i + 1)] if i < 4 else [(0, 4), (4, 5)]):
                            bank = psum[:, 4 + turned_jobs[0] % 2, :]
                            T.wait(sem("fox_turned_drained"), turned_jobs[0] - 1)
                            T.hold()
                            for j in range(first, last):
                                mm = transpose(bank[0:SIZE[j], (j - first) * m:(j - first + 1) * m],
                                               fox_p[0:m, n % 2, OFF[j]:OFF[j] + SIZE[j]], m)
                            T.did(mm, sem("fox_turned"))
                            turned_jobs[0] += 1
                        T.wait(sem("fox_turned_drained"), turned_jobs[0])
                        out = psum[0:m, 6 + n % 2, 0:HD]
                        T.wait(sem("fox_out_drained"), n - 1)
                        T.hold()
                        for j in range(i + 1):
                            k = SIZE[j]
                            mm = pe.matmul(out, fox_pt[0:k, n % 2, j, 0:m], u2[0:k, j, U_VF + h * HD:U_VF + (h + 1) * HD],
                                           start=(j == 0), stop=(j == i))
                        T.did(mm, sem("fox_out"))

                    n = 0
                    for h in range(FH):
                        half = slice(h % 2 * HD, h % 2 * HD + HD)
                        for c in range(2):
                            bank = lv_ring.bank(T)
                            job = lv_ring.ship(T, pe.matmul(bank[:, 0:HALF], ident[0:FH, h:h + 1].broadcast_to([FH, P]),
                                                            f_row[0:FH, 1, c * HALF:(c + 1) * HALF], start=True, stop=True))
                        for i in range(NT2):
                            w = OFF[i] + SIZE[i]
                            pair = psum[0:SIZE[i], 0:2, :].rearrange("p b s -> p (b s)")
                            T.wait(lv_ring.drained, lv_ring.sent)
                            if n:
                                T.wait(sem("fox_scores_drained"), n)
                            T.hold()
                            for a, b in ([(0, w)] if w <= 512 else [(0, 512), (512, w)]):
                                mm = pe.matmul(pair[:, a:b], qk_f[half, h // 2, OFF[i]:OFF[i] + SIZE[i]], qk_f[half, 3 + h // 2, a:b],
                                               start=True, stop=True, skip_group_check=True)
                            T.did(mm, sem("fox_scores"))
                            waiting.append((h, i, n))
                            n += 1
                            if len(waiting) > 1:
                                attend()
                        T.wait(sem("fox_scores_drained"), n)
                    attend()

                def mix():
                    T.wait(sem("mix2_ready"), 1)
                    turned(u2, [U_V, U_V + P, U_V + 2 * P, U_U, U_U + P, U_QK, U_QK + P, U_QK + 2 * P])
                    for half in range(2):
                        w = weights(W_OUT + half)
                        for t in range(NT2):
                            bank = lv_ring.bank(T)
                            for k in range(KT):
                                mm = pe.matmul(bank[0:SIZE[t], :], h2_t[:, k, OFF[t]:OFF[t] + SIZE[t]], w[:, k, :],
                                               start=(k == 0), stop=(k == KT - 1))
                            layer_free[W_OUT + half] = (lv_ring.filled, lv_ring.ship(T, mm))

                def feed_forward():
                    T.wait(sem("mid_ready"), 1)
                    turned(h2, range(0, D, P))
                    for f in range(FT):
                        n = W_FFN + f // 2
                        w = weights(n)
                        for c in range(2):
                            for ring_of, at in ((la_ring, 0), (lv_ring, 256)):
                                at += f % 2 * P
                                bank = ring_of.bank(T)
                                for k in range(KT):
                                    mm = pe.matmul(bank[:, 0:HALF], w[:, k, at:at + P], h2_t[:, k, c * HALF:(c + 1) * HALF],
                                                   start=(k == 0), stop=(k == KT - 1))
                                layer_free[n] = (ring_of.filled, ring_of.ship(T, mm))
                    T.wait(lv_ring.drained, lv_ring.sent)
                    for half in range(2):
                        for t in range(NT2):
                            bank = lv_ring.bank(T)
                            for f in range(FT):
                                n = W_DOWN + 3 * half + f // KT
                                w = weights(n) if t == 0 else slot[(n + LATE) % SLOTS]
                                mm = pe.matmul(bank[0:SIZE[t], :], ff_t[:, f, OFF[t]:OFF[t] + SIZE[t]], w[:, f % KT, :],
                                               start=(f == 0), stop=(f == FT - 1))
                            job = lv_ring.ship(T, mm)
                        for n in range(3):
                            layer_free[W_DOWN + 3 * half + n] = (lv_ring.filled, job)

                project()
                turn_rotated()
                retention()
                pool()
                forget()
                mix()
                feed_forward()

            pe.wait_ge(a_ring.drained, a_ring.sent)
            pe.wait_ge(v_ring.drained, v_ring.sent)
            with pe.Fori(0, LAYERS) as i:
                T = Turn(pe, i, None, LAYER_PER, LAYER_CREDIT, sem("passed"))
                T.wait(sem("layer_start"), 1)
                layer(T)
                T.check()

        @block.sync
        def _(sp):
            sp.dma_start(x_t, io["x_t"]).then_inc(x_landed, 16)

            def load_piece(n, src, words=PIECE):
                if n >= SLOTS:
                    sp.wait_ge(*slot_free[n - SLOTS])
                sp.dma_start(ring[:, n % SLOTS * PIECE:n % SLOTS * PIECE + words], src).then_inc(landed[n % SLOTS], 16)

            for n in range(2):
                load_piece(n, io["weights1"][n])
            for dst, name in SETUP:
                src = io[name]
                part = src.shape[0]
                if name == "rows":
                    sp.dma_start(dst, src.broadcast_to([P, ROWS.width])).then_inc(setup_landed, 16)
                elif name == "gate_up":
                    sp.dma_start(dst[96:112, :], src).then_inc(setup_landed, 16)
                else:
                    sp.dma_start(dst, src).then_inc(setup_landed, 16)
            for n in range(2, 7):
                load_piece(n, io["weights1"][n])
            sp.wait_ge(sums_drained, 2 * H)
            sp.dma_start(c2, io["const2"]).then_inc(sem("const2_landed"), 16)
            for n in range(7, 9):
                load_piece(n, io["weights1"][n])

            def expert_source(e, k):
                if k < 4:
                    return io["exp_gu"][bass.ds(e * 4 + k, 1), :, :].rearrange("o p n -> (o p) n")
                return io["exp_down"][bass.ds(e * 2 + (k - 4), 1), :, :].rearrange("o p n -> (o p) n")

            def expert_slot(k):
                s = (3 + k) % SLOTS
                return ring[:, s * PIECE:(s + 1) * PIECE]

            for k in range(4):
                sp.wait_ge(*slot_free[3 + k])
                sp.dma_start(expert_slot(k), expert_source(0, k)).then_inc(expert_landed[k], 16)
            sp.wait_ge(sem("mixed"), 1)
            sp.dma_start(x1, io["x"]).then_inc(sem("x_rows_landed"), 16)
            sp.dma_start(ln_par, io["ln1"].broadcast_to([P, 2 * D])).then_inc(sem("ln_landed"), 16)
            sp.dma_start(router_w, io["router_w"]).then_inc(sem("router_landed"), 16)
            sp.dma_start(router_b, io["router_b"].broadcast_to([P, E])).then_inc(sem("router_landed"), 16)
            sp.dma_start(c3, io["const3"]).then_inc(sem("router_landed"), 16)
            sp.dma_start(b_down[0:E, :], io["b_down"]).then_inc(sem("router_landed"), 16)
            for k in (4, 5):
                sp.wait_ge(*slot_free[3 + k])
                sp.dma_start(expert_slot(k), expert_source(0, k)).then_inc(expert_landed[k], 16)
            sp.wait_ge(sem("routed"), 4)
            blocks = sp.value_load(block_count[0:1, 0:1], min_val=E, max_val=NB - 1)

            def load_bias(e):
                sp.dma_start(b_gu, io["b_gu"][bass.ds(e, 1), :].broadcast_to([P, 2 * D])).then_inc(bias_landed, 16)

            load_bias(0)
            with sp.Fori(1, blocks) as i:
                e = sp.value_load(block_expert[0:1, bass.ds(i, 1)], min_val=0, max_val=E - 1)
                for k in range(6):
                    if k < 4:
                        sp.wait_ge(ev_ring.filled, i * 12 + (k + 1 - 12))
                    else:
                        sp.wait_ge(ea_ring.filled, i * 9 + (k + 3 - 9))
                    sp.dma_start(expert_slot(k), expert_source(e, k)).then_inc(expert_landed[k], 16)
                    if k == 3:
                        sp.wait_ge(ev_ring.drained, i * 12 + (4 + 3 - 12))
                        load_bias(e)
            sp.wait_ge(ea_ring.filled, blocks * 9)
            sp.wait_ge(sem("ffn_ready"), 1)

            def load_piece2(n, src, words=PIECE):
                if n >= SLOTS:
                    sp.wait_ge(*slot_free2[n - SLOTS])
                s = (3 + n) % SLOTS
                sp.dma_start(ring[:, s * PIECE:s * PIECE + words], src).then_inc(landed2[s], 16)

            load_piece2(0, io["ple_gate"][0])
            load_piece2(1, io["ple_gate"][1])
            load_piece2(2, io["ple_proj"], 2 * D)
            sp.dma_start(p_t, io["p_t"]).then_inc(sem("p_landed"), 16)
            sp.dma_start(ln_par, io["ln2"].broadcast_to([P, 2 * D])).then_inc(sem("ln_landed"), 16)
            sp.dma_start(h2[0:META, 0, :], io["meta"]).then_inc(sem("meta_landed"), 16)
            sp.wait_ge(sem("embedded"), 1)
            sp.dma_start(ln_par, io["ln_emb"].broadcast_to([P, 2 * D])).then_inc(sem("ln_landed"), 16)
            with sp.Fori(0, LAYERS) as i:
                T = Turn(sp, i, None, LAYER_PER, LAYER_CREDIT)
                params = sem("layer_params_landed")
                T.wait(sem("layer_start"), 1)
                for dst, name, part in ((f_w, "f_w", P), (f_b, "f_b", FH), (pool_w, "pool_w", P)):
                    src = io[name][bass.ds(i, 1)].rearrange("o p n -> (o p) n")
                    dst = dst[0:part] if len(dst.shape) == 2 else dst.rearrange("p a b -> p (a b)")
                    sp.dma_start(dst, src).then_inc(params, 16)
                sp.dma_start(rows2, io["rows2"][bass.ds(i, 1), :].broadcast_to([P, ROWS2.width])).then_inc(params, 16)

                def load_piece3(n):
                    if n >= SLOTS:
                        T.wait(*layer_free[n - SLOTS])
                    s = (n + LATE) % SLOTS
                    sp.dma_start(ring[:, s * PIECE:(s + 1) * PIECE],
                                 io["weights2"][bass.ds(i * LAYER_PIECES + n, 1)].rearrange("o p n -> (o p) n")
                                 ).then_inc(layer_landed[n % SLOTS], 16)

                for n in range(5):
                    load_piece3(n)
                sp.dma_start(c4, io["const4"]).then_inc(params, 16)
                for n in (5, 6, 7, 8, 9):
                    load_piece3(n)
                T.wait(lv_ring.filled, layer_mark["projected"])
                sp.dma_start(retained.rearrange("p h s -> p (h s)"), io["retention_decay"]).then_inc(sem("retention_decay_landed"), 16)
                load_piece3(10)
                T.wait(sem("mix2_ready"), 1)
                sp.dma_start(ln_par2, io["ln_mid"][bass.ds(i, 1), :].broadcast_to([P, 2 * D])).then_inc(sem("layer_ln_landed"), 16)
                for n in range(11, W_DOWN):
                    load_piece3(n)
                T.wait(sem("mid_ready"), 1)
                sp.dma_start(ln_par2, io["ln_end"][bass.ds(i, 1), :].broadcast_to([P, 2 * D])).then_inc(sem("layer_ln_landed"), 16)
                for n in range(W_DOWN, LAYER_PIECES):
                    load_piece3(n)
            sp.wait_ge(sem("layer_start"), 1 + LAYERS)
            sp.dma_start(io["out"].rearrange("(t p) d -> p t d", p=P), h2[:, 1:, :]).then_inc(out_landed, 16)
            sp.wait_ge(out_landed, 16)

        @block.scalar
        def _(act):
            A = Steps(act, act_step)

            def project_block1():
                for a, width in ((T_GOG, 256), (T_Z, 512), (T_MOG, 512)):
                    for t in range(TT):
                        bank = a_ring.take(act)
                        A.did(act.copy(u_tok[:, t, a:a + width], bank[:, 0:width]), a_ring.drained)

            def softplus_rows():
                act.wait_ge(rows_biased, 4)
                act.wait_ge(a_ring.filled, mark["projected"])
                two = hrow[0:4, 2:4, :]
                A.did(act.activation(two, hrow[0:4, 0:2, :], ACT.Abs))
                A.settle()
                A.did(act.activation(two, two, ACT.Exp, scale=-1.0))
                A.did(act.activation(expa[0:4, :], COLS(cols, "a_log")[0:4, :], ACT.Exp))
                act.wait_ge(act_step, 2)
                A.did(act.activation(two, two, ACT.Ln, bias=ones[0:4, 0:1]), rows_softplus)

            def conv_silu():
                for i in range(8):
                    act.wait_ge(conv_summed, i + 1)
                    b = COLS(cols, "ssd_cb", i, i + 1) if i < 4 else COLS(cols, "m_cb", i - 4, i - 3)
                    A.did(act.activation(u_feat[:, F_SSD + i, PAD:], decay[:, i % 2, :], ACT.Silu, bias=b), conv_ready)

            def gates():
                A.settle()
                A.did(act.activation(u_tok[:, :, T_Z:T_Z + W], u_tok[:, :, T_Z:T_Z + W], ACT.Silu), z_ready)
                A.did(act.activation(u_tok[:, :, T_MOG:T_MOG + W], u_tok[:, :, T_MOG:T_MOG + W], ACT.Sigmoid), z_ready)
                A.did(act.activation(u_tok[:, :, T_GOG:T_GOG + W], u_tok[:, :, T_GOG:T_GOG + W], ACT.Silu), z_ready)

            def decays():
                act.wait_ge(hcol_ready, 1)
                A.did(act.activation(hcol[:, 3], hcol[:, 3], ACT.Exp), sem("floor_ready"))
                for n in range(2 * H * TT):
                    i = n % TT
                    act.wait_ge(decay_arg, n + 1)
                    part = decay[:, n % 2, 0:SEQ - i * P]
                    A.did(act.activation(part, part, ACT.Exp, scale=1.0 if n < H * TT else -1.0), decay_ready)

            def root(n, parts, scale, eps_col, view=None):
                act.wait_ge(stat_sum, n)
                view = stat if view is None else view
                A.did(act.activation(view[:, 0:parts], view[:, 0:parts], ACT.Sqrt, scale=scale,
                                     bias=CONST1(c1, "eps", eps_col, eps_col + 1)[0:view.shape[0]]), stat_root)

            act.wait_ge(setup_landed, 16 * len(SETUP))
            project_block1()
            softplus_rows()
            conv_silu()
            gates()
            decays()
            root(1, TT, 1.0 / W, 0)
            root(2, TT * H, 1.0 / HD, 0)

            def gla():
                asked = sem("gla_asked")
                given = sem("gla_given")
                act.wait_ge(asked, 1)
                A.did(act.activation(gla_tmp, gla_la, ACT.Abs))
                A.settle()
                A.did(act.activation(gla_tmp, gla_tmp, ACT.Exp, scale=-1.0))
                A.settle()
                A.did(act.activation(gla_tmp, gla_tmp, ACT.Ln, bias=ones[:, 0:1]), given)
                act.wait_ge(asked, 2)
                A.did(act.activation(gla_la, gla_cum, ACT.Exp), given)
                A.did(act.activation(gla_tmp, gla_cum, ACT.Exp, scale=-1.0), given)
                act.wait_ge(asked, 3)
                A.did(act.activation(gla_tmp, gla_tmp, ACT.Exp), given)

            def rwkv_features():
                lora = u_feat[:, F_RWKV + 6, PAD:]
                act.wait_ge(sem("shifted"), 1)
                A.did(act.activation(lora[0:32, :], lora[0:32, :], ACT.Tanh), sem("lora_ready"))
                A.did(act.activation(lora[64:128, :], lora[64:128, :], ACT.Sigmoid), sem("lora_ready"))
                for dst, b in ((r_lw, "w0"), (r_a, "a0")):
                    for f in range(2):
                        bank = a_ring.take(act)
                        A.did(act.activation(dst[:, :, f, :], bank.rearrange("p (t s) -> p t s", t=TT), ACT.Sigmoid,
                                             bias=COLS(cols, b, f, f + 1)), a_ring.drained)
                for t in range(TT):
                    bank = a_ring.take(act)
                    A.did(act.copy(g_tok[:, t, :], bank[:, 0:W]), a_ring.drained)
                mark["rwkv_gates"] = a_ring.taken
                for t in range(TT // 2):
                    bank = a_ring.take(act)
                    A.did(act.activation(r_t1[:, 2 * t:2 * t + 2, :, :], bank.rearrange("p (t f s) -> p t f s", t=2, f=2), ACT.Sqrt),
                          a_ring.drained)
                mark["rwkv_norms"] = a_ring.taken
                asked, given = sem("rwkv_asked"), sem("rwkv_given")
                act.wait_ge(asked, 1)
                A.did(act.activation(r_t1, r_cw, ACT.Exp), given)
                act.wait_ge(asked, 2)
                A.did(act.activation(r_t2, r_cw, ACT.Exp, scale=-1.0), given)
                act.wait_ge(asked, 3)
                A.did(act.activation(r_t1, r_lw, ACT.Exp), given)
                act.wait_ge(asked, 4)
                A.did(act.activation(r_t2, r_t2, ACT.Exp), given)

            gla()
            root(3, TT * H, 1.0 / HD, 0)
            rwkv_features()
            root(4, TT * H, 1.0 / HD, 1)

            def transposed_rows(out):
                for t in range(TT):
                    for half in range(2):
                        bank = a_ring.take(act)
                        A.did(act.copy(out[:, 4 * half:4 * half + 4, t * P:(t + 1) * P], bank.rearrange("p (k s) -> p k s", k=4)),
                              a_ring.drained)

            def layer_root(t0, tiles, parts=P):
                act.wait_ge(sem("ln_asked"), layer_roots[0] + 1)
                layer_roots[0] += 1
                v = ln_mean[0:parts, t0:t0 + tiles, 1:2]
                A.did(act.activation(v, v, ACT.Sqrt, bias=CONST1(c1, "eps", 0, 1)[0:parts]), sem("ln_given"))

            layer_roots = [0]

            def route():
                act.wait_ge(sem("gate_asked"), 1)
                A.did(act.activation(gate4[:, :, 0:TOP], gate4[:, :, 0:TOP], ACT.Exp), sem("gate_given"))

            def experts():
                for half in range(2):
                    bank = a_ring.take(act)
                    A.did(act.copy(xg[:, 4 * half:4 * half + 4, :], bank.rearrange("p (k r) -> p k r", k=4)), a_ring.drained)
                act.wait_ge(sem("routed"), 4)
                blocks = act.value_load(block_count[0:1, 0:1], min_val=E, max_val=NB - 1)
                act.sem_inc(ea_ring.drained, 3)
                with act.Fori(0, blocks) as i:
                    T = Turn(act, i, None, PER, CREDIT)
                    ea_ring.taken = 0

                    def swish(c):
                        T.wait(swish_asked, c + 1)
                        T.did(act.activation(swi[:, 512:768], swi[:, 0:256], ACT.Sigmoid, scale=SWIGLU_ALPHA), swish_given)

                    def out(dst, words, **split):
                        bank = ea_ring.take(T)[:, 0:words]
                        if split:
                            bank = bank.rearrange("p (k r) -> p k r", **split)
                        T.did(act.copy(dst, bank), ea_ring.drained)

                    swish(0)
                    swish(1)
                    out(hid_t[:, 0:2, :], 256, k=2)
                    swish(2)
                    out(hid_t[:, 2:4, :], 256, k=2)
                    swish(3)
                    out(hid_t[:, 4:6, :], 256, k=2)
                    out(from_t, 512)
                    out(xg[:, 0:4, :], 512, k=4)
                    out(hid_t[:, 6:8, :], 256, k=2)
                    out(y_blk[:, 0:512], 512)
                    out(y_blk[:, 512:1024], 512)
                    out(xg[:, 4:8, :], 512, k=4)

            def gated_embedding():
                transposed_rows(h_t)
                mark["ple_gates"] = a_ring.taken
                for n in range(2 * TT):
                    bank = a_ring.take(act)
                    if n >= TT:
                        act.wait_ge(sem("gate_used"), n - TT + 1)
                    A.did(act.activation(ple_gate[:, n % TT, :], bank, ACT.Sigmoid), a_ring.drained)

            transposed_rows(y_t)
            layer_root(0, TT)
            transposed_rows(x1_t)
            route()
            experts()
            gated_embedding()
            layer_root(0, TT)
            layer_root(1, TT)
            layer_root(0, 1, META)

            def layer(T):
                la_ring.taken = 0

                def turned(meta_banks=2):
                    for t in range(NT2):
                        n = SIZE[t]
                        banks = 2 if t else meta_banks
                        k = KT // banks
                        for b in range(banks):
                            bank = la_ring.take(T)
                            T.did(act.copy(h2_t[:, k * b:k * b + k, OFF[t]:OFF[t] + n],
                                           bank[:, 0:k * n].rearrange("p (k s) -> p k s", k=k)), la_ring.drained)

                def project():
                    for n in range(4):
                        width = 512 if n < 3 else 256
                        for t in range(NT2):
                            bank = la_ring.take(T)
                            T.did(act.copy(u2[0:SIZE[t], t, n * 512:n * 512 + width], bank[0:SIZE[t], 0:width]), la_ring.drained)
                    T.settle()
                    for part, tiles in PARTS:
                        g = u2[0:part, tiles, U_G:U_G + RH * RV]
                        T.did(act.activation(g, g, ACT.Silu), sem("ret_gate_ready"))

                def forget_gate():
                    T.wait(sem("forget_asked"), 1)
                    T.did(act.activation(f_row[0:FH, 1, :], f_row[0:FH, 0, :], ACT.Abs))
                    T.settle()
                    T.did(act.activation(f_row[0:FH, 1, :], f_row[0:FH, 1, :], ACT.Exp, scale=-1.0))
                    T.settle()
                    T.did(act.activation(f_row[0:FH, 1, :], f_row[0:FH, 1, :], ACT.Ln, bias=ones[0:FH, 0:1]), sem("forget_given"))

                def ret_roots():
                    for n, (part, tiles) in enumerate(PARTS):
                        T.wait(sem("ret_stat"), n + 1)
                        v = stat2[0:part, tiles.start * RH:tiles.stop * RH]
                        T.did(act.activation(v, v, ACT.Sqrt, scale=1.0 / RV, bias=CONST1(c1, "eps", 0, 1)[0:part]), sem("ret_root"))

                def forget():
                    waiting = []
                    turned_jobs = [0]

                    def turn_weights():
                        i, n = waiting.pop(0)
                        m = SIZE[i]
                        for first, last in ([(0, i + 1)] if i < 4 else [(0, 4), (4, 5)]):
                            bank = psum[:, 4 + turned_jobs[0] % 2, :]
                            T.wait(sem("fox_turned"), turned_jobs[0] + 1)
                            if first == 0:
                                if n >= 2:
                                    T.wait(sem("fox_out"), n - 1)
                                T.did(act.copy(fox_pt[0:META, n % 2, 0, 0:m], bank[0:META, 0:m]),
                                      sem("fox_turned_drained") if last == 1 else None)
                            if last > 1:
                                a = max(first, 1)
                                T.did(act.copy(fox_pt[:, n % 2, a:last, 0:m],
                                               bank[:, (a - first) * m:(last - first) * m].rearrange("p (j s) -> p j s", s=m)),
                                      sem("fox_turned_drained"))
                            turned_jobs[0] += 1

                    n = 0
                    for h in range(FH):
                        for i in range(NT2):
                            T.wait(sem("fox_max"), n + 1)
                            p = fox_p[0:SIZE[i], n % 2, 0:OFF[i] + SIZE[i]]
                            T.did(act.activation(p, p, ACT.Exp, bias=row_max[0:SIZE[i], n % 2:n % 2 + 1],
                                                 accum_out=row_sum[0:SIZE[i], n % 2:n % 2 + 1]), sem("fox_weights_ready"))
                            waiting.append((i, n))
                            n += 1
                            if len(waiting) > 1:
                                turn_weights()
                    turn_weights()

                def norm_root():
                    for part, tiles in PARTS:
                        T.wait(sem("layer_ln_asked"), roots[0] + 1)
                        roots[0] += 1
                        v = ln_mean[0:part, tiles, 1:2]
                        T.did(act.activation(v, v, ACT.Sqrt, bias=CONST1(c1, "eps", 0, 1)[0:part]), sem("layer_ln_given"))

                roots = [0]
                turned(1)
                project()
                forget_gate()
                ret_roots()
                forget()
                turned()
                norm_root()
                turned()
                for f in range(FT):
                    for c in range(2):
                        bank = la_ring.take(T)
                        T.did(act.activation(ff_t[:, f, c * HALF:(c + 1) * HALF], bank[:, 0:HALF], ACT.Silu), la_ring.drained)
                norm_root()

            act.sem_inc(la_ring.drained, 3)
            act.sem_inc(sem("fox_turned_drained"), 2)
            with act.Fori(0, LAYERS) as i:
                T = Turn(act, i, sem("layer_scalar_step"), LAYER_PER, LAYER_CREDIT)
                T.wait(sem("layer_start"), 1)
                layer(T)
                T.check()

        @block.vector
        def _(dve):
            V = Steps(dve, dve_step)

            def then(ins, s=None):
                V.did(ins, s)
                V.settle()

            def project_block1():
                then(dve.memset(u_feat[:, :, 0:PAD], 0.0))
                for i in range(NF):
                    bank = v_ring.take(dve)
                    V.did(dve.tensor_copy(u_feat[:, i, PAD:], bank), v_ring.drained)

            def bias_rows():
                b = COLS(cols, "rows_b")
                dve.wait_ge(a_ring.filled, mark["projected"])
                V.settle()
                u = u_feat[:, F_ROWS, PAD:]
                V.did(dve.tensor_scalar(hrow[0:4, R_DT, :], u[0:4, :], b[0:4, :], None, ALU.add), rows_biased)
                V.did(dve.tensor_scalar(hrow[0:4, R_NF, :], u[64:68, :], b[64:68, :], -1.0, ALU.add, ALU.mult), rows_biased)
                V.did(dve.tensor_scalar(hrow[0:4, R_G, :], u[32:36, :], b[32:36, :], None, ALU.add), rows_biased)
                V.did(dve.memset(den, 0.0), rows_biased)

            def finish_rows():
                dve.wait_ge(rows_softplus, 1)
                then(dve.scalar_tensor_tensor(hrow[0:4, 0:2, :], hrow[0:4, 0:2, :], 0.0, hrow[0:4, 2:4, :], ALU.max, ALU.add))
                one = ones[0:4, 0:1].broadcast_to([4, SEQ])
                then(dve.tensor_scalar(hrow[0:4, 2, :], hrow[0:4, R_DT, :], expa[0:4, :], -1.0, ALU.mult, ALU.mult))
                V.did(dve.tensor_tensor_scan(hrow[0:4, R_A, :], one, hrow[0:4, 2, :], 0.0, ALU.mult, ALU.add))
                then(dve.tensor_tensor_scan(hrow[0:4, R_F, :], one, hrow[0:4, R_NF, :], 0.0, ALU.mult, ALU.subtract))
                then(dve.tensor_tensor(hrow[0:4, R_G, :], hrow[0:4, R_G, :], hrow[0:4, R_F, :], ALU.subtract))
                then(dve.tensor_tensor_scan(hrow[0:4, R_M, :], hrow[0:4, R_G, :], hrow[0:4, R_G, :], 0.0, ALU.max, ALU.max))
                V.did(dve.scalar_tensor_tensor(hrow[0:4, R_F, :], hrow[0:4, R_F, :], -1.0, hrow[0:4, R_M, :], ALU.mult, ALU.subtract), hrow_ready)

            def convolve():
                for i in range(8):
                    u = u_feat[:, F_SSD + i, :]
                    w = COLS(cols, "ssd_cw", 4 * i, 4 * i + 4) if i < 4 else COLS(cols, "m_cw", 4 * i - 16, 4 * i - 12)
                    acc = decay[:, i % 2, :]
                    if i >= 2:
                        dve.wait_ge(conv_ready, i - 1)
                    then(dve.tensor_scalar(acc, u[:, 3:3 + SEQ], w[:, 3:4], None, ALU.mult))
                    for tap in (2, 1):
                        then(dve.scalar_tensor_tensor(acc, u[:, tap:tap + SEQ], w[:, tap:tap + 1], acc, ALU.mult, ALU.add))
                    V.did(dve.scalar_tensor_tensor(acc, u[:, 0:SEQ], w[:, 0:1], acc, ALU.mult, ALU.add), conv_summed)

            def head_columns():
                bank = v_ring.take(dve)
                then(dve.tensor_copy(small[:, 0:64], bank[:, 0:64]), v_ring.drained)
                V.did(dve.memset(den, 0.0), hcol_ready)

            def ssd_values():
                for t in range(TT):
                    bank = v_ring.take(dve)
                    V.did(dve.tensor_copy(xs_tok[:, t, :], bank[:, 0:W]), v_ring.drained)
                V.settle()

            def decayed_attention():
                def argument(n):
                    g, i = n // TT, n % TT
                    m, h = g // H, g % H
                    w = SEQ - i * P
                    V.settle()
                    V.did(dve.scalar_tensor_tensor(decay[:, n % 2, 0:w], row_cast[:, g % 2, i * P:], hcol[:, 1 + m, i, h:h + 1],
                                                   CONST1(c1, "causal", 0, w), ALU.subtract,
                                                   ALU.add if m == 0 else ALU.subtract), decay_arg)

                def weights(n):
                    g, i = n // TT, n % TT
                    m, h = g // H, g % H
                    w = SEQ - i * P
                    dve.wait_ge(decay_ready, n + 1)
                    if n >= 2:
                        dve.wait_ge(pv_done, n - 1)
                    bank = v_ring.take(dve)
                    V.did(dve.scalar_tensor_tensor(weigh[:, n % 2, 0:w], bank[:, 0:w],
                                                   hcol[:, 0, i, h:h + 1] if m == 0 else HD ** -0.5,
                                                   decay[:, n % 2, 0:w], ALU.mult, ALU.mult), v_ring.drained)

                def collect(g):
                    m, h = g // H, g % H
                    sums = psum[:, 6 + g % 2, :]
                    acc = sums[:, 0:TT * HD].rearrange("p (t d) -> p t d", t=TT)
                    dve.wait_ge(pv_done, TT * (g + 1))
                    if m == 0:
                        V.did(dve.scalar_tensor_tensor(y[:, :, h * HD:(h + 1) * HD], xs_tok[:, :, h * HD:(h + 1) * HD],
                                                       ROWS(rows, "ssd_d", h, h + 1), acc, ALU.mult, ALU.add), sums_drained)
                    else:
                        d = sums[:, TT * HD:TT * HD + TT]
                        dve.wait_ge(sem("floor_ready"), 1)
                        then(dve.tensor_copy(stat[:, 0:TT], d))
                        then(dve.scalar_tensor_tensor(den, stat[:, 0:TT], -1.0, stat[:, 0:TT], ALU.mult, ALU.max))
                        then(dve.tensor_tensor(den, den, hcol[:, 3, :, h], ALU.max))
                        then(dve.reciprocal(den, den))
                        V.did(dve.tensor_tensor(y[:, :, 3 * W + h * HD:3 * W + (h + 1) * HD], acc,
                                                den.rearrange("p (t o) -> p t o", o=1).broadcast_to([P, TT, HD]), ALU.mult), sums_drained)

                dve.wait_ge(conv_ready, 8)
                for g in range(2 * H):
                    bank = v_ring.take(dve)
                    then(dve.tensor_copy(row_cast[:, g % 2, :], bank), v_ring.drained)
                    for i in range(TT):
                        argument(g * TT + i)
                        if i:
                            weights(g * TT + i - 1)
                    weights(g * TT + TT - 1)
                    if g:
                        collect(g - 1)
                collect(2 * H - 1)
                V.settle()

            norms = [0]

            def group_norm(view, groups, centered, gain, bias=None, tmp=norm_tmp):
                n = W // groups
                t = TT * groups
                y4 = heads_of(view, groups)
                tmp4 = tmp.rearrange("p (t h d) -> p t h d", t=TT, h=groups)
                s = stat[:, 0:t].rearrange("p (t h) -> p t h", t=TT)
                s4 = stat[:, 0:t].rearrange("p (t h o) -> p t h o", t=TT, o=1).broadcast_to([P, TT, groups, n])
                if centered:
                    then(dve.tensor_reduce(s, y4, AX.X, ALU.add))
                    then(dve.tensor_scalar(stat[:, 0:t], stat[:, 0:t], 1.0 / n, None, ALU.mult))
                    then(dve.tensor_tensor(y4, y4, s4, ALU.subtract))
                then(dve.tensor_tensor(tmp4, y4, y4, ALU.mult))
                then(dve.tensor_reduce(s, tmp4, AX.X, ALU.add), stat_sum)
                norms[0] += 1
                dve.wait_ge(stat_root, norms[0])
                then(dve.reciprocal(stat[:, 0:t], stat[:, 0:t]))
                then(dve.tensor_tensor(y4, y4, s4, ALU.mult))
                g3 = gain.rearrange("p (o d) -> p o d", o=1).broadcast_to([P, TT, W])
                then(dve.tensor_tensor(view, view, g3, ALU.mult))
                if bias is not None:
                    b3 = bias.rearrange("p (o d) -> p o d", o=1).broadcast_to([P, TT, W])
                    then(dve.tensor_tensor(view, view, b3, ALU.add))

            dve.wait_ge(setup_landed, 16 * len(SETUP))
            project_block1()
            bias_rows()
            finish_rows()
            convolve()
            head_columns()
            ssd_values()
            decayed_attention()
            dve.wait_ge(z_ready, 3)
            then(dve.tensor_tensor(y[:, :, 0:W], y[:, :, 0:W], u_tok[:, :, T_Z:T_Z + W], ALU.mult))
            group_norm(y[:, :, 0:W], 1, False, ROWS(rows, "ssd_g"))
            then(dve.tensor_tensor(y[:, :, 3 * W:], y[:, :, 3 * W:], u_tok[:, :, T_MOG:T_MOG + W], ALU.mult))
            group_norm(y[:, :, 3 * W:], H, True, ROWS(rows, "m_g"))

            def gla():
                asked, given, ready = sem("gla_asked"), sem("gla_given"), sem("gla_ready")
                q, k = u_feat[:, F_GLA, PAD:], u_feat[:, F_GLA + 1, PAD:]
                bank = v_ring.take(dve)
                then(dve.tensor_scalar(gla_la, bank, COLS(cols, "gate_b"), None, ALU.add), v_ring.drained)
                V.did(dve.memset(gla_state[:, 0, :], 0.0), asked)
                dve.wait_ge(given, 1)
                then(dve.scalar_tensor_tensor(gla_la, gla_la, 0.0, gla_tmp, ALU.min, ALU.subtract))
                then(dve.tensor_scalar(gla_la, gla_la, 1.0 / 16.0, None, ALU.mult))
                dve.wait_ge(sem("const2_landed"), 16)
                then(dve.tensor_tensor_scan(gla_cum, CONST2(c2, "reset"), gla_la, 0.0, ALU.mult, ALU.add), asked)
                dve.wait_ge(given, 3)
                then(dve.scalar_tensor_tensor(q, q, (P // H) ** -0.5, gla_la, ALU.mult, ALU.mult))
                V.did(dve.tensor_copy(gla_eb, gla_la[:, CH - 1::CH]))
                then(dve.tensor_tensor(gla_kdec.rearrange("p t c -> p (t c)"), k, gla_tmp, ALU.mult))
                c3 = gla_cum.rearrange("p (c s) -> p c s", s=CH)
                V.did(dve.tensor_tensor(gla_tmp.rearrange("p (c s) -> p c s", s=CH), c3[:, :, CH - 1:CH].broadcast_to([P, 8, CH]), c3,
                                        ALU.subtract), asked)
                dve.wait_ge(given, 4)
                then(dve.tensor_tensor(gla_tmp, k, gla_tmp, ALU.mult))
                V.did(dve.tensor_copy(k, gla_kdec.rearrange("p t c -> p (t c)")), ready)
                V.settle()
                V.did(dve.memset(den, 0.0), ready)
                bank = v_ring.take(dve)
                then(dve.tensor_copy(gla_kdec.rearrange("p t c -> p (t c)"), bank), v_ring.drained)
                for c in range(7):
                    bank = v_ring.take(dve)
                    then(dve.tensor_tensor(gla_state[:, c + 1, :], bank[:, 0:W], CONST2(c2, "glamask"), ALU.mult), v_ring.drained)
                    then(dve.scalar_tensor_tensor(gla_state[:, c + 1, :], gla_state[:, c, :], gla_eb[:, c:c + 1], gla_state[:, c + 1, :],
                                                  ALU.mult, ALU.add), ready if c == 6 else None)
                incl = CONST2(c2, "mask4", P, 2 * P).rearrange("p (o s) -> p o s", o=1).broadcast_to([P, H, P])

                def mask_queries(t):
                    if t >= 2:
                        dve.wait_ge(v_ring.filled, scores_taken[t - 2])
                    V.settle()
                    for h in range(H):
                        ins = dve.tensor_scalar(gla_qm[:, t % 2 * 2 + h // 2, h % 2, :], q[:, t * P:(t + 1) * P],
                                                CONST2(c2, "glamask", h * HD, h * HD + 1), None, ALU.mult)
                        V.did(ins, sem("gla_masked") if h == H - 1 else None)

                scores_taken = []

                def mask_scores(t):
                    bank = v_ring.take(dve)
                    scores_taken.append(v_ring.taken)
                    V.did(dve.tensor_tensor(gla_st[:, t % 2], bank.rearrange("p (h s) -> p h s", h=H), incl, ALU.mult), v_ring.drained)

                mask_queries(0)
                mask_queries(1)
                mask_scores(0)
                for t in range(TT):
                    if t + 2 < TT:
                        mask_queries(t + 2)
                    if t + 1 < TT:
                        mask_scores(t + 1)
                    bank = v_ring.take(dve)
                    V.did(dve.tensor_copy(y[:, t, 2 * W:3 * W], bank[:, 0:W]), v_ring.drained)
                V.settle()

            def rwkv_features():
                ready, asked, given = sem("rwkv_ready"), sem("rwkv_asked"), sem("rwkv_given")

                def pair(i):
                    return u_feat[:, F_RWKV + i:F_RWKV + i + 2, PAD:].rearrange("p f (t s) -> p t f s", t=TT)

                def col(name):
                    return [COLS(cols, name, f, f + 1) for f in range(2)]

                def flat(v, f):
                    return v[:, :, f, :]

                for i in range(7):
                    u = u_feat[:, F_RWKV + i, :]
                    s = gla_cum if i % 2 else gla_la
                    then(dve.tensor_tensor(s, u[:, 2:2 + SEQ], u[:, 3:3 + SEQ], ALU.subtract))
                    then(dve.scalar_tensor_tensor(u[:, PAD:], s, COLS(cols, "mu", i, i + 1), u[:, PAD:], ALU.mult, ALU.add),
                         sem("shifted") if i == 6 else None)
                r, k = pair(0), pair(2)
                kk = r_kk
                for f in range(2):
                    V.did(dve.tensor_scalar(flat(kk, f), flat(k, f), col("k_k")[f], None, ALU.mult))
                V.did(dve.tensor_scalar(r_omka, COLS(cols, "k_a"), -1.0, 1.0, ALU.mult, ALU.add))
                V.settle()
                then(dve.tensor_tensor(r_tmp, kk, kk, ALU.mult), ready)
                for t in range(TT):
                    bank = v_ring.take(dve)
                    V.did(dve.tensor_copy(v_tok[:, t, :], bank[:, 0:W]), v_ring.drained)
                dve.wait_ge(a_ring.drained, mark["rwkv_gates"])
                then(dve.tensor_scalar(r_lw, r_lw, -float(np.exp(-0.5)), None, ALU.mult))
                reset = CONST2(c2, "reset", 0, P)
                for t in range(TT):
                    for f in range(2):
                        V.did(dve.tensor_tensor_scan(r_cw[:, t, f, :], reset, r_lw[:, t, f, :], 0.0, ALU.mult, ALU.add))
                for f in range(2):
                    V.did(dve.tensor_scalar(flat(r_t2, f), flat(r_a, f), col("k_a")[f], r_omka[:, f:f + 1], ALU.mult, ALU.add))
                V.settle()
                then(dve.tensor_tensor(k, k, r_t2, ALU.mult))
                dve.wait_ge(a_ring.drained, mark["rwkv_norms"])
                then(dve.tensor_scalar(r_t1, r_t1, 1e-12, None, ALU.max))
                then(dve.reciprocal(r_t1, r_t1))
                then(dve.tensor_tensor(kk, kk, r_t1, ALU.mult), asked)
                then(dve.tensor_tensor(r_tmp, r, k, ALU.mult))
                for f in range(2):
                    V.did(dve.tensor_scalar(flat(r_tmp, f), flat(r_tmp, f), col("r_k")[f], None, ALU.mult), ready if f else None)
                dve.wait_ge(given, 1)
                then(dve.tensor_tensor(r_at[:, :, :, 1, :], r, r_t1, ALU.mult), asked)
                then(dve.tensor_copy(r_wl, r_t1[:, :, :, CH - 1::CH]))
                then(dve.tensor_tensor(r_lw, r_cw, r_lw, ALU.subtract), asked)
                then(dve.tensor_tensor(r_a, kk, r_a, ALU.mult))
                bank = v_ring.take(dve)
                then(dve.tensor_copy(small[:, 120:136], bank[:, 0:16]), v_ring.drained)
                dve.wait_ge(given, 2)
                V.did(dve.tensor_tensor(r_bk[:, 0], r_a, r_t2, ALU.mult))
                then(dve.tensor_tensor(r_bk[:, 1], k, r_t2, ALU.mult))
                c5 = r_cw.rearrange("p t f (c s) -> p (t f) c s", s=CH)
                t5 = r_t2.rearrange("p t f (c s) -> p t (f c) s", s=CH)
                for t in range(TT):
                    ct = r_cw[:, t].rearrange("p f (c s) -> p (f c) s", s=CH)
                    V.did(dve.tensor_tensor(t5[:, t], ct[:, :, CH - 1:CH].broadcast_to([P, 4, CH]), ct, ALU.subtract),
                          asked if t == TT - 1 else None)
                dve.wait_ge(given, 3)
                then(dve.tensor_scalar(r_t1, r_t1, -1.0, None, ALU.mult))
                then(dve.tensor_tensor(r_at[:, :, :, 0, :], kk, r_t1, ALU.mult))
                dve.wait_ge(given, 4)
                V.did(dve.tensor_tensor(r_dec[:, 0], r_a, r_t2, ALU.mult))
                V.did(dve.tensor_tensor(r_dec[:, 1], k, r_t2, ALU.mult))
                V.settle()
                V.did(dve.memset(r_state[:, 0], 0.0))
                V.did(dve.memset(r_gt, 0.0), ready)
                V.settle()
                V.did(dve.memset(den, 0.0), sem("state_ready"))

            def rwkv_tile(t):
                def over_heads(mask):
                    return mask.rearrange("p (o s) -> p o s", o=1).broadcast_to([P, H, P])

                def over_pairs(mask):
                    return mask.rearrange("p (o u s) -> p o u s", o=1, u=1).broadcast_to([P, 2, 2, P])

                def four(bank):
                    return bank.rearrange("p (h s) -> p h s", h=H)

                def pairs(v):
                    return v.rearrange("p (f g) s -> p f g s", f=2)

                for g in range(2):
                    V.did(dve.tensor_scalar(r_atm[:, :, g].rearrange("p f k s -> p f (k s)"), r_at[:, t].rearrange("p f k s -> p f (k s)"),
                                            CONST2(c2, "headsum", g, g + 1), None, ALU.mult), sem("rwkv_masked") if g else None)
                for f in range(2):
                    for kind in range(2):
                        bank = v_ring.take(dve)
                        V.did(dve.tensor_tensor(r_mt[:, f, kind].rearrange("p g q s -> p (g q s)"), bank, CONST2(c2, "mask4"), ALU.mult),
                              v_ring.drained)
                bank = v_ring.take(dve)
                then(dve.tensor_tensor(r_mlo, four(bank), over_heads(CONST2(c2, "lower")), ALU.mult), v_ring.drained)
                bank = v_ring.take(dve)
                V.did(dve.tensor_copy(r_anv[:, :, 0:HD], bank[:, 0:W].rearrange("p (h d) -> p h d", h=H)), v_ring.drained)
                bank = v_ring.take(dve)
                V.did(dve.tensor_copy(r_dtok, four(bank)), v_ring.drained)

                def level(n, upper, spread=over_heads):
                    return spread(CONST2(c2, "level", (2 * n + upper) * P, (2 * n + upper + 1) * P))

                V.settle()
                V.did(dve.tensor_tensor(r_x, r_mlo, level(0, 0), ALU.mult))
                V.did(dve.tensor_tensor(pairs(r_xt), r_mt[:, :, 0, :, 0, :], level(0, 1, over_pairs), ALU.mult))
                V.settle()
                V.did(dve.tensor_tensor(r_x, r_x, over_heads(ident), ALU.add))
                V.did(dve.tensor_tensor(r_xt, r_xt, over_heads(ident), ALU.add))
                bank = v_ring.take(dve)
                V.did(dve.tensor_copy(r_anv[:, :, HD:P], bank[:, 0:W].rearrange("p (h d) -> p h d", h=H)), v_ring.drained)
                for n in range(1, 6):
                    V.settle()
                    V.did(dve.tensor_tensor(pairs(r_mot), r_mt[:, :, 0, :, 0, :], level(n, 1, over_pairs), ALU.mult), sem("level_ready"))
                    bank = v_ring.take(dve)
                    V.did(dve.tensor_copy(r_prod, four(bank)), v_ring.drained)
                    if n < 5:
                        bank = v_ring.take(dve)
                        dve.wait_ge(v_ring.filled, v_ring.taken + 1)
                        V.did(dve.tensor_tensor(r_x, r_x, four(bank), ALU.add), v_ring.drained)
                    bank = v_ring.take(dve)
                    V.did(dve.tensor_tensor(r_xt, r_xt, four(bank), ALU.add), v_ring.drained)
                bank = v_ring.take(dve)
                V.did(dve.tensor_copy(r_xau, four(bank)), v_ring.drained)
                bank = v_ring.take(dve)
                V.did(dve.tensor_tensor(r_rot, bank[:, 0:2 * P].rearrange("p (f s) -> p f s", f=2), r_at[:, t, :, 1, :], ALU.add), v_ring.drained)
                for c in range(2):
                    bank = v_ring.take(dve)
                    for g in range(2):
                        part = slice(g * HD, (g + 1) * HD)
                        V.did(dve.tensor_copy(r_gt[part, c, :, part], bank[part, 0:P].rearrange("p (f v) -> p f v", f=2)),
                              v_ring.drained if g else None)
                for c in range(2):
                    n = 2 * t + c
                    bank = v_ring.take(dve)
                    V.settle()
                    for f in range(2):
                        V.did(dve.scalar_tensor_tensor(r_state[:, (n + 1) % 3, f, :], r_state[:, n % 3, f, :], r_wl[:, t, f, c:c + 1],
                                                       bank[:, f * P:(f + 1) * P], ALU.mult, ALU.add), v_ring.drained if f else None)
                    V.settle()
                    V.did(dve.memset(den, 0.0), sem("state_ready"))
                dve.wait_ge(sem("rwkv_out_filled"), t + 1)
                V.did(dve.tensor_copy(y[:, t, W:2 * W], psum[:, 6 + t % 2, 0:W]), sem("rwkv_out_drained"))

            gla()
            group_norm(y[:, :, 2 * W:3 * W], H, False, ROWS(rows, "gla_g"))
            then(dve.tensor_tensor(y[:, :, 2 * W:3 * W], y[:, :, 2 * W:3 * W], u_tok[:, :, T_GOG:T_GOG + W], ALU.mult))
            rwkv_features()
            for t in range(TT):
                rwkv_tile(t)
            V.settle()
            yr = y[:, :, W:2 * W]
            group_norm(yr, H, True, ROWS(rows, "rwkv_g"), ROWS(rows, "rwkv_b"))
            then(dve.tensor_tensor(heads_of(norm_tmp.rearrange("p (t w) -> p t w", t=TT), H), heads_of(v_tok, H),
                                   r_bonus.rearrange("p t (h o) -> p t h o", o=1).broadcast_to([P, TT, H, HD]), ALU.mult))
            then(dve.tensor_tensor(yr, yr, norm_tmp.rearrange("p (t w) -> p t w", t=TT), ALU.add))
            then(dve.tensor_tensor(yr, yr, g_tok, ALU.mult), sem("mixed"))

            layer_norms = [0, 0]

            def layer_norm(x, t0, tiles, par, ready=None, parts=P):
                for t in range(t0, t0 + tiles):
                    V.settle()
                    for half in range(2):
                        V.did(dve.bn_stats(ln_stats[0:parts, t, half * 6:half * 6 + 6], x[0:parts, t, half * 512:(half + 1) * 512]))
                    V.settle()
                    V.did(dve.bn_aggr(ln_mean[0:parts, t, :], ln_stats[0:parts, t, :]), sem("ln_asked") if t == t0 + tiles - 1 else None)
                layer_norms[0] += 1
                dve.wait_ge(sem("ln_given"), layer_norms[0])
                v = ln_mean[0:parts, t0:t0 + tiles, 1:2]
                then(dve.reciprocal(v, v))
                for t in range(t0, t0 + tiles):
                    row = x[0:parts, t, :]
                    then(dve.tensor_scalar(row, row, ln_mean[0:parts, t, 0:1], ln_mean[0:parts, t, 1:2], ALU.subtract, ALU.mult))
                    then(dve.tensor_tensor(row, row, par[0:parts, 0, :], ALU.mult))
                    then(dve.tensor_tensor(row, row, par[0:parts, 1, :], ALU.add), ready)

            def mix_out():
                dve.wait_ge(sem("x_rows_landed"), 16)
                for half in range(2):
                    part = slice(half * 512, (half + 1) * 512)
                    for t in range(TT):
                        bank = v_ring.take(dve)
                        V.did(dve.scalar_tensor_tensor(x1[:, t, part], x1[:, t, part], ALPHA1, bank, ALU.mult, ALU.add), v_ring.drained)
                dve.wait_ge(sem("ln_landed"), 16)
                layer_norm(x1, 0, TT, ln_par, sem("x1_ready"))

            def route():
                iota = CONST3(c3, "iota")
                routed = sem("routed")
                dve.wait_ge(sem("router_landed"), 16 * 4)
                bank = v_ring.take(dve)
                then(dve.tensor_tensor(logits, bank[:, 0:TT * E].rearrange("p (t e) -> p t e", t=TT),
                                       router_b.rearrange("p (o e) -> p o e", o=1).broadcast_to([P, TT, E]), ALU.add), v_ring.drained)
                for t in range(TT):
                    then(dve.max(top[:, t, :], logits[:, t, :]))
                    then(dve.max_index(top_i[:, t, :].bitcast(mybir.dt.uint32), top[:, t, :], logits[:, t, :]))
                then(dve.tensor_tensor(gate4[:, :, 0:TOP], top[:, :, 0:TOP], top[:, :, 0:1].broadcast_to([P, TT, TOP]), ALU.subtract),
                     sem("gate_asked"))
                then(dve.tensor_copy(top, top_i.bitcast(mybir.dt.uint32)))
                dve.wait_ge(sem("gate_given"), 1)
                then(dve.tensor_reduce(rank[:, 8:12].rearrange("p (t o) -> p t o", o=1), gate4[:, :, 0:TOP], AX.X, ALU.add))
                then(dve.reciprocal(rank[:, 8:12], rank[:, 8:12]))
                then(dve.tensor_tensor(gate4[:, :, 0:TOP], gate4[:, :, 0:TOP],
                                       rank[:, 8:12].rearrange("p (t o) -> p t o", o=1).broadcast_to([P, TT, TOP]), ALU.mult))
                for t in range(TT):
                    for n in range(TOP):
                        dst = gates[:, t, :] if n == 0 else assigned[:, t, :]
                        then(dve.tensor_scalar(dst, iota[:, 0:E], top[:, t, n:n + 1], gate4[:, t, n:n + 1], ALU.is_equal, ALU.mult))
                        if n:
                            then(dve.tensor_tensor(gates[:, t, :], gates[:, t, :], assigned[:, t, :], ALU.add))
                then(dve.tensor_scalar(assigned, gates, 0.0, None, ALU.is_gt), routed)
                bank = v_ring.take(dve)
                then(dve.tensor_copy(gates_t[0:E, :], bank[0:E, :]), v_ring.drained)
                bank = v_ring.take(dve)
                then(dve.scalar_tensor_tensor(pos, bank[:, 0:TT * E].rearrange("p (t e) -> p t e", t=TT), 1.0, assigned, ALU.add, ALU.mult),
                     v_ring.drained)
                then(dve.tensor_scalar(pos, pos, -1.0, None, ALU.add))
                bank = v_ring.take(dve)
                then(dve.tensor_copy(rank[0:E, 7:8], bank[0:E, 0:1]), v_ring.drained)
                V.did(dve.memset(rank[0:E, 3:4], 0.0))
                for n in range(3):
                    V.did(dve.tensor_scalar(rank[0:E, n:n + 1], rank[0:E, 7:8], float(P * (n + 1)), None, ALU.is_gt))
                V.settle()
                then(dve.tensor_copy(rank[0:E, 4:5], rank[0:E, 0:1]))
                then(dve.tensor_tensor(rank[0:E, 5:6], rank[0:E, 4:5], rank[0:E, 1:2], ALU.add))
                then(dve.tensor_tensor(rank[0:E, 6:7], rank[0:E, 5:6], rank[0:E, 2:3], ALU.add), routed)
                bank = v_ring.take(dve)
                then(dve.tensor_copy(pos_t[0:E, :], bank[0:E, :]), v_ring.drained)
                bank = v_ring.take(dve)
                then(dve.tensor_copy(rank[0:E, 8:11], bank[0:E, 0:3]), v_ring.drained)
                bank = v_ring.take(dve)
                then(dve.tensor_scalar(block_count, bank[:, 0:1], float(E), None, ALU.add), v_ring.drained)
                V.did(dve.tensor_copy(hot[0:E, 0:E], ident[0:E, 0:E]))
                V.did(dve.memset(hot[0:E, E:], 0.0))
                V.did(dve.memset(base_w[0:E, :], 0.0))
                V.settle()
                for n in range(3):
                    then(dve.tensor_scalar(rank[0:E, 11:12], rank[0:E, n:n + 1], float(P * (n + 1)), None, ALU.mult))
                    for dst, s in ((hot, n), (base_w, 11)):
                        then(dve.tensor_scalar(logits[0:E, 0, 0:NB - E], iota[0:E, 0:NB - E], rank[0:E, 8 + n:9 + n], rank[0:E, s:s + 1],
                                               ALU.is_equal, ALU.mult))
                        then(dve.tensor_tensor(dst[0:E, E:], dst[0:E, E:], logits[0:E, 0, 0:NB - E], ALU.add),
                             routed if n == 2 and s == 11 else None)
                bank = v_ring.take(dve)
                V.did(dve.tensor_copy(block_expert, bank[:, 0:NB]))
                then(dve.tensor_copy(base_w, bank[:, 64:64 + NB]), v_ring.drained)
                bank = v_ring.take(dve)
                then(dve.tensor_tensor(block_pos, bank[:, 0:TT * NB].rearrange("p (t n) -> p t n", t=TT),
                                       base_w.rearrange("p (o n) -> p o n", o=1).broadcast_to([P, TT, NB]), ALU.subtract), v_ring.drained)
                bank = v_ring.take(dve)
                then(dve.tensor_copy(block_gate, bank[:, 0:TT * NB].rearrange("p (t n) -> p t n", t=TT)), v_ring.drained)
                for t in range(TT):
                    V.did(dve.tensor_scalar(to_block[:, t, :], iota, block_pos[:, t, 0:1], None, ALU.is_equal),
                          sem("first_block_ready") if t == TT - 1 else None)
                V.did(dve.memset(rank[0:E, 0:1], 0.0), routed)
                for t in range(TT):
                    for half in range(2):
                        part = slice(half * 512, (half + 1) * 512)
                        bank = v_ring.take(dve)
                        V.did(dve.scalar_tensor_tensor(ffn[:, t, part], x1[:, t, part], ALPHA1, bank, ALU.mult, ALU.add), v_ring.drained)
                V.settle()

            def experts():
                iota = CONST3(c3, "iota")
                own = sem("expert_vector_step")
                per = {**PER, own.name: 14}
                blocks = dve.value_load(block_count[0:1, 0:1], min_val=E, max_val=NB - 1)
                dve.sem_inc(ev_ring.drained, 3)
                with dve.Fori(0, blocks) as i:
                    T = Turn(dve, i, own, per, CREDIT)
                    ev_ring.taken = 0

                    def maps(out, n, gated, ready):
                        for t in range(TT):
                            at = block_pos[:, t, bass.ds(n, 1)]
                            if gated:
                                ins = dve.tensor_scalar(out[:, t, :], iota, at, block_gate[:, t, bass.ds(n, 1)], ALU.is_equal, ALU.mult)
                            else:
                                ins = dve.tensor_scalar(out[:, t, :], iota, at, None, ALU.is_equal)
                            T.did(ins, ready if t == TT - 1 else None)

                    for c in range(4):
                        part = slice(c * 512, (c + 1) * 512)
                        if c == 0:
                            T.wait(bias_landed, 16)
                        bank = ev_ring.take(T)
                        T.did(dve.tensor_tensor(swi[:, 0:512], bank, b_gu[:, part], ALU.add), ev_ring.drained)
                        T.settle()
                        T.did(dve.tensor_scalar(swi[:, 0:256], swi[:, 0:256], SWIGLU_LIMIT, None, ALU.min), swish_asked)
                        T.did(dve.tensor_scalar(swi[:, 256:512], swi[:, 256:512], SWIGLU_LIMIT, -SWIGLU_LIMIT, ALU.min, ALU.max))
                        T.wait(swish_given, c + 1)
                        T.did(dve.tensor_tensor(swi[:, 512:768], swi[:, 0:256], swi[:, 512:768], ALU.mult))
                        T.settle()
                        T.did(dve.scalar_tensor_tensor(hid[:, c * 256:(c + 1) * 256], swi[:, 256:512], 1.0, swi[:, 512:768], ALU.add, ALU.mult),
                              hidden_ready)
                        T.settle()
                        if c == 0:
                            maps(from_block, i, True, from_ready)
                        if c == 1:
                            T.wait(ea_ring.filled, 1)
                            maps(to_block, i + 1, False, to_ready)
                    for t in range(TT):
                        for half in range(2):
                            part = slice(half * 512, (half + 1) * 512)
                            bank = ev_ring.take(T)
                            T.did(dve.tensor_tensor(ffn[:, t, part], ffn[:, t, part], bank, ALU.add), ev_ring.drained)
                    assert T.count[own.name] == per[own.name]
                    T.settle()
                dve.wait_ge(ev_ring.drained, blocks * 12 + 3)
                V.did(dve.memset(den, 0.0), sem("ffn_ready"))

            def gated_embedding():
                for n in range(2 * TT):
                    t, part = n % TT, slice(n // TT * 512, (n // TT + 1) * 512)
                    bank = v_ring.take(dve)
                    dve.wait_ge(a_ring.drained, mark["ple_gates"] + n + 1)
                    V.settle()
                    then(dve.tensor_tensor(ple_gate[:, t, :], ple_gate[:, t, :], bank, ALU.mult), v_ring.drained)
                    then(dve.tensor_tensor(ffn[:, t, part], ffn[:, t, part], ple_gate[:, t, :], ALU.add), sem("gate_used"))
                dve.wait_ge(sem("ln_landed"), 32)
                layer_norm(ffn, 0, TT, ln_par)

            mix_out()
            route()
            experts()
            gated_embedding()
            V.settle()
            V.did(dve.memset(den, 0.0), sem("embedded"))
            dve.wait_ge(sem("ln_landed"), 48)
            dve.wait_ge(sem("meta_landed"), 16)
            layer_norm(h2, 1, TT, ln_par)
            layer_norm(h2, 0, 1, ln_par, None, META)
            V.did(dve.memset(den, 0.0), sem("layer_start"))

            def layer(T):
                lv_ring.taken = 0

                def then(ins, s=None):
                    T.did(ins, s)
                    T.settle()

                def project():
                    for u in range(6):
                        for c in range(2):
                            bank = lv_ring.take(T)
                            T.did(dve.tensor_scalar(qk_f[:, u, c * HALF:(c + 1) * HALF], bank[:, 0:HALF], HD ** -0.5 if u < 3 else 1.0, None,
                                                    ALU.mult), lv_ring.drained)
                    T.wait(sem("layer_params_landed"), 16 * 5)
                    for c in range(2):
                        bank = lv_ring.take(T)
                        T.did(dve.tensor_scalar(f_row[0:FH, 0, c * HALF:(c + 1) * HALF], bank[0:FH, 0:HALF], f_b[0:FH, :], None, ALU.add),
                              lv_ring.drained)
                    T.settle()
                    T.did(dve.memset(work.rearrange("p b s -> p (b s)"), 0.0), sem("forget_asked"))

                def forget_gate():
                    T.wait(sem("forget_given"), 1)
                    x = f_row[0:FH, 0, :]
                    then(dve.scalar_tensor_tensor(x, x, 0.0, f_row[0:FH, 1, :], ALU.min, ALU.subtract))
                    then(dve.tensor_tensor_scan(f_row[0:FH, 1, :], ones[0:FH, 0:1].broadcast_to([FH, LEN]), x, 0.0, ALU.mult, ALU.add))

                def rotate():
                    T.wait(la_ring.drained, 9 + 20)
                    for t in range(NT2):
                        n = SIZE[t]
                        x = u2[0:n, t, U_QK:U_QK + 8 * RK].rearrange("p (h k d) -> p h k d", h=8, k=2)
                        out = work[0:n, t % 2, :].rearrange("p (h d) -> p h d", h=8)
                        a, b = (f_row[0:n, 0, j * 192:(j + 1) * 192].rearrange("p (h d) -> p h d", h=8) for j in range(2))
                        cos, sin = (CONST4(c4, name, t * 24, (t + 1) * 24)[0:n].rearrange("p (o d) -> p o d", o=1).broadcast_to([n, 8, 24])
                                    for name in ("cos", "sin"))
                        if t >= 2:
                            T.wait(lv_ring.filled, rotated_jobs + t - 1)
                        then(dve.tensor_tensor(a, x[:, :, 0, :], cos, ALU.mult))
                        then(dve.tensor_tensor(b, x[:, :, 1, :], sin, ALU.mult))
                        then(dve.tensor_tensor(out[:, :, 0:24], a, b, ALU.subtract))
                        then(dve.tensor_tensor(a, x[:, :, 0, :], sin, ALU.mult))
                        then(dve.tensor_tensor(b, x[:, :, 1, :], cos, ALU.mult))
                        then(dve.tensor_tensor(out[:, :, 24:48], a, b, ALU.add), sem("rotated_ready"))
                        if t:
                            collect_rotated(t - 1)
                    collect_rotated(NT2 - 1)

                rotated_jobs = 14

                def collect_rotated(t):
                    n = SIZE[t]
                    bank = lv_ring.take(T)
                    T.did(dve.tensor_copy(rotated[:, :, OFF[t]:OFF[t] + n], bank[:, 0:4 * n].rearrange("p (u s) -> p u s", u=4)), lv_ring.drained)
                    T.settle()

                def retention():
                    T.wait(sem("retention_decay_landed"), 16)

                    def collect(h):
                        T.wait(sem("retention_done"), 6 * (h + 1))
                        for part, tiles in PARTS:
                            sums = psum[0:part, 6 + h % 2, tiles.start * RV:tiles.stop * RV].rearrange("p (t d) -> p t d", d=RV)
                            T.did(dve.tensor_copy(u2[0:part, tiles, U_V + h * RV:U_V + (h + 1) * RV], sums),
                                  sem("retained_drained") if part == P else None)

                    for h in range(RH):
                        for seg, (i, a, b) in enumerate(SEGMENTS):
                            n = 6 * h + seg
                            if n >= 2:
                                T.wait(sem("retention_done"), n - 1)
                            bank = lv_ring.take(T)
                            T.did(dve.tensor_tensor(work[0:SIZE[i], seg % 2, 0:b - a], bank[0:SIZE[i], 0:b - a],
                                                    retained[0:SIZE[i], h, a - OFF[i]:b - OFF[i]], ALU.mult), lv_ring.drained)
                        if h:
                            collect(h - 1)
                    collect(RH - 1)
                    T.settle()

                def ret_norm():
                    T.wait(sem("ret_gate_ready"), 2)
                    for n, (part, tiles) in enumerate(PARTS):
                        t = tiles.stop - tiles.start
                        v = u2[0:part, tiles, U_V:U_V + RH * RV]
                        v4 = v.rearrange("p t (h d) -> p t h d", h=RH)
                        sq = retained.rearrange("p h s -> p (h s)")[0:part, 0:t * RH * RV].rearrange("p (t h d) -> p t h d", t=t, h=RH)
                        flat = stat2[0:part, tiles.start * RH:tiles.stop * RH]
                        s = flat.rearrange("p (t h) -> p t h", t=t)
                        s4 = flat.rearrange("p (t h o) -> p t h o", t=t, o=1).broadcast_to([part, t, RH, RV])
                        then(dve.tensor_reduce(s, v4, AX.X, ALU.add))
                        then(dve.tensor_scalar(flat, flat, 1.0 / RV, None, ALU.mult))
                        then(dve.tensor_tensor(v4, v4, s4, ALU.subtract))
                        then(dve.tensor_tensor(sq, v4, v4, ALU.mult))
                        then(dve.tensor_reduce(s, sq, AX.X, ALU.add), sem("ret_stat"))
                        T.wait(sem("ret_root"), n + 1)
                        then(dve.reciprocal(flat, flat))
                        then(dve.tensor_tensor(v4, v4, s4, ALU.mult))
                        g = ROWS2(rows2, "ret_g")[0:part].rearrange("p (o d) -> p o d", o=1).broadcast_to([part, t, RH * RV])
                        then(dve.tensor_tensor(v, v, g, ALU.mult))
                        then(dve.tensor_tensor(v, v, u2[0:part, tiles, U_G:U_G + RH * RV], ALU.mult))

                def pool():
                    for t in reversed(range(NT2)):
                        n = SIZE[t]
                        bank = lv_ring.take(T)
                        T.did(dve.tensor_copy(work[:, t % 2, 0:2 * n], bank[:, 0:2 * n]), lv_ring.drained)
                        for g in range(2):
                            bank = lv_ring.take(T)
                            T.did(dve.tensor_tensor(u2[0:n, t, U_U + g * P:U_U + (g + 1) * P], bank[0:n, 0:P],
                                                    ROWS2(rows2, "pool_scale", g * P, (g + 1) * P)[0:n], ALU.mult), lv_ring.drained)

                def forget():
                    bank = lv_ring.take(T)
                    T.settle()
                    T.did(dve.tensor_copy(c_col[0:META, 0, :], bank[0:META, 0:FH]))
                    then(dve.tensor_copy(c_col[:, 1:, :], bank[:, FH:NT2 * FH].rearrange("p (t h) -> p t h", t=TT)), lv_ring.drained)
                    waiting = []

                    def finish():
                        h, i, n = waiting.pop(0)
                        m = SIZE[i]
                        T.wait(sem("fox_out"), n + 1)
                        then(dve.reciprocal(row_sum[0:m, n % 2:n % 2 + 1], row_sum[0:m, n % 2:n % 2 + 1]))
                        T.did(dve.tensor_scalar(u2[0:m, i, U_QK + h * HD:U_QK + (h + 1) * HD], psum[0:m, 6 + n % 2, 0:HD],
                                                row_sum[0:m, n % 2:n % 2 + 1], None, ALU.mult), sem("fox_out_drained"))
                        T.settle()

                    n = 0
                    for h in range(FH):
                        for c in range(2):
                            bank = lv_ring.take(T)
                            T.settle()
                            T.did(dve.tensor_scalar(fox_c[:, h % 2, c * HALF:(c + 1) * HALF], bank[:, 0:HALF], -1.0, None, ALU.mult),
                                  lv_ring.drained)
                        T.settle()
                        for i in range(NT2):
                            m, w = SIZE[i], OFF[i] + SIZE[i]
                            T.wait(sem("fox_scores"), n + 1)
                            if n >= 2:
                                T.wait(sem("fox_turned"), FOX_TURNED[n - 2])
                            pair = psum[0:m, 0:2, :].rearrange("p b s -> p (b s)")
                            p = fox_p[0:m, n % 2, 0:w]
                            then(dve.scalar_tensor_tensor(p, pair[:, 0:w], c_col[0:m, i, h:h + 1], fox_c[0:m, h % 2, 0:w], ALU.add, ALU.add),
                                 sem("fox_scores_drained"))
                            diag = p[:, OFF[i]:w]
                            then(dve.tensor_tensor(diag, diag, CONST4(c4, "row_causal")[0:m, 0:m], ALU.add))
                            if n >= 2:
                                finish()
                            then(dve.tensor_reduce(row_max[0:m, n % 2:n % 2 + 1], p, AX.X, ALU.max))
                            then(dve.tensor_scalar(row_max[0:m, n % 2:n % 2 + 1], row_max[0:m, n % 2:n % 2 + 1], -1.0, None, ALU.mult),
                                 sem("fox_max"))
                            waiting.append((h, i, n))
                            n += 1
                    finish()
                    finish()
                    T.did(dve.memset(stat2, 0.0), sem("mix2_ready"))

                def add_rows(jobs=2):
                    for half in range(2):
                        for t in range(NT2):
                            m, part = SIZE[t], slice(half * 512, (half + 1) * 512)
                            bank = lv_ring.take(T)
                            T.did(dve.scalar_tensor_tensor(h2[0:m, t, part], h2[0:m, t, part], ALPHA2, bank[0:m, :], ALU.mult, ALU.add),
                                  lv_ring.drained)

                def norm():
                    T.wait(sem("layer_ln_landed"), 16 * (norms[0] + 1))
                    for n, (part, tiles) in enumerate(PARTS):
                        for t in range(tiles.start, tiles.stop):
                            T.settle()
                            for half in range(2):
                                T.did(dve.bn_stats(ln_stats[0:part, t, half * 6:half * 6 + 6], h2[0:part, t, half * 512:(half + 1) * 512]))
                            T.settle()
                            T.hold()
                            T.did(dve.bn_aggr(ln_mean[0:part, t, :], ln_stats[0:part, t, :]),
                                  sem("layer_ln_asked") if t == tiles.stop - 1 else None)
                        T.wait(sem("layer_ln_given"), 2 * norms[0] + n + 1)
                        v = ln_mean[0:part, tiles, 1:2]
                        then(dve.reciprocal(v, v))
                        for t in range(tiles.start, tiles.stop):
                            row = h2[0:part, t, :]
                            then(dve.tensor_scalar(row, row, ln_mean[0:part, t, 0:1], ln_mean[0:part, t, 1:2], ALU.subtract, ALU.mult))
                            then(dve.tensor_tensor(row, row, ln_par2[0:part, 0, :], ALU.mult))
                            then(dve.tensor_tensor(row, row, ln_par2[0:part, 1, :], ALU.add))
                    norms[0] += 1

                norms = [0]
                project()
                forget_gate()
                rotate()
                retention()
                pool()
                ret_norm()
                forget()
                add_rows()
                norm()
                T.did(dve.memset(stat2, 0.0), sem("mid_ready"))
                for f in range(FT):
                    for c in range(2):
                        bank = lv_ring.take(T)
                        g = ff_t[:, f, c * HALF:(c + 1) * HALF]
                        T.wait(la_ring.drained, 9 + 20 + 10 + 10 + 2 * f + c + 1)
                        T.did(dve.tensor_tensor(g, g, bank[:, 0:HALF], ALU.mult), lv_ring.drained)
                add_rows()
                norm()
                T.did(dve.memset(stat2, 0.0), sem("layer_start"))

            dve.sem_inc(lv_ring.drained, 3)
            dve.sem_inc(sem("retained_drained"), 2)
            dve.sem_inc(sem("fox_out_drained"), 2)
            with dve.Fori(0, LAYERS) as i:
                T = Turn(dve, i, sem("layer_vector_step"), LAYER_PER, LAYER_CREDIT, sem("passed"))
                layer(T)
                T.check()


def units(w, widths):
    w = np.ascontiguousarray(w)
    k, n = w.shape
    pieces = -(-n // 512)
    out = np.zeros((pieces, P, k // P, 512), np.float32)
    for i in range(pieces):
        part = w[:, i * 512:(i + 1) * 512]
        out[i, :, :, 0:part.shape[1]] = part.reshape(k // P, P, -1).transpose(1, 0, 2)
    return out.reshape(pieces, P, -1)


def columns(v):
    return np.asarray(v).reshape(-1, P).T


def layout_block1(a):
    w = np.asarray(a["w_in"])[0]
    names = dict(z=W, xbc=512, dt=H, rwkv=896, gqk=W, gv=W, gd=16, gog=W, mqk=512, mv=W, i=H, f=H, mog=W)
    at, part = 0, {}
    for name, n in names.items():
        part[name] = w[:, at:at + n]
        at += n
    assert at == w.shape[1]
    rows = np.zeros((D, P), np.float32)
    for name, at in (("dt", 0), ("i", 32), ("f", 64), ("gd", 96)):
        rows[:, at:at + part[name].shape[1]] = part[name]
    order = [part["xbc"], part["mqk"], part["gqk"], part["rwkv"], rows, part["gog"], part["z"], part["mv"],
             part["mog"], part["gv"]]
    w_in = units(np.concatenate(order, 1), None)
    io = {"x_t": np.ascontiguousarray(np.asarray(a["x"])[0].T.reshape(KT, P, SEQ).transpose(1, 0, 2))}
    io["weights1"] = np.concatenate([w_in, units(np.asarray(a["w_out"])[0], None)])
    io["const1"] = const1()
    io["const2"] = const2()
    cols = np.zeros((P, COLS.width), np.float32)
    for name, tiles in (("ssd", 4), ("m", 4)):
        cw = np.asarray(a[{"ssd": "ssd_conv_w", "m": "mlstm_conv_w"}[name]])[0]
        COLS(cols, name + "_cw")[:] = cw.reshape(4, tiles, P).transpose(2, 1, 0).reshape(P, 16)
        COLS(cols, name + "_cb")[:] = columns(a[{"ssd": "ssd_conv_b", "m": "mlstm_conv_b"}[name]])
    for name, key in (("mu", "rwkv_mu"), ("w0", "rwkv_w0"), ("a0", "rwkv_a0"), ("k_k", "rwkv_k_k"),
                      ("k_a", "rwkv_k_a"), ("r_k", "rwkv_r_k"), ("gate_b", "gla_gate_b")):
        COLS(cols, name)[:] = columns(a[key])
    b = COLS(cols, "rows_b")
    for key, at in (("ssd_dt_bias", 0), ("mlstm_i_b", 32), ("mlstm_f_b", 64)):
        b[at:at + H, 0] = np.asarray(a[key])[0]
    COLS(cols, "a_log")[0:H, 0] = np.asarray(a["ssd_a_log"])[0]
    io["cols"] = cols
    rows = [np.asarray(a[key]).reshape(-1) for key in
            ("ssd_d", "ssd_norm_g", "rwkv_ln_g", "rwkv_ln_b", "gla_norm_g", "mlstm_norm_g")]
    io["rows"] = np.concatenate(rows)[None]
    io["lora_up"] = np.concatenate([np.asarray(a[k])[0] for k in ("rwkv_w_up", "rwkv_a_up", "rwkv_g_up")])
    io["gate_up"] = np.asarray(a["gla_gate_up"])[0]
    io["const3"] = const3()
    io["x"] = np.ascontiguousarray(np.asarray(a["x"])[0].reshape(TT, P, D).transpose(1, 0, 2))
    io["p_t"] = np.ascontiguousarray(np.asarray(a["p"])[0, 0].T.reshape(2, P, SEQ).transpose(1, 0, 2))
    for n in "12":
        io["ln" + n] = np.concatenate([np.asarray(a[f"ln{n}_g"])[0], np.asarray(a[f"ln{n}_b"])[0]])[None]
    io["router_w"] = np.ascontiguousarray(np.asarray(a["router_w"])[0].reshape(KT, P, E).transpose(1, 0, 2))
    io["router_b"] = np.asarray(a["router_b"])
    io["b_down"] = np.asarray(a["exp_b_down"])[0]
    io["b_gu"] = np.ascontiguousarray(np.asarray(a["exp_b_gu"])[0].reshape(E, 2, 4, 256).transpose(0, 2, 1, 3).reshape(E, 2 * D))
    io["ple_gate"] = units(np.asarray(a["ple_gate_w"])[0], None)
    io["ple_proj"] = np.ascontiguousarray(np.asarray(a["ple_proj"])[0].reshape(2, P, D).transpose(1, 0, 2)).reshape(P, 2 * D)
    gu = np.asarray(a["exp_w_gu"])[0].reshape(E, KT, P, 2, 4, 256)
    io["exp_gu"] = np.ascontiguousarray(gu.transpose(0, 4, 2, 1, 3, 5)).reshape(E * 4, P, PIECE)
    down = np.asarray(a["exp_w_down"])[0].reshape(E, KT, P, 2, 512)
    io["exp_down"] = np.ascontiguousarray(down.transpose(0, 3, 2, 1, 4)).reshape(E * 2, P, PIECE)
    return io


def layout_block2(a):
    g = {k[:-2]: np.asarray(v) for k, v in a.items() if k.endswith("_2")}
    pieces = []
    for l in range(LAYERS):
        w = g["w_in"][l]
        names = dict(qr=192, kr=192, vr=384, gr=384, u=256, qf=384, kf=384, vf=384, f=FH)
        at, part = 0, {}
        for name, n in names.items():
            part[name] = w[:, at:at + n]
            at += n
        pieces.append(units(np.concatenate([part[n] for n in ("qr", "kr", "vr", "gr", "u", "vf", "qf", "kf")], 1), None))
        pieces.append(units(g["w_out"][l], None))
        w1, w3 = (g[n][l].reshape(D, FT // 2, 256) for n in ("w_ffn1", "w_ffn3"))
        pieces.append(units(np.concatenate([w1, w3], 2).reshape(D, 2 * FF), None))
        w2 = np.zeros((3 * D, D), np.float32)
        w2[0:FF] = g["w_ffn2"][l]
        w2 = w2.reshape(3, KT, P, 2, 512).transpose(3, 0, 2, 1, 4)
        pieces.append(w2.reshape(6, P, PIECE))
    io = {"weights2": np.concatenate(pieces)}
    f_w = g["w_in"][:, :, -FH:].reshape(LAYERS, KT, P, FH).transpose(0, 2, 1, 3)
    io["f_w"] = np.ascontiguousarray(f_w).reshape(LAYERS, P, KT * FH)
    io["f_b"] = g["b_f"].reshape(LAYERS, FH, 1)
    pool = np.zeros((LAYERS, 2, HD, 2, 2, HD), np.float32)
    for i in range(2):
        pool[:, i, :, :, i, :] = g["pool_w"].reshape(LAYERS, 2, 2, HD, HD)[:, :, i].transpose(0, 2, 1, 3)
    io["pool_w"] = pool.reshape(LAYERS, P, 4 * HD)
    io["rows2"] = np.concatenate([g["ret_gn_g"], g["pool_scale"]], 1)
    io["meta"] = g["meta"]
    io["ln_emb"] = np.concatenate([g["ln_emb_g"], g["ln_emb_b"]])[None]
    io["ln_mid"] = np.concatenate([g["ln1_g"], g["ln1_b"]], 1)
    io["ln_end"] = np.concatenate([g["ln2_g"], g["ln2_b"]], 1)
    io["const4"] = const4()
    io["retention_decay"] = retention_decay()
    return io


def layout(a):
    io = {**layout_block1(a), **layout_block2(a)}
    return {name: np.ascontiguousarray(v) for name, v in io.items()}


def kernel(**inputs):
    import concourse.bacc as bacc
    from concourse.bass_utils import run_bass_kernel_spmd

    arrays = layout(inputs)
    nc = bacc.Bacc("TRN2", target_bir_lowering=False, num_devices=1)
    io = {name: nc.dram_tensor(name, v.shape, F32, kind="ExternalInput").ap() for name, v in arrays.items()}
    out = nc.dram_tensor("out", (1, SEQ, D), F32, kind="ExternalOutput").ap()
    io["out"] = out.rearrange("o s d -> (o s) d")
    build(nc, io)
    result = run_bass_kernel_spmd(nc, [arrays], core_ids=[0])
    return result.results[0]["out"]
```

```python
from contextlib import ExitStack

import concourse.bass as bass
import numpy as np
from concourse import mybir

F32 = mybir.dt.float32
ALU = mybir.AluOpType
ACT = mybir.ActivationFunctionType
AX = mybir.AxisListType

P = 128
D = 1024
KT = D // P
SEQ = 512
TT = SEQ // P
H = 4
HD = 64
W = H * HD
CH = 64
E = 32
TOP = 4
SWIGLU_ALPHA, SWIGLU_LIMIT = 1.702, 7.0
EXTRA = SEQ * TOP // P - 1
MIN_BLOCKS = 2
HALF_AT = E + EXTRA + 1
NB = HALF_AT + E + 1
HALF_ROWS = P // 2
KINDS = 5
ALPHA1 = 2 ** 0.25
ALPHA2 = 4 ** 0.25
LN_EPS = 1e-5
GN_EPS_RWKV = 64e-5
NEG = -1e30

SLOTS = 6
PIECE = KT * 512
PAD = 3

F_SSD, F_MQK, F_GLA, F_RWKV, F_ROWS = 0, 4, 8, 10, 17
NF = 18
T_Z, T_MV, T_MOG, T_GV, T_GOG = 0, 256, 512, 768, 1024
NT = 1280


META = 16
LEN = META + SEQ
NT2 = TT + 1
OFF = [0] + [META + P * t for t in range(TT)]
SIZE = [META] + [P] * TT
LAYERS = 2
RH, RK, RV = 4, 48, 96
WINDOWS = (2, 4, 8, 16)
FH = 6
FF = 2816
FT = FF // P
HALF = LEN // 2
U_QK, U_V, U_G, U_U, U_VF = 0, 384, 768, 1152, 1408
NU = 1792
W_OUT, W_FFN, W_DOWN, LAYER_PIECES = 5, 7, 18, 24

LAYER_SIGNALS = dict(
    early_slots_free=1, forget_asked=1, forget_given=1, fox_max=30, fox_out=30, fox_out_drained=30, fox_scores=30,
    fox_scores_drained=30, fox_turned=36, fox_turned_drained=36, fox_weights_ready=30, layer_scalar_drained=90,
    layer_scalar_filled=90, layer_scalar_step=29, layer_start=5, layer_vector_drained=135, layer_vector_filled=135,
    layer_vector_step=163, mid_ready=5, mix2_ready=1, ret_gate_ready=2, retained_drained=4, retention_done=24,
    root_ready=12, rotated_ready=5, variance_ready=12,
    layer_params_landed=16 * 5, retention_decay_landed=16, layer_ln_landed=16 * 2,
    **{f"layer_weights_landed_{s}": 16 * LAYER_PIECES // SLOTS for s in range(SLOTS)})


class Layout:

    def __init__(self, **widths):
        self.at, self.width = {}, 0
        for name, w in widths.items():
            self.at[name] = (self.width, w)
            self.width += w

    def __call__(self, tensor, name, a=0, b=None):
        at, w = self.at[name]
        return tensor[:, at + a:at + (w if b is None else b)]


CONST1 = Layout(ident=P, causal=SEQ, select=H * P, eps=1, ones=P)
CONST2 = Layout(mask4=4 * P, lower=P, level=12 * P, headones=P, headsum=2, reset=SEQ, glamask=W)
CONST3 = Layout(before=P, iota=P, expert=P)
CONST4 = Layout(pool=4 * P, pool_before=4 * P, pool_meta=4 * P, pool_first=4 * META, cos=NT2 * 24, sin=NT2 * 24, row_causal=P)
ROWS2 = Layout(ret_g=RH * RV, pool_scale=4 * HD)
COLS = Layout(ssd_cw=16, ssd_cb=4, m_cw=16, m_cb=4, mu=7, w0=2, a0=2, k_k=2, k_a=2, r_k=2, gate_b=1,
              rows_b=1, a_log=1)
ROWS = Layout(ssd_d=H, ssd_g=W, rwkv_g=W, rwkv_b=W, gla_g=W, m_g=W)


def const1():
    c = np.zeros((P, CONST1.width), np.float32)
    s = np.arange(P)[:, None]
    CONST1(c, "ident")[:] = np.eye(P)
    CONST1(c, "causal")[:] = np.where(np.arange(SEQ)[None] >= s, 0.0, NEG)
    CONST1(c, "select")[:] = (np.arange(H * P)[None] // P == s)
    CONST1(c, "eps")[:] = LN_EPS
    CONST1(c, "ones")[:] = 1.0
    return c


def const2():
    c = np.zeros((P, CONST2.width), np.float32)
    s, t = np.arange(P)[:, None], np.arange(P)[None]
    same = s // CH == t // CH
    strict, incl = same & (s < t), same & (s <= t)
    CONST2(c, "mask4")[:] = np.concatenate([strict, incl, strict, incl], 1)
    CONST2(c, "lower")[:] = same & (s > t)
    levels = []
    for n in (1, 2, 4, 8, 16, 32):
        off = (s // (2 * n) == t // (2 * n)) & (s % (2 * n) >= n) & (t % (2 * n) < n)
        levels += [off, off.T]
    CONST2(c, "level")[:] = np.concatenate(levels, 1)
    CONST2(c, "headones")[:] = s // HD == t // HD
    CONST2(c, "headsum")[:] = s // HD == np.arange(2)[None]
    CONST2(c, "reset")[:] = (np.arange(SEQ)[None] % CH != 0)
    CONST2(c, "glamask")[:] = s // (P // H) == np.arange(W)[None] // HD
    return c


def const3():
    c = np.zeros((P, CONST3.width), np.float32)
    s, t = np.arange(P)[:, None], np.arange(P)[None]
    CONST3(c, "before")[:] = s < t
    CONST3(c, "iota")[:] = t
    CONST3(c, "expert")[:] = s
    return c


def const4():
    c = np.zeros((P, CONST4.width), np.float32)
    s, t = np.arange(P)[:, None], np.arange(P)[None]

    def pool(w, s, t, first=False):
        count = np.minimum(t + 1, w) if first else w
        return ((s <= t) & (s > t - w)) / count - (s == t)

    for g, w in enumerate(WINDOWS):
        CONST4(c, "pool", g * P, (g + 1) * P)[:] = pool(w, s, t)
        CONST4(c, "pool_before", g * P, (g + 1) * P)[:] = pool(w, s - P, t)
        CONST4(c, "pool_meta", g * P, (g + 1) * P)[0:META] = pool(w, s[0:META] - META, t)
        CONST4(c, "pool_first", g * META, (g + 1) * META)[0:META] = pool(w, s[0:META], t[:, 0:META], True)
    freq = 10000.0 ** (-np.arange(24) / 24)
    for i in range(NT2):
        angle = (OFF[i] + np.arange(SIZE[i]))[:, None] * freq[None]
        CONST4(c, "cos", i * 24, (i + 1) * 24)[0:SIZE[i]] = np.cos(angle)
        CONST4(c, "sin", i * 24, (i + 1) * 24)[0:SIZE[i]] = np.sin(angle)
    CONST4(c, "row_causal")[:] = np.where(t <= s, 0.0, NEG)
    return c


def retention_decay():
    s, t = np.arange(P)[:, None], np.arange(LEN)[None]
    gamma = 1.0 - 2.0 ** (-5.0 - np.arange(RH))
    return np.concatenate([np.where(t >= s, g ** np.maximum(t - s, 0) * RK ** -0.5, 0.0) for g in gamma], 1).astype(np.float32)


class Steps:

    def __init__(self, engine, own):
        self.engine, self.own, self.count, self.last = engine, own, {}, None

    def did(self, instruction, sem=None):
        sem = self.own if sem is None else sem
        instruction.then_inc(sem, 1)
        self.count[sem.name] = self.count.get(sem.name, 0) + 1
        self.last = (sem, self.count[sem.name])
        return self.count[sem.name]

    def settle(self):
        self.engine.wait_ge(*self.last)

    def wait(self, sem, n):
        self.engine.wait_ge(sem, n)

    def hold(self):
        pass


class Turn:

    def __init__(self, engine, i, own, per, credit, passed=None):
        self.engine, self.i, self.own, self.per, self.credit, self.passed = engine, i, own, per, credit, passed
        self.count, self.last = {}, None

    def value(self, sem, n):
        return self.i * self.per[sem.name] + (self.credit.get(sem.name, 0) + n)

    def wait(self, sem, n):
        self.engine.wait_ge(sem, self.value(sem, n))

    def did(self, instruction, sem=None):
        sem = self.own if sem is None else sem
        instruction.then_inc(sem, 1)
        self.count[sem.name] = self.count.get(sem.name, 0) + 1
        assert self.count[sem.name] <= self.per[sem.name]
        self.last = (sem, self.count[sem.name])

    def settle(self):
        self.wait(*self.last)

    def hold(self):
        self.engine.sem_inc(self.passed, 1)

    def check(self):
        for name, n in self.count.items():
            assert n == self.per[name], (name, n)


class TurnRing:

    def __init__(self, psum, first, filled, drained, banks=3):
        self.psum, self.first, self.filled, self.drained, self.banks = psum, first, filled, drained, banks
        self.sent = self.taken = 0

    def bank(self, turn):
        turn.wait(self.drained, self.sent + 1 - self.banks)
        return self.psum[:, self.first + self.sent % self.banks, :]

    def ship(self, turn, matmul):
        turn.did(matmul, self.filled)
        self.sent += 1
        return self.sent

    def take(self, turn):
        self.taken += 1
        turn.wait(self.filled, self.taken)
        return self.psum[:, self.first + (self.taken - 1) % self.banks, :]


class BankRing:

    def __init__(self, psum, first, filled, drained, banks=3):
        self.psum, self.first, self.filled, self.drained, self.banks = psum, first, filled, drained, banks
        self.sent = self.taken = 0

    def bank(self, pe):
        if self.sent >= self.banks:
            pe.wait_ge(self.drained, self.sent - self.banks + 1)
        return self.psum[:, self.first + self.sent % self.banks, :]

    def ship(self, matmul):
        matmul.then_inc(self.filled, 1)
        self.sent += 1
        return self.sent

    def take(self, engine):
        self.taken += 1
        engine.wait_ge(self.filled, self.taken)
        return self.psum[:, self.first + (self.taken - 1) % self.banks, :]


def build(nc, io):
    with ExitStack() as ctx:
        sems = {}

        def sem(name):
            if name not in sems:
                sems[name] = ctx.enter_context(nc.semaphore(name))
            return sems[name]

        def sb(name, words):
            return ctx.enter_context(nc.sbuf_tensor(name, [P, words], F32))

        ring = sb("weight_ring", SLOTS * PIECE)
        arena_words = 28600
        arena = sb("arena", arena_words)
        psum = ctx.enter_context(nc.psum_tensor("psum", [P, 8, 512], F32))
        used = [0]

        def take(words):
            at = used[0]
            used[0] += words
            assert used[0] <= arena_words, (used[0], arena_words)
            return arena[:, at:at + words]

        slot = [ring[:, s * PIECE:(s + 1) * PIECE].rearrange("p (k n) -> p k n", k=KT) for s in range(SLOTS)]

        c1 = take(CONST1.width)
        cols = take(COLS.width)
        rows = take(ROWS.width)
        lora_up = take(W)
        gate_up = take(P)
        y = take(TT * D).rearrange("p (t d) -> p t d", t=TT)
        small = take(256)
        u_tok = take(TT * NT).rearrange("p (t n) -> p t n", t=TT)
        u_feat = take(NF * (PAD + SEQ)).rearrange("p (i s) -> p i s", i=NF)
        mixer_base = used[0]
        ident = CONST1(c1, "ident")
        ones = CONST1(c1, "ones")
        x_t = take(KT * SEQ).rearrange("p (k s) -> p k s", k=KT)
        used[0] = mixer_base
        hrow = take(6 * SEQ).rearrange("p (r s) -> p r s", r=6)
        row_cast = take(2 * SEQ).rearrange("p (r s) -> p r s", r=2)
        decay = take(2 * SEQ).rearrange("p (r s) -> p r s", r=2)
        conv_acc = y[:, 0, :].rearrange("p (b s) -> p b s", b=2)
        weigh = take(2 * SEQ).rearrange("p (r s) -> p r s", r=2)
        xs_tok = y[:, :, 256:512]
        feat_flat = u_feat.rearrange("p i s -> p (i s)")
        norm_tmp = feat_flat[:, 0:TT * W]
        used[0] = mixer_base
        c2 = take(CONST2.width)
        spare = take(3600)
        gla_la, gla_cum, gla_tmp = (spare[:, i * SEQ:(i + 1) * SEQ] for i in range(3))
        gla_kdec = spare[:, 3 * SEQ:4 * SEQ].rearrange("p (t c) -> p t c", t=TT)
        gla_st = spare[:, 4 * SEQ:6 * SEQ].rearrange("p (b h s) -> p b h s", b=2, h=H)
        gla_state = feat_flat[:, 1024:1024 + 8 * W].rearrange("p (c d) -> p c d", c=8)
        gla_eb = small[:, 96:104]
        r_at = feat_flat[:, 0:2048].rearrange("p (t f k s) -> p t f k s", t=TT, f=2, k=2)
        r_bk = feat_flat[:, 2048:4096].rearrange("p (k t f s) -> p k t f s", k=2, t=TT, f=2)
        r_tmp = feat_flat[:, 4096:5120].rearrange("p (t f s) -> p t f s", t=TT, f=2)
        r_dec = spare[:, 0:2048].rearrange("p (k t f s) -> p k t f s", k=2, t=TT, f=2)
        r_lw, r_cw = r_dec[:, 0], r_dec[:, 1]
        r_kk = spare[:, 2048:3072].rearrange("p (t f s) -> p t f s", t=TT, f=2)
        r_a, r_t1, r_t2 = (u_tok[:, :, c:c + W].rearrange("p t (f s) -> p t f s", f=2) for c in (512, 768, 1024))
        g_tok, v_tok = u_tok[:, :, 0:W], u_tok[:, :, W:2 * W]
        r_wl = small[:, 104:120].rearrange("p (t f c) -> p t f c", t=TT, f=2)
        r_bonus = small[:, 120:136].rearrange("p (t h) -> p t h", t=TT)
        r_omka = small[:, 136:138]
        c_area = feat_flat[:, F_RWKV * (PAD + SEQ):(F_RWKV + 7) * (PAD + SEQ)]
        r_mt = c_area[:, 0:2048].rearrange("p (f k g q s) -> p f k g q s", f=2, k=2, g=2, q=2)
        r_x, r_xt, r_prod = (c_area[:, 2048 + i * 512:2560 + i * 512].rearrange("p (h s) -> p h s", h=H) for i in range(3))
        r_anv, r_xau, r_mot, r_mlo = (u_tok[:, :, 512 + i * P:512 + (i + 1) * P] for i in range(4))
        r_dtok = u_tok[:, :, 1024:1024 + P]
        r_rot = spare[:, 2048:2304].rearrange("p (f s) -> p f s", f=2)
        r_gt = spare[:, 2304:2816].rearrange("p (c f v) -> p c f v", c=2, f=2)
        r_state = spare[:, 2816:3584].rearrange("p (n f v) -> p n f v", n=3, f=2)
        r_atm = feat_flat[:, 4096:5120].rearrange("p (f g k s) -> p f g k s", f=2, g=2, k=2)
        gla_qm = y[:, :, W:2 * W].rearrange("p b (h s) -> p b h s", h=2)
        R_DT, R_NF, R_M, R_F, R_G, R_A = range(6)
        hcol = small[:, 0:64].rearrange("p (k t h) -> p k t h", k=4, t=TT)
        expa = small[:, 64:65]
        den = small[:, 68:72]
        stat = small[:, 80:96]

        at_y = CONST1.width + COLS.width + ROWS.width + W + P
        at_tok = at_y + TT * D + 256
        at_feat = at_tok + TT * NT
        at_mix = at_feat + NF * (PAD + SEQ)
        ffn = y
        x1 = arena[:, at_tok:at_tok + TT * D].rearrange("p (t d) -> p t d", t=TT)
        y_t = arena[:, at_feat:at_feat + KT * SEQ].rearrange("p (k s) -> p k s", k=KT)
        x1_t = arena[:, at_mix:at_mix + KT * SEQ].rearrange("p (k s) -> p k s", k=KT)
        ln_emb = ring[:, (3 + 2) % SLOTS * PIECE + 2 * D:(3 + 2) % SLOTS * PIECE + 4 * D].rearrange("p (k d) -> p k d", k=2)
        ln_par = arena[:, at_mix + KT * SEQ:at_mix + KT * SEQ + 2 * D].rearrange("p (k d) -> p k d", k=2)
        used[0] = at_mix + KT * SEQ + 2 * D
        router_w = take(KT * E).rearrange("p (k e) -> p k e", k=KT)
        router_b = take(E)
        block_expert = take(NB).bitcast(mybir.dt.int32)
        block_count = take(2).bitcast(mybir.dt.int32)
        ln_stats = take(5 * 12).rearrange("p (t s) -> p t s", t=5)
        ln_mean = take(5 * 2).rearrange("p (t s) -> p t s", t=5)
        used[0] = at_feat + KT * SEQ
        c3 = take(CONST3.width)
        b_down = take(D)
        to_block, from_block = (take(TT * P).rearrange("p (t r) -> p t r", t=TT) for _ in range(2))
        from_t = take(TT * P)
        gates, assigned, logits, pos = (take(TT * E).rearrange("p (t e) -> p t e", t=TT) for _ in range(4))
        gates_t = take(SEQ)
        pos_t = from_t
        top, top_i, gate4 = (take(TT * 8).rearrange("p (t e) -> p t e", t=TT) for _ in range(3))
        rank = take(32)
        hot, base_w = take(NB), take(NB)
        block_pos, block_gate = (take(TT * NB).rearrange("p (t n) -> p t n", t=TT) for _ in range(2))
        assert used[0] <= at_mix
        half_iota = assigned.rearrange("p t e -> p (t e)")
        used[0] = at_feat
        xg = take(KT * P).rearrange("p (k r) -> p k r", k=KT)
        hid = take(D)
        hid_t = take(KT * P).rearrange("p (k r) -> p k r", k=KT)
        y_blk = take(D)
        b_gu = arena[:, at_mix:at_mix + 2 * D]
        swi = arena[:, at_mix + 2 * D:at_mix + 2 * D + 1024]
        h_t = y_t
        p_t = arena[:, at_mix + 2 * D:at_mix + 2 * D + 2 * SEQ].rearrange("p (k s) -> p k s", k=2)
        ple_gate = arena[:, at_mix:at_mix + TT * 512].rearrange("p (b s) -> p b s", b=TT)
        ev_ring = TurnRing(psum, 0, sem("expert_vector_filled"), sem("expert_vector_drained"))
        ea_ring = TurnRing(psum, 3, sem("expert_scalar_filled"), sem("expert_scalar_drained"))
        expert_landed = [sem(f"expert_landed_{k}") for k in range(6)]
        landed2 = [sem(f"late_weights_landed_{k}") for k in range(SLOTS)]
        slot_free2 = {}
        hidden_ready, swish_asked, swish_given = sem("hidden_ready"), sem("swish_asked"), sem("swish_given")
        to_ready, from_ready, bias_landed = sem("to_block_ready"), sem("from_block_ready"), sem("bias_landed")
        PER = {ev_ring.filled.name: 12, ev_ring.drained.name: 12, ea_ring.filled.name: 9, ea_ring.drained.name: 9,
               hidden_ready.name: 4, swish_asked.name: 4, swish_given.name: 4, to_ready.name: 1, from_ready.name: 1,
               bias_landed.name: 16, **{x.name: 16 for x in expert_landed}}
        CREDIT = {ev_ring.filled.name: 12, ev_ring.drained.name: 12 + 3, ea_ring.filled.name: 9, ea_ring.drained.name: 3}
        hv_ring = TurnRing(psum, 0, sem("half_vector_filled"), sem("half_vector_drained"))
        ha_ring = TurnRing(psum, 3, sem("half_scalar_filled"), sem("half_scalar_drained"))
        half_landed = [sem(f"half_landed_{k}") for k in range(6)]
        half_hidden, half_asked, half_given = sem("half_hidden_ready"), sem("half_swish_asked"), sem("half_swish_given")
        half_to_ready, half_from_ready, half_bias = sem("half_to_block_ready"), sem("half_from_block_ready"), sem("half_bias_landed")
        HALF_PER = {hv_ring.filled.name: 12, hv_ring.drained.name: 12, ha_ring.filled.name: 6, ha_ring.drained.name: 6,
                    half_hidden.name: 2, half_asked.name: 2, half_given.name: 2, half_to_ready.name: 1,
                    half_from_ready.name: 1, half_bias.name: 32, **{x.name: 16 for x in half_landed}}
        HALF_CREDIT = {hv_ring.filled.name: 12, hv_ring.drained.name: 12 + 3, ha_ring.filled.name: 6, ha_ring.drained.name: 3}
        HALF_DOWN = 5

        def block_counts(engine):
            return (engine.value_load(block_count[0:1, 0:1], min_val=MIN_BLOCKS, max_val=E + EXTRA),
                    engine.value_load(block_count[0:1, 1:2], min_val=MIN_BLOCKS, max_val=E))

        used[0] = CONST1.width
        rows2 = take(ROWS2.width)
        assert used[0] <= at_y - D
        h2 = arena[:, at_y - D:at_y + TT * D].rearrange("p (t d) -> p t d", t=NT2)
        used[0] = at_y + TT * D
        small2 = take(200)
        h2_t = take(KT * LEN)
        retained = h2_t[:, 0:4 * LEN].rearrange("p (h s) -> p h s", h=4)
        rotated = h2_t[:, 4 * LEN:8 * LEN].rearrange("p (u s) -> p u s", u=4)
        fox_c = h2_t[:, 0:2 * LEN].rearrange("p (b s) -> p b s", b=2)
        fox_p = h2_t[:, 2 * LEN:5 * LEN].rearrange("p (b s) -> p b s", b=3)
        fox_pt = h2_t[:, 5 * LEN:5 * LEN + 2 * NT2 * P].rearrange("p (b j s) -> p b j s", b=2, j=NT2)
        h2_t = h2_t.rearrange("p (k s) -> p k s", k=KT)
        at_qk = used[0]
        qk_f = take(6 * LEN).rearrange("p (u s) -> p u s", u=6)
        u2 = take(NT2 * NU).rearrange("p (t n) -> p t n", t=NT2)
        ff_t = arena[:, at_qk:at_qk + FT * LEN].rearrange("p (f s) -> p f s", f=FT)
        assert at_qk + FT * LEN <= used[0]
        c4 = take(CONST4.width)
        pool_w = take(4 * HD).rearrange("p (u d) -> p u d", u=2)
        f_w = take(KT * FH).rearrange("p (k h) -> p k h", k=KT)
        f_b = take(1)
        ln_par2 = arena[:, used[0]:used[0] + 2 * D].rearrange("p (k d) -> p k d", k=2)
        f_row = take(2 * LEN).rearrange("p (r s) -> p r s", r=2)
        work = take(2 * 512).rearrange("p (b s) -> p b s", b=2)
        c_col = small2[:, 0:NT2 * FH].rearrange("p (t h) -> p t h", t=NT2)
        stat2 = small2[:, 32:52]
        row_max, row_sum = small2[:, 52:56], small2[:, 56:60]
        lv_ring = TurnRing(psum, 0, sem("layer_vector_filled"), sem("layer_vector_drained"))
        la_ring = TurnRing(psum, 3, sem("layer_scalar_filled"), sem("layer_scalar_drained"))

        layer_landed = [sem(f"layer_weights_landed_{s}") for s in range(SLOTS)]
        layer_free, layer_mark = {}, {}
        LATE = (3 + 3) % SLOTS
        WIDTHS = (512, 512, 512, 256)
        ROTATED = [*range(1, NT2), 0]
        PROJECTED = 1 + 2 * TT + 4 * TT + 1
        PARTS = ((META, slice(0, 1)), (P, slice(1, NT2)))
        SEGMENTS = [(0, 0, OFF[3]), (0, OFF[3], LEN)] + [(i, OFF[i], LEN) for i in range(1, NT2)]
        FOX_TURNED = []
        for n in range(FH * NT2):
            FOX_TURNED.append((FOX_TURNED[-1] if n else 0) + (2 if n % NT2 == NT2 - 1 else 1))
        EARLY_ROOTS = 4 + TT + 1 + 2 * TT
        LAYER_PER = LAYER_SIGNALS
        LAYER_CREDIT = {lv_ring.drained.name: 3, la_ring.drained.name: 3, "retained_drained": 2, "early_slots_free": 1,
                        "variance_ready": EARLY_ROOTS, "root_ready": EARLY_ROOTS, "fox_turned_drained": 2,
                        "fox_out_drained": 2}

        v_ring = BankRing(psum, 0, sem("vector_bank_filled"), sem("vector_bank_drained"))
        a_ring = BankRing(psum, 3, sem("scalar_bank_filled"), sem("scalar_bank_drained"))
        x_landed, setup_landed = sem("x_landed"), sem("setup_landed")
        landed = [sem(f"weights_landed_{s}") for s in range(SLOTS)]
        dve_step, act_step = sem("vector_step"), sem("scalar_step")
        conv_summed, conv_ready = sem("conv_summed"), sem("conv_ready")
        rows_biased, rows_softplus, hrow_ready, hcol_ready = sem("rows_biased"), sem("rows_softplus"), sem("hrow_ready"), sem("hcol_ready")
        decay_arg, decay_ready, pv_done = sem("decay_arg"), sem("decay_ready"), sem("pv_done")
        sums_drained = sem("sums_drained")
        z_ready = sem("z_ready")
        variance_ready, root_ready = sem("variance_ready"), sem("root_ready")
        out_landed = sem("out_landed")

        SETUP = [(c1, "const1"), (cols, "cols"), (rows, "rows"), (lora_up, "lora_up"), (gate_up, "gate_up")]
        slot_free = {}
        mark = {}

        def heads_of(view, n):
            return view.rearrange("p t (h d) -> p t h d", h=n)

        block = ctx.enter_context(nc.Block())

        @block.tensor
        def _(pe):
            def piece(n):
                pe.wait_ge(landed[n % SLOTS], 16 * (n // SLOTS + 1))
                return slot[n % SLOTS]

            def transpose(out, in_, parts=P):
                return pe.transpose(out, in_, ident[0:parts, 0:parts] if parts < P else ident)

            def project_block1():
                pe.wait_ge(x_landed, 16)
                for i in range(NF):
                    w = piece(i // 4)
                    bank = v_ring.bank(pe)
                    for k in range(KT):
                        mm = pe.matmul(bank, w[:, k, i % 4 * P:(i % 4 + 1) * P], x_t[:, k, :],
                                       start=(k == 0), stop=(k == KT - 1))
                    slot_free[i // 4] = (v_ring.filled, v_ring.ship(mm))
                for n, a, width in ((4, 256, 256), (5, 0, 512), (6, 0, 512)):
                    w = piece(n)
                    for t in range(TT):
                        bank = a_ring.bank(pe)
                        for k in range(KT):
                            mm = pe.matmul(bank[:, 0:width], x_t[:, k, t * P:(t + 1) * P], w[:, k, a:a + width],
                                           start=(k == 0), stop=(k == KT - 1))
                        slot_free[n] = (a_ring.filled, a_ring.ship(mm))
                mark["projected"] = a_ring.sent

            def head_columns():
                pe.wait_ge(setup_landed, 16 * len(SETUP))
                pe.wait_ge(hrow_ready, 1)
                bank = v_ring.bank(pe)
                for kind, r in enumerate((R_DT, R_A, R_G, R_F)):
                    for t in range(TT):
                        mm = transpose(bank[:, kind * 16 + t * 4:kind * 16 + t * 4 + 4],
                                       hrow[0:4, r, t * P:(t + 1) * P], 4)
                v_ring.ship(mm)

            def ssd_values():
                pe.wait_ge(conv_ready, 2)
                for t in range(TT):
                    bank = v_ring.bank(pe)
                    for i in range(2):
                        mm = transpose(bank[:, i * P:(i + 1) * P], u_feat[:, F_SSD + i, PAD + t * P:PAD + (t + 1) * P])
                    v_ring.ship(mm)
                mark["ssd_values"] = v_ring.sent

            def decayed_attention():
                waiting = []

                def weigh_values():
                    n, job = waiting.pop(0)
                    g, i = n // TT, n % TT
                    m, h = g // H, g % H
                    sums = psum[:, 6 + g % 2, :]
                    pe.wait_ge(v_ring.drained, job)
                    if i == 0 and g >= 2:
                        pe.wait_ge(sums_drained, g - 1)
                    for j in range(i, TT):
                        keys = weigh[:, n % 2, (j - i) * P:(j - i + 1) * P]
                        values = (xs_tok[:, i, h * HD:(h + 1) * HD] if m == 0
                                  else u_tok[:, i, T_MV + h * HD:T_MV + (h + 1) * HD])
                        mm = pe.matmul(sums[:, j * HD:(j + 1) * HD], keys, values, start=(i == 0 and j == 0),
                                       stop=(i == TT - 1), skip_group_check=True)
                        if m == 1:
                            mm = pe.matmul(sums[:, TT * HD + j:TT * HD + j + 1], keys, ones[:, 0:1], start=False,
                                           stop=(i == TT - 1), skip_group_check=True)
                    mm.then_inc(pv_done, 1)

                for g in range(2 * H):
                    m, h = g // H, g % H
                    bank = v_ring.bank(pe)
                    v_ring.ship(pe.matmul(bank, CONST1(c1, "select", h * P, (h + 1) * P)[0:4, :],
                                          hrow[0:4, R_A if m == 0 else R_M, :], start=True, stop=True))
                    for i in range(TT):
                        if m == 0:
                            keys, queries = u_feat[:, F_SSD + 2, :], u_feat[:, F_SSD + 3, :]
                        else:
                            half = slice(h % 2 * HD, h % 2 * HD + HD)
                            keys, queries = u_feat[half, F_MQK + 2 + h // 2, :], u_feat[half, F_MQK + h // 2, :]
                        pe.wait_ge(conv_ready, 4 if m == 0 else 8)
                        bank = v_ring.bank(pe)
                        mm = pe.matmul(bank[:, 0:SEQ - i * P], keys[:, PAD + i * P:PAD + (i + 1) * P],
                                       queries[:, PAD + i * P:PAD + SEQ], start=True, stop=True)
                        waiting.append((g * TT + i, v_ring.ship(mm)))
                        if len(waiting) > 1:
                            weigh_values()
                weigh_values()

            project_block1()
            head_columns()
            ssd_values()
            decayed_attention()

            def gla():
                pe.wait_ge(sem("const2_landed"), 16)
                ready = sem("gla_ready")
                bank = v_ring.bank(pe)
                v_ring.ship(pe.matmul(bank, gate_up[96:112, :], u_feat[96:112, F_ROWS, PAD:], start=True, stop=True))
                q, k = u_feat[:, F_GLA, PAD:], u_feat[:, F_GLA + 1, PAD:]
                pe.wait_ge(ready, 2)
                bank = v_ring.bank(pe)
                for t in range(TT):
                    mm = transpose(bank[:, t * P:(t + 1) * P], gla_tmp[:, t * P:(t + 1) * P])
                kdec_job = v_ring.ship(mm)
                scored = []

                def scores(t):
                    bank = v_ring.bank(pe)
                    pe.wait_ge(sem("gla_masked"), t + 1)
                    scored.append(v_ring.ship(pe.matmul(bank, k[:, t * P:(t + 1) * P], gla_qm[:, t % 2 * 2:t % 2 * 2 + 2],
                                                        start=True, stop=True)))

                pe.wait_ge(v_ring.drained, kdec_job)
                for c in range(7):
                    half = slice(c % 2 * CH, c % 2 * CH + CH)
                    bank = v_ring.bank(pe)
                    job = v_ring.ship(pe.matmul(bank[:, 0:W], gla_kdec[half, c // 2, :],
                                                u_tok[half, c // 2, T_GV:T_GV + W], start=True, stop=True))
                scores(0)
                pe.wait_ge(ready, 3)
                for t in range(TT):
                    if t + 1 < TT:
                        scores(t + 1)
                    pe.wait_ge(v_ring.drained, scored[t])
                    bank = v_ring.bank(pe)
                    for h in range(H):
                        pe.matmul(bank[:, h * HD:(h + 1) * HD], gla_st[:, t % 2, h, :], u_tok[:, t, T_GV + h * HD:T_GV + (h + 1) * HD],
                                  start=(h == 0), stop=False, skip_group_check=True)
                    for c in range(2):
                        at = t * P + c * CH
                        mm = pe.matmul(bank[c * CH:(c + 1) * CH, 0:W], q[:, at:at + CH], gla_state[:, 2 * t + c, :],
                                       start=False, stop=True, skip_group_check=True)
                    v_ring.ship(mm)

            def rwkv_features():
                lora = u_feat[:, F_RWKV + 6, PAD:]
                pe.wait_ge(sem("lora_ready"), 2)
                for part in (slice(0, 32), slice(32, 64)):
                    for f in range(2):
                        bank = a_ring.bank(pe)
                        a_ring.ship(pe.matmul(bank, lora_up[part, f * P:(f + 1) * P], lora[part, :], start=True, stop=True))
                for t in range(TT):
                    bank = a_ring.bank(pe)
                    a_ring.ship(pe.matmul(bank[:, 0:W], lora[64:128, t * P:(t + 1) * P], lora_up[64:128, :], start=True, stop=True))
                pe.wait_ge(sem("shifted"), 2)
                for t in range(TT):
                    bank = v_ring.bank(pe)
                    for f in range(2):
                        mm = transpose(bank[:, f * P:(f + 1) * P], u_feat[:, F_RWKV + 4 + f, PAD + t * P:PAD + (t + 1) * P])
                    v_ring.ship(mm)
                ready = sem("rwkv_ready")
                pe.wait_ge(ready, 1)
                for t in range(TT // 2):
                    bank = a_ring.bank(pe)
                    a_ring.ship(pe.matmul(bank, CONST2(c2, "headones"), r_tmp[:, 2 * t:2 * t + 2, :, :], start=True, stop=True))
                pe.wait_ge(ready, 2)
                bank = v_ring.bank(pe)
                for t in range(TT):
                    for f in range(2):
                        mm = pe.matmul(bank[:, t * H + 2 * f:t * H + 2 * f + 2], r_tmp[:, t, f, :], CONST2(c2, "headsum"), start=True, stop=True)
                v_ring.ship(mm)
                pe.wait_ge(ready, 3)

            def rwkv_tile(t):
                half = [slice(h % 2 * HD, h % 2 * HD + HD) for h in range(H)]
                pe.wait_ge(sem("rwkv_masked"), t + 1)
                for f in range(2):
                    for kind in range(2):
                        bank = v_ring.bank(pe)
                        inner = v_ring.ship(pe.matmul(bank, r_bk[:, kind, t, f, :], r_atm[:, f], start=True, stop=True))
                bank = v_ring.bank(pe)
                for h in range(H):
                    mm = pe.matmul(bank[:, h * P:(h + 1) * P], r_atm[:, h // 2, h % 2, 0, :], r_bk[:, 0, t, h // 2, :],
                                   start=True, stop=True)
                v_ring.ship(mm)
                bank = v_ring.bank(pe)
                for f in range(2):
                    mm = transpose(bank[:, f * P:(f + 1) * P], r_at[:, t, f, 0, :])
                v_ring.ship(mm)
                bank = v_ring.bank(pe)
                for kind in range(2):
                    for f in range(2):
                        n = 2 * kind + f
                        mm = transpose(bank[:, n * P:(n + 1) * P], r_dec[:, kind, t, f, :])
                v_ring.ship(mm)
                pe.wait_ge(v_ring.drained, inner)
                bank = v_ring.bank(pe)
                for h in range(H):
                    mm = pe.matmul(bank[:, h * HD:(h + 1) * HD], r_mt[:, h // 2, 1, h % 2, 0, :], v_tok[:, t, h * HD:(h + 1) * HD], start=True, stop=True)
                nv = v_ring.ship(mm)
                levels = sem("level_ready")
                for n in range(1, 6):
                    pe.wait_ge(levels, 5 * t + n)
                    if n > 1:
                        pe.wait_ge(v_ring.drained, x_job)
                    bank = v_ring.bank(pe)
                    for h in range(H):
                        mm = pe.matmul(bank[:, h * P:(h + 1) * P], r_mot[:, h, :], r_x[:, h, :], start=True, stop=True)
                    job = v_ring.ship(mm)
                    pe.wait_ge(v_ring.drained, job)
                    if n < 5:
                        bank = v_ring.bank(pe)
                        for h in range(H):
                            mm = pe.matmul(bank[:, h * P:(h + 1) * P], r_xt[:, h, :], r_prod[:, h, :], start=True, stop=True)
                        x_job = v_ring.ship(mm)
                    bank = v_ring.bank(pe)
                    for h in range(H):
                        mm = pe.matmul(bank[:, h * P:(h + 1) * P], r_prod[:, h, :], r_xt[:, h, :], start=True, stop=True)
                    job = v_ring.ship(mm)
                pe.wait_ge(v_ring.drained, job)
                bank = v_ring.bank(pe)
                for h in range(H):
                    mm = pe.matmul(bank[:, h * P:(h + 1) * P], r_xt[:, h, :], r_anv[:, h, :], start=True, stop=True)
                job = v_ring.ship(mm)
                pe.wait_ge(v_ring.drained, job)
                bank = v_ring.bank(pe)
                for h in range(H):
                    mm = pe.matmul(bank[half[h], h // 2 * P:(h // 2 + 1) * P], r_xau[:, h, 0:HD], r_mt[:, h // 2, 0, h % 2, 1, :], start=True, stop=True,
                                   skip_group_check=True)
                v_ring.ship(mm)
                for c in range(2):
                    bank = v_ring.bank(pe)
                    chunk = slice(c * CH, (c + 1) * CH)
                    for h in range(H):
                        at = h // 2 * HD
                        mm = pe.matmul(bank[half[h], at:at + HD], r_xau[chunk, h, 0:HD], r_dtok[chunk, h // 2, h % 2 * HD:(h % 2 + 1) * HD],
                                       start=True, stop=True, skip_group_check=True)
                    gt_job = v_ring.ship(mm)
                out = psum[:, 6 + t % 2, :]
                if t >= 2:
                    pe.wait_ge(sem("rwkv_out_drained"), t - 1)
                for h in range(H):
                    o = out[:, h * HD:(h + 1) * HD]
                    pe.matmul(o, r_mt[:, h // 2, 0, h % 2, 1, :], r_xau[:, h, HD:P], start=(h == 0), stop=False, skip_group_check=True)
                    pe.matmul(o, r_mt[:, h // 2, 1, h % 2, 1, :], v_tok[:, t, h * HD:(h + 1) * HD], start=False, stop=False, skip_group_check=True)
                for c in range(2):
                    chunk = slice(c * CH, (c + 1) * CH)
                    bank = v_ring.bank(pe)
                    pe.wait_ge(v_ring.drained, gt_job)
                    pe.wait_ge(sem("state_ready"), 2 * t + c + 1)
                    state = r_state[:, (2 * t + c) % 3]
                    for f in range(2):
                        pe.matmul(bank[:, f * P:(f + 1) * P], r_gt[:, c, f, :], state[:, f, :], start=(f == 0), stop=False,
                                  skip_group_check=True)
                    for h in range(H):
                        at = h * HD
                        cols_of = slice(h % 2 * HD, (h % 2 + 1) * HD)
                        pe.matmul(bank[half[h], at:at + HD], r_dtok[chunk, h // 2, cols_of], r_xau[chunk, h, HD:P],
                                  start=False, stop=False, skip_group_check=True)
                        mm = pe.matmul(bank[half[h], at:at + HD], r_dtok[chunk, 2 + h // 2, cols_of], v_tok[chunk, t, h * HD:(h + 1) * HD],
                                       start=False, stop=True, skip_group_check=True)
                    v_ring.ship(mm)
                    for f in range(2):
                        mm = pe.matmul(out[chunk, f * P:(f + 1) * P], r_rot[:, f, chunk], state[:, f, :],
                                       start=False, stop=True, skip_group_check=True)
                mm.then_inc(sem("rwkv_out_filled"), 1)

            gla()
            rwkv_features()
            for t in range(TT):
                rwkv_tile(t)

            def transposed_rows(source, ready):
                for t in range(TT):
                    if ready is not None:
                        pe.wait_ge(ready, t + 1)
                    for half in range(2):
                        bank = a_ring.bank(pe)
                        for k in range(4):
                            mm = transpose(bank[:, k * P:(k + 1) * P], source[:, t, (4 * half + k) * P:(4 * half + k + 1) * P])
                        job = a_ring.ship(mm)
                return job

            def mix_out():
                pe.wait_ge(sem("mixed"), 1)
                pe.wait_ge(a_ring.drained, transposed_rows(y, None))
                for half in range(2):
                    w = piece(7 + half)
                    for t in range(TT):
                        bank = v_ring.bank(pe)
                        for k in range(KT):
                            mm = pe.matmul(bank, y_t[:, k, t * P:(t + 1) * P], w[:, k, :], start=(k == 0), stop=(k == KT - 1))
                        slot_free[7 + half] = (v_ring.filled, v_ring.ship(mm))

            def route():
                before, iota, expert = (CONST3(c3, n) for n in ("before", "iota", "expert"))
                routed = sem("routed")
                pe.wait_ge(sem("router_landed"), 16 * 4)
                pe.wait_ge(a_ring.drained, transposed_rows(x1, sem("x1_ready")))
                bank = v_ring.bank(pe)
                for t in range(TT):
                    for k in range(KT):
                        mm = pe.matmul(bank[:, t * E:(t + 1) * E], x1_t[:, k, t * P:(t + 1) * P], router_w[:, k, :],
                                       start=(k == 0), stop=(k == KT - 1), skip_group_check=True)
                v_ring.ship(mm)
                pe.wait_ge(routed, 1)
                bank = v_ring.bank(pe)
                for t in range(TT):
                    mm = transpose(bank[0:E, t * P:(t + 1) * P], gates[:, t, :])
                v_ring.ship(mm)
                bank = v_ring.bank(pe)
                for t in range(TT):
                    for u in range(t + 1):
                        mm = pe.matmul(bank[:, t * E:(t + 1) * E], before if u == t else ones, assigned[:, u, :],
                                       start=(u == 0), stop=(u == t), skip_group_check=True)
                v_ring.ship(mm)
                bank = v_ring.bank(pe)
                for t in range(TT):
                    mm = pe.matmul(bank[0:E, 0:1], assigned[:, t, :], ones[:, 0:1], start=(t == 0), stop=(t == TT - 1))
                v_ring.ship(mm)
                pe.wait_ge(routed, 2)
                bank = v_ring.bank(pe)
                for t in range(TT):
                    mm = transpose(bank[0:E, t * P:(t + 1) * P], pos[:, t, :])
                v_ring.ship(mm)
                bank = v_ring.bank(pe)
                pe.matmul(bank[0:E, 0:KINDS], before[0:E, 0:E], rank[0:E, 0:KINDS], start=True, stop=False, skip_group_check=True)
                mm = pe.matmul(bank[0:E, 0:KINDS], ones[0:E, 0:E], rank[0:E, KINDS:2 * KINDS], start=False, stop=True,
                               skip_group_check=True)
                v_ring.ship(mm)
                bank = v_ring.bank(pe)
                v_ring.ship(pe.matmul(bank[:, 0:2], ones[0:E, :], rank[0:E, 10:12], start=True, stop=True))
                pe.wait_ge(routed, 3)
                bank = v_ring.bank(pe)
                pe.matmul(bank[:, 0:NB], expert[0:E, :], hot[0:E, :], start=True, stop=True, skip_group_check=True)
                mm = pe.matmul(bank[:, P:P + NB], ones[0:E, :], base_w[0:E, :], start=True, stop=True, skip_group_check=True)
                v_ring.ship(mm)
                for rows_t in (pos_t, gates_t):
                    bank = v_ring.bank(pe)
                    for t in range(TT):
                        mm = pe.matmul(bank[:, t * NB:(t + 1) * NB], rows_t[0:E, t * P:(t + 1) * P], hot[0:E, :], start=True, stop=True,
                                       skip_group_check=True)
                    v_ring.ship(mm)
                for t in range(TT):
                    for half in range(2):
                        bank = v_ring.bank(pe)
                        v_ring.ship(pe.matmul(bank, gates_t[0:E, t * P:(t + 1) * P], b_down[0:E, half * 512:(half + 1) * 512],
                                              start=True, stop=True))

            def gather(half, bank):
                for k in range(4 * half, 4 * half + 4):
                    for t in range(TT):
                        mm = pe.matmul(bank[:, k % 4 * P:(k % 4 + 1) * P], x1[:, t, k * P:(k + 1) * P], to_block[:, t, :],
                                       start=(t == 0), stop=(t == TT - 1), skip_group_check=True)
                return mm

            def experts():
                pe.wait_ge(sem("first_block_ready"), 1)
                for half in range(2):
                    bank = a_ring.bank(pe)
                    job = a_ring.ship(gather(half, bank))
                pe.wait_ge(a_ring.drained, job)
                pe.wait_ge(v_ring.drained, v_ring.sent)
                blocks, half_blocks = block_counts(pe)
                pe.sem_inc(ev_ring.filled, 12)
                pe.sem_inc(ea_ring.filled, 9)
                with pe.Fori(0, blocks) as i:
                    T = Turn(pe, i, None, PER, CREDIT)
                    ev_ring.sent = ea_ring.sent = 0

                    def gate_up(c):
                        T.wait(expert_landed[c], 16)
                        bank = ev_ring.bank(T)
                        w = slot[(3 + c) % SLOTS]
                        for k in range(KT):
                            mm = pe.matmul(bank, xg[:, k, :], w[:, k, :], start=(k == 0), stop=(k == KT - 1))
                        ev_ring.ship(T, mm)

                    def turn_hidden(c):
                        T.wait(hidden_ready, c + 1)
                        bank = ea_ring.bank(T)
                        for k in range(2):
                            mm = transpose(bank[:, k * P:(k + 1) * P], hid[:, (2 * c + k) * P:(2 * c + k + 1) * P])
                        return ea_ring.ship(T, mm)

                    def down(half):
                        T.wait(expert_landed[4 + half], 16)
                        bank = ea_ring.bank(T)
                        w = slot[(7 + half) % SLOTS]
                        for k in range(KT):
                            mm = pe.matmul(bank, hid_t[:, k, :], w[:, k, :], start=(k == 0), stop=(k == KT - 1))
                        return ea_ring.ship(T, mm)

                    T.wait(ea_ring.drained, 0)
                    gate_up(0)
                    gate_up(1)
                    turn_hidden(0)
                    gate_up(2)
                    turn_hidden(1)
                    gate_up(3)
                    turn_hidden(2)
                    T.wait(to_ready, 1)
                    bank = ea_ring.bank(T)
                    ea_ring.ship(T, gather(0, bank))
                    hidden_turned = turn_hidden(3)
                    T.wait(from_ready, 1)
                    bank = ea_ring.bank(T)
                    for t in range(TT):
                        mm = transpose(bank[:, t * P:(t + 1) * P], from_block[:, t, :])
                    ea_ring.ship(T, mm)
                    T.wait(ea_ring.drained, hidden_turned)
                    down(0)
                    rows_done = down(1)
                    bank = ea_ring.bank(T)
                    ea_ring.ship(T, gather(1, bank))
                    T.wait(ea_ring.drained, rows_done)
                    for t in range(TT):
                        for half in range(2):
                            bank = ev_ring.bank(T)
                            ev_ring.ship(T, pe.matmul(bank, from_t[:, t * P:(t + 1) * P], y_blk[:, half * 512:(half + 1) * 512],
                                                      start=True, stop=True))
                pe.wait_ge(ev_ring.drained, blocks * 12 + (12 + 3))
                pe.wait_ge(ea_ring.drained, blocks * 9 + 3)
                pe.wait_ge(sem("first_block_ready"), 2)
                for half in range(2):
                    bank = a_ring.bank(pe)
                    job = a_ring.ship(gather(half, bank))
                pe.wait_ge(a_ring.drained, job)
                pe.sem_inc(hv_ring.filled, 12)
                pe.sem_inc(ha_ring.filled, 6)
                with pe.Fori(0, half_blocks) as i:
                    T = Turn(pe, i, None, HALF_PER, HALF_CREDIT)
                    hv_ring.sent = ha_ring.sent = 0
                    halves = [slice(g * HALF_ROWS, (g + 1) * HALF_ROWS) for g in range(2)]

                    def half_gate_up(pair):
                        for g in range(2):
                            T.wait(half_landed[2 * pair + g], 16)
                        for c in range(2):
                            bank = hv_ring.bank(T)
                            for k in range(KT):
                                for g, part in enumerate(halves):
                                    w = slot[(3 + 2 * pair + g) % SLOTS]
                                    mm = pe.matmul(bank[part, 0:256], xg[:, k, part], w[:, k, c * 256:(c + 1) * 256],
                                                   start=(k == 0), stop=(k == KT - 1), skip_group_check=True)
                            hv_ring.ship(T, mm)

                    def half_turn_hidden(pair):
                        T.wait(half_hidden, pair + 1)
                        bank = ha_ring.bank(T)
                        for k in range(2):
                            mm = transpose(bank[:, k * P:(k + 1) * P], hid[:, pair * 256 + k * P:pair * 256 + (k + 1) * P])
                        return ha_ring.ship(T, mm)

                    T.wait(ha_ring.drained, 0)
                    half_gate_up(0)
                    half_gate_up(1)
                    half_turn_hidden(0)
                    T.wait(half_to_ready, 1)
                    bank = ha_ring.bank(T)
                    ha_ring.ship(T, gather(0, bank))
                    hidden_turned = half_turn_hidden(1)
                    T.wait(half_from_ready, 1)
                    bank = ha_ring.bank(T)
                    for t in range(TT):
                        mm = transpose(bank[:, t * P:(t + 1) * P], from_block[:, t, :])
                    ha_ring.ship(T, mm)
                    T.wait(ha_ring.drained, hidden_turned)
                    bank = ha_ring.bank(T)
                    for g in range(2):
                        T.wait(half_landed[4 + g], 16)
                    for k in range(KT):
                        for g, part in enumerate(halves):
                            mm = pe.matmul(bank[part, :], hid_t[:, k, 0:HALF_ROWS], slot[(7 + g) % SLOTS][:, k, :],
                                           start=(k == 0), stop=(k == KT - 1), skip_group_check=True)
                    rows_done = ha_ring.ship(T, mm)
                    assert rows_done == HALF_DOWN
                    bank = ha_ring.bank(T)
                    ha_ring.ship(T, gather(1, bank))
                    T.wait(ha_ring.drained, rows_done)
                    for t in range(TT):
                        for part in halves:
                            bank = hv_ring.bank(T)
                            hv_ring.ship(T, pe.matmul(bank, from_t[part, t * P:(t + 1) * P], y_blk[part, 0:512], start=True, stop=True))
                pe.wait_ge(hv_ring.drained, half_blocks * 12 + (12 + 3))
                pe.wait_ge(ha_ring.drained, half_blocks * 6 + 3)

            def piece2(n):
                pe.wait_ge(landed2[(3 + n) % SLOTS], 16 * (n // SLOTS + 1))
                return slot[(3 + n) % SLOTS]

            def gated_embedding():
                pe.wait_ge(sem("ffn_ready"), 1)
                pe.wait_ge(a_ring.drained, transposed_rows(ffn, None))
                for half in range(2):
                    w = piece2(half)
                    w_proj = piece2(2)
                    for t in range(TT):
                        bank = a_ring.bank(pe)
                        for k in range(KT):
                            mm = pe.matmul(bank, h_t[:, k, t * P:(t + 1) * P], w[:, k, :], start=(k == 0), stop=(k == KT - 1))
                        slot_free2[half] = (a_ring.filled, a_ring.ship(mm))
                        bank = v_ring.bank(pe)
                        if t == 0 and half == 0:
                            pe.wait_ge(sem("p_landed"), 16)
                        for k in range(2):
                            mm = pe.matmul(bank, p_t[:, k, t * P:(t + 1) * P],
                                           w_proj.rearrange("p k n -> p (k n)")[:, k * D + half * 512:k * D + (half + 1) * 512],
                                           start=(k == 0), stop=(k == 1))
                        slot_free2[2] = (v_ring.filled, v_ring.ship(mm))

            mix_out()
            route()
            experts()
            gated_embedding()

            def layer(T):
                lv_ring.sent = la_ring.sent = 0

                def weights(n):
                    T.wait(layer_landed[n % SLOTS], 16 * (n // SLOTS + 1))
                    return slot[(n + LATE) % SLOTS]

                def turned(source, parts, ready, meta_banks=2):
                    for t in range(NT2):
                        n = SIZE[t]
                        banks = 2 if t else meta_banks
                        if ready is not None:
                            T.wait(ready, t + 1)
                        for b in range(banks):
                            bank = la_ring.bank(T)
                            if t == 0:
                                T.hold()
                            for k in range(KT // banks):
                                at = parts[KT // banks * b + k]
                                mm = transpose(bank[:, k * n:(k + 1) * n], source[0:n, t, at:at + P], n)
                            job = la_ring.ship(T, mm)
                    T.wait(la_ring.drained, job)

                def project():
                    turned(h2, range(0, D, P), sem("layer_start"), 1)
                    for n in range(4):
                        w = weights(n)
                        for t in range(1, NT2):
                            bank = la_ring.bank(T)
                            for k in range(KT):
                                mm = pe.matmul(bank[:, 0:WIDTHS[n]], h2_t[:, k, OFF[t]:OFF[t] + P], w[:, k, 0:WIDTHS[n]],
                                               start=(k == 0), stop=(k == KT - 1))
                            la_ring.ship(T, mm)
                    bank = la_ring.bank(T)
                    for k in range(KT):
                        for n in range(4):
                            mm = pe.matmul(bank[32 * n:32 * n + META, 0:WIDTHS[n]], h2_t[:, k, 0:META], slot[(n + LATE) % SLOTS][:, k, 0:WIDTHS[n]],
                                           start=(k == 0), stop=(k == KT - 1), skip_group_check=True)
                    job = la_ring.ship(T, mm)
                    for n in range(4):
                        layer_free[n] = (la_ring.filled, job)
                    for u in range(6):
                        n, at = (3, 256 + u * P) if u < 2 else (4, (u - 2) * P)
                        w = weights(n)
                        for c in range(2):
                            bank = lv_ring.bank(T)
                            for k in range(KT):
                                mm = pe.matmul(bank[:, 0:HALF], w[:, k, at:at + P], h2_t[:, k, c * HALF:(c + 1) * HALF],
                                               start=(k == 0), stop=(k == KT - 1))
                            layer_free[n] = (lv_ring.filled, lv_ring.ship(T, mm))
                    T.wait(sem("layer_params_landed"), 16 * 5)
                    for c in range(2):
                        bank = lv_ring.bank(T)
                        for k in range(KT):
                            mm = pe.matmul(bank[0:FH, 0:HALF], f_w[:, k, :], h2_t[:, k, c * HALF:(c + 1) * HALF],
                                           start=(k == 0), stop=(k == KT - 1))
                        lv_ring.ship(T, mm)
                    layer_mark["projected"] = lv_ring.sent

                def turn_rotated():
                    for n_th, t in enumerate(ROTATED):
                        T.wait(sem("rotated_ready"), n_th + 1)
                        bank = lv_ring.bank(T)
                        n = SIZE[t]
                        if t == 0:
                            T.hold()
                        for u in range(4):
                            mm = transpose(bank[:, u * n:(u + 1) * n], work[0:n, n_th % 2, u * P:(u + 1) * P], n)
                        job = lv_ring.ship(T, mm)
                    T.wait(lv_ring.drained, job)

                def retention():
                    waiting = []

                    def weigh_values():
                        h, i, a, b, seg, job = waiting.pop(0)
                        sums = psum[:, 6 + h % 2, :]
                        T.wait(lv_ring.drained, job)
                        if seg == 0:
                            T.wait(sem("retained_drained"), h - 1)
                        if i == 0:
                            T.hold()
                        for j in range(NT2):
                            if not a <= OFF[j] < b:
                                continue
                            n = SIZE[j]
                            mm = pe.matmul(sums[0:n, j * RV:(j + 1) * RV], work[0:SIZE[i], seg % 2, OFF[j] - a:OFF[j] - a + n],
                                           u2[0:SIZE[i], i, U_V + h * RV:U_V + (h + 1) * RV], start=(i == 0 and j <= 1),
                                           stop=(i == j), skip_group_check=True)
                        T.did(mm, sem("retention_done"))

                    for h in range(RH):
                        half = slice(h % 2 * HD, h % 2 * HD + HD)
                        for seg, (i, a, b) in enumerate(SEGMENTS):
                            bank = lv_ring.bank(T)
                            if i == 0:
                                T.hold()
                            mm = pe.matmul(bank[0:SIZE[i], 0:b - a], rotated[half, 2 + h // 2, OFF[i]:OFF[i] + SIZE[i]],
                                           rotated[half, h // 2, a:b], start=True, stop=True)
                            waiting.append((h, i, a, b, seg, lv_ring.ship(T, mm)))
                            if len(waiting) > 1:
                                weigh_values()
                    weigh_values()

                def pool():
                    for t in reversed(range(NT2)):
                        n = SIZE[t]
                        bank = lv_ring.bank(T)
                        for g in range(4):
                            out = bank[g % 2 * HD:(g % 2 + 1) * HD, g // 2 * n:(g // 2 + 1) * n]
                            u = slice(U_U + g * HD, U_U + (g + 1) * HD)
                            here = CONST4(c4, "pool", g * P, (g + 1) * P) if t else CONST4(c4, "pool_first", g * META, (g + 1) * META)
                            mm = pe.matmul(out, u2[0:n, t, u], here[0:n, :], start=True, stop=(t == 0), skip_group_check=True)
                            if t:
                                m = SIZE[t - 1]
                                before = CONST4(c4, "pool_before" if t > 1 else "pool_meta", g * P, (g + 1) * P)
                                mm = pe.matmul(out, u2[0:m, t - 1, u], before[0:m, :], start=False, stop=True, skip_group_check=True)
                        T.wait(lv_ring.drained, lv_ring.ship(T, mm))
                        for g in range(2):
                            bank = lv_ring.bank(T)
                            lv_ring.ship(T, pe.matmul(bank[0:n, 0:P], work[:, t % 2, g * n:(g + 1) * n], pool_w[:, g, :],
                                                      start=True, stop=True))

                def forget():
                    bank = lv_ring.bank(T)
                    T.hold()
                    for t in range(NT2):
                        mm = transpose(bank[0:SIZE[t], t * FH:(t + 1) * FH], f_row[0:FH, 1, OFF[t]:OFF[t] + SIZE[t]], FH)
                    lv_ring.ship(T, mm)
                    scored, turned_tiles = [], []
                    turned_jobs = [0]

                    def turn_weights():
                        h, i, n = scored.pop(0)
                        turned_tiles.append((h, i, n))
                        m = SIZE[i]
                        T.wait(sem("fox_weights_ready"), n + 1)
                        for first, last in ([(0, i + 1)] if i < 4 else [(0, 4), (4, 5)]):
                            bank = psum[:, 4 + turned_jobs[0] % 2, :]
                            T.wait(sem("fox_turned_drained"), turned_jobs[0] - 1)
                            if i == 0:
                                T.hold()
                            for j in range(first, last):
                                mm = transpose(bank[0:SIZE[j], (j - first) * m:(j - first + 1) * m],
                                               fox_p[0:m, n % 3, OFF[j]:OFF[j] + SIZE[j]], m)
                            T.did(mm, sem("fox_turned"))
                            turned_jobs[0] += 1

                    def attend():
                        h, i, n = turned_tiles.pop(0)
                        m = SIZE[i]
                        T.wait(sem("fox_turned_drained"), FOX_TURNED[n])
                        out = psum[0:m, 6 + n % 2, 0:HD]
                        T.wait(sem("fox_out_drained"), n - 1)
                        if i == 0:
                            T.hold()
                        for j in range(i + 1):
                            k = SIZE[j]
                            mm = pe.matmul(out, fox_pt[0:k, n % 2, j, 0:m], u2[0:k, j, U_VF + h * HD:U_VF + (h + 1) * HD],
                                           start=(j == 0), stop=(j == i))
                        T.did(mm, sem("fox_out"))

                    n = 0
                    for h in range(FH):
                        half = slice(h % 2 * HD, h % 2 * HD + HD)
                        for c in range(2):
                            bank = lv_ring.bank(T)
                            job = lv_ring.ship(T, pe.matmul(bank[:, 0:HALF], ident[0:FH, h:h + 1].broadcast_to([FH, P]),
                                                            f_row[0:FH, 1, c * HALF:(c + 1) * HALF], start=True, stop=True))
                        for i in range(NT2):
                            w = OFF[i] + SIZE[i]
                            pair = psum[0:SIZE[i], n % 2 * 2:n % 2 * 2 + 2, :].rearrange("p b s -> p (b s)")
                            if i == 0:
                                T.wait(lv_ring.drained, lv_ring.sent)
                            if n > 1 and i:
                                T.wait(sem("fox_scores_drained"), n - 1)
                            if i == 0:
                                T.hold()
                            for a, b in ([(0, w)] if w <= 512 else [(0, 512), (512, w)]):
                                mm = pe.matmul(pair[:, a:b], qk_f[half, h // 2, OFF[i]:OFF[i] + SIZE[i]], qk_f[half, 3 + h // 2, a:b],
                                               start=True, stop=True, skip_group_check=True)
                            T.did(mm, sem("fox_scores"))
                            scored.append((h, i, n))
                            n += 1
                            if len(scored) > 2:
                                turn_weights()
                            if len(turned_tiles) > 1:
                                attend()
                        T.wait(sem("fox_scores_drained"), n)
                    for _ in range(2):
                        turn_weights()
                        attend()
                    attend()

                def rows_product(bank, t, tiles, lhs, rhs):
                    for k in range(tiles):
                        if t:
                            mm = pe.matmul(bank[0:SIZE[t], :], lhs(k), rhs(k), start=(k == 0), stop=(k == tiles - 1))
                        else:
                            at = k % 4 * 32
                            mm = pe.matmul(bank[at:at + META, :], lhs(k), rhs(k), start=(k < 4), stop=(k >= tiles - 4),
                                           skip_group_check=True)
                    return mm

                def mix():
                    T.wait(sem("mix2_ready"), 1)
                    turned(u2, [U_V, U_V + P, U_V + 2 * P, U_U, U_U + P, U_QK, U_QK + P, U_QK + 2 * P], None)
                    for half in range(2):
                        w = weights(W_OUT + half)
                        for t in range(NT2):
                            bank = lv_ring.bank(T)
                            mm = rows_product(bank, t, KT, lambda k: h2_t[:, k, OFF[t]:OFF[t] + SIZE[t]], lambda k: w[:, k, :])
                            layer_free[W_OUT + half] = (lv_ring.filled, lv_ring.ship(T, mm))

                def feed_forward():
                    turned(h2, range(0, D, P), sem("mid_ready"))
                    for f in range(FT):
                        n = W_FFN + f // 2
                        w = weights(n)
                        for c in range(2):
                            for ring_of, at in ((la_ring, 0), (lv_ring, 256)):
                                at += f % 2 * P
                                bank = ring_of.bank(T)
                                for k in range(KT):
                                    mm = pe.matmul(bank[:, 0:HALF], w[:, k, at:at + P], h2_t[:, k, c * HALF:(c + 1) * HALF],
                                                   start=(k == 0), stop=(k == KT - 1))
                                layer_free[n] = (ring_of.filled, ring_of.ship(T, mm))
                    T.wait(lv_ring.drained, lv_ring.sent)
                    for half in range(2):
                        for t in range(NT2):
                            if t == 0:
                                w = [weights(W_DOWN + 3 * half + n) for n in range(3)]
                            bank = lv_ring.bank(T)
                            mm = rows_product(bank, t, FT, lambda f: ff_t[:, f, OFF[t]:OFF[t] + SIZE[t]], lambda f: w[f // KT][:, f % KT, :])
                            job = lv_ring.ship(T, mm)
                        for n in range(3):
                            layer_free[W_DOWN + 3 * half + n] = (lv_ring.filled, job)

                project()
                turn_rotated()
                retention()
                pool()
                forget()
                mix()
                feed_forward()

            pe.wait_ge(a_ring.drained, a_ring.sent)
            pe.wait_ge(v_ring.drained, v_ring.sent)
            with pe.Fori(0, LAYERS) as i:
                T = Turn(pe, i, None, LAYER_PER, LAYER_CREDIT, sem("passed"))
                layer(T)
                T.check()

        @block.sync
        def _(sp):
            sp.dma_start(x_t, io["x_t"]).then_inc(x_landed, 16)

            def load_piece(n, src, words=PIECE):
                if n >= SLOTS:
                    sp.wait_ge(*slot_free[n - SLOTS])
                sp.dma_start(ring[:, n % SLOTS * PIECE:n % SLOTS * PIECE + words], src).then_inc(landed[n % SLOTS], 16)

            for n in range(2):
                load_piece(n, io["weights1"][n])
            for dst, name in SETUP:
                src = io[name]
                part = src.shape[0]
                if name == "rows":
                    sp.dma_start(dst, src.broadcast_to([P, ROWS.width])).then_inc(setup_landed, 16)
                elif name == "gate_up":
                    sp.dma_start(dst[96:112, :], src).then_inc(setup_landed, 16)
                else:
                    sp.dma_start(dst, src).then_inc(setup_landed, 16)
            for n in range(2, 7):
                load_piece(n, io["weights1"][n])
            sp.wait_ge(sums_drained, 2 * H)
            sp.dma_start(c2, io["const2"]).then_inc(sem("const2_landed"), 16)
            for n in range(7, 9):
                load_piece(n, io["weights1"][n])

            def expert_source(e, k):
                if k < 4:
                    return io["exp_gu"][bass.ds(e * 4 + k, 1), :, :].rearrange("o p n -> (o p) n")
                return io["exp_down"][bass.ds(e * 2 + (k - 4), 1), :, :].rearrange("o p n -> (o p) n")

            def expert_slot(k):
                s = (3 + k) % SLOTS
                return ring[:, s * PIECE:(s + 1) * PIECE]

            for k in range(4):
                sp.wait_ge(*slot_free[3 + k])
                sp.dma_start(expert_slot(k), expert_source(0, k)).then_inc(expert_landed[k], 16)
            sp.wait_ge(sem("mixed"), 1)
            sp.dma_start(x1, io["x"]).then_inc(sem("x_rows_landed"), 16)
            sp.dma_start(ln_par, io["ln1"].broadcast_to([P, 2 * D])).then_inc(sem("ln_landed"), 16)
            sp.dma_start(router_w, io["router_w"]).then_inc(sem("router_landed"), 16)
            sp.dma_start(router_b, io["router_b"].broadcast_to([P, E])).then_inc(sem("router_landed"), 16)
            sp.dma_start(c3, io["const3"]).then_inc(sem("router_landed"), 16)
            sp.dma_start(b_down[0:E, :], io["b_down"]).then_inc(sem("router_landed"), 16)
            for k in (4, 5):
                sp.wait_ge(*slot_free[3 + k])
                sp.dma_start(expert_slot(k), expert_source(0, k)).then_inc(expert_landed[k], 16)
            sp.wait_ge(sem("routed"), 4)
            blocks, half_blocks = block_counts(sp)

            def load_bias(e):
                sp.dma_start(b_gu, io["b_gu"][bass.ds(e, 1), :].broadcast_to([P, 2 * D])).then_inc(bias_landed, 16)

            load_bias(0)
            with sp.Fori(1, blocks) as i:
                e = sp.value_load(block_expert[0:1, bass.ds(i, 1)], min_val=0, max_val=E - 1)
                for k in range(6):
                    if k < 4:
                        sp.wait_ge(ev_ring.filled, i * 12 + (k + 1))
                    else:
                        sp.wait_ge(ea_ring.filled, i * 9 + (k + 3))
                    sp.dma_start(expert_slot(k), expert_source(e, k)).then_inc(expert_landed[k], 16)
                    if k == 3:
                        sp.wait_ge(ev_ring.drained, i * 12 + (4 + 3))
                        load_bias(e)

            def load_half_bias(e):
                for g in range(2):
                    dst = b_gu[g * HALF_ROWS:(g + 1) * HALF_ROWS, 0:D].rearrange("p (c n) -> p c n", c=2)
                    src = io["b_gu"][bass.ds(e, 1), :].rearrange("o (c g n) -> o c g n", c=2, g=2)[:, :, g, :]
                    sp.dma_start(dst, src.broadcast_to([HALF_ROWS, 2, 512])).then_inc(half_bias, 16)

            e = sp.value_load(block_expert[0:1, HALF_AT:HALF_AT + 1], min_val=0, max_val=E - 1)
            for k in range(6):
                if k < 4:
                    sp.wait_ge(ev_ring.filled, blocks * 12 + (k + 1))
                else:
                    sp.wait_ge(ea_ring.filled, blocks * 9 + (k + 3))
                sp.dma_start(expert_slot(k), expert_source(e, k)).then_inc(half_landed[k], 16)
                if k == 3:
                    sp.wait_ge(ev_ring.drained, blocks * 12 + (4 + 3))
                    load_half_bias(e)
            with sp.Fori(1, half_blocks) as i:
                e = sp.value_load(block_expert[0:1, bass.ds(i + HALF_AT, 1)], min_val=0, max_val=E - 1)
                for k in range(6):
                    if k < 4:
                        sp.wait_ge(hv_ring.filled, i * 12 + 2 * (k // 2 + 1))
                    else:
                        sp.wait_ge(ha_ring.filled, i * 6 + HALF_DOWN)
                    sp.dma_start(expert_slot(k), expert_source(e, k)).then_inc(half_landed[k], 16)
                    if k == 3:
                        sp.wait_ge(hv_ring.drained, i * 12 + (4 + 3))
                        load_half_bias(e)
            sp.wait_ge(hv_ring.filled, half_blocks * 12 + 4)

            def load_piece2(n, src, words=PIECE):
                if n >= SLOTS:
                    sp.wait_ge(*slot_free2[n - SLOTS])
                s = (3 + n) % SLOTS
                sp.dma_start(ring[:, s * PIECE:s * PIECE + words], src).then_inc(landed2[s], 16)

            load_piece2(0, io["ple_gate"][0])
            load_piece2(1, io["ple_gate"][1])
            load_piece2(2, io["ple_proj"], 2 * D)
            sp.dma_start(ln_par, io["ln2"].broadcast_to([P, 2 * D])).then_inc(sem("ln_landed"), 16)
            sp.dma_start(ln_emb, io["ln_emb"].broadcast_to([P, 2 * D])).then_inc(sem("ln_landed"), 16)
            sp.dma_start(h2[0:META, 0, :], io["meta"]).then_inc(sem("meta_landed"), 16)
            sp.wait_ge(sem("ffn_ready"), 1)
            sp.dma_start(p_t, io["p_t"]).then_inc(sem("p_landed"), 16)
            with sp.Fori(0, LAYERS) as i:
                T = Turn(sp, i, None, LAYER_PER, LAYER_CREDIT)
                params = sem("layer_params_landed")
                def load_piece3(n):
                    if n >= SLOTS:
                        T.wait(*layer_free[n - SLOTS])
                    s = (n + LATE) % SLOTS
                    sp.dma_start(ring[:, s * PIECE:(s + 1) * PIECE],
                                 io["weights2"][bass.ds(i * LAYER_PIECES + n, 1)].rearrange("o p n -> (o p) n")
                                 ).then_inc(layer_landed[n % SLOTS], 16)

                T.wait(sem("early_slots_free"), 0)
                for n in range(3):
                    load_piece3(n)
                T.wait(sem("layer_start"), NT2)
                for dst, name, part in ((f_w, "f_w", P), (f_b, "f_b", FH), (pool_w, "pool_w", P)):
                    src = io[name][bass.ds(i, 1)].rearrange("o p n -> (o p) n")
                    dst = dst[0:part] if len(dst.shape) == 2 else dst.rearrange("p a b -> p (a b)")
                    sp.dma_start(dst, src).then_inc(params, 16)
                sp.dma_start(rows2, io["rows2"][bass.ds(i, 1), :].broadcast_to([P, ROWS2.width])).then_inc(params, 16)

                sp.dma_start(c4, io["const4"]).then_inc(params, 16)
                for n in range(3, 5):
                    load_piece3(n)
                for n in (5, 6, 7, 8, 9):
                    load_piece3(n)
                T.wait(lv_ring.filled, layer_mark["projected"])
                sp.dma_start(retained.rearrange("p h s -> p (h s)"), io["retention_decay"]).then_inc(sem("retention_decay_landed"), 16)
                load_piece3(10)
                T.wait(sem("mix2_ready"), 1)
                sp.dma_start(ln_par2, io["ln_mid"][bass.ds(i, 1), :].broadcast_to([P, 2 * D])).then_inc(sem("layer_ln_landed"), 16)
                for n in range(11, W_DOWN):
                    load_piece3(n)
                T.wait(sem("mid_ready"), NT2)
                sp.dma_start(ln_par2, io["ln_end"][bass.ds(i, 1), :].broadcast_to([P, 2 * D])).then_inc(sem("layer_ln_landed"), 16)
                for n in range(W_DOWN, LAYER_PIECES):
                    load_piece3(n)
            sp.wait_ge(sem("layer_start"), NT2 * (1 + LAYERS))
            sp.dma_start(io["out"].rearrange("(t p) d -> p t d", p=P), h2[:, 1:, :]).then_inc(out_landed, 16)
            sp.wait_ge(out_landed, 16)

        @block.scalar
        def _(act):
            A = Steps(act, act_step)

            def project_block1():
                for a, width in ((T_GOG, 256), (T_Z, 512), (T_MOG, 512)):
                    for t in range(TT):
                        bank = a_ring.take(act)
                        A.did(act.copy(u_tok[:, t, a:a + width], bank[:, 0:width]), a_ring.drained)
                        if a_ring.taken <= 8:
                            conv_silu(a_ring.taken - 1)

            def softplus_rows():
                act.wait_ge(rows_biased, 4)
                act.wait_ge(a_ring.filled, mark["projected"])
                two = hrow[0:4, 2:4, :]
                A.did(act.activation(two, hrow[0:4, 0:2, :], ACT.Abs))
                A.settle()
                A.did(act.activation(two, two, ACT.Exp, scale=-1.0))
                A.did(act.activation(expa[0:4, :], COLS(cols, "a_log")[0:4, :], ACT.Exp))
                act.wait_ge(act_step, 2)
                A.did(act.activation(two, two, ACT.Ln, bias=ones[0:4, 0:1]), rows_softplus)

            def conv_silu(i):
                act.wait_ge(conv_summed, i + 1)
                b = COLS(cols, "ssd_cb", i, i + 1) if i < 4 else COLS(cols, "m_cb", i - 4, i - 3)
                A.did(act.activation(u_feat[:, F_SSD + i, PAD:], conv_acc[:, i % 2, :], ACT.Silu, bias=b), conv_ready)

            def gates():
                A.settle()
                A.did(act.activation(u_tok[:, :, T_Z:T_Z + W], u_tok[:, :, T_Z:T_Z + W], ACT.Silu), z_ready)
                A.did(act.activation(u_tok[:, :, T_MOG:T_MOG + W], u_tok[:, :, T_MOG:T_MOG + W], ACT.Sigmoid), z_ready)
                A.did(act.activation(u_tok[:, :, T_GOG:T_GOG + W], u_tok[:, :, T_GOG:T_GOG + W], ACT.Silu), z_ready)

            def decays():
                act.wait_ge(hcol_ready, 1)
                A.did(act.activation(hcol[:, 3], hcol[:, 3], ACT.Exp), sem("floor_ready"))
                for n in range(2 * H * TT):
                    i = n % TT
                    act.wait_ge(decay_arg, n + 1)
                    part = decay[:, n % 2, 0:SEQ - i * P]
                    A.did(act.activation(part, part, ACT.Exp, scale=1.0 if n < H * TT else -1.0), decay_ready)

            def root(S, variance, eps=True):
                S.roots += 1
                S.wait(variance_ready, S.roots)
                bias = CONST1(c1, "eps", 0, 1)[0:variance.shape[0]] if eps else 0.0
                S.did(act.activation(variance, variance, ACT.Sqrt, bias=bias), root_ready)

            def group_root(groups):
                root(A, stat[:, 0:TT * groups], False)

            def rows_root(S, t, parts=P):
                root(S, ln_mean[0:parts, t, 1:2])

            A.roots = 0
            act.wait_ge(setup_landed, 16 * len(SETUP))
            project_block1()
            softplus_rows()
            gates()
            decays()
            group_root(1)
            group_root(H)

            def gla():
                asked = sem("gla_asked")
                given = sem("gla_given")
                act.wait_ge(asked, 1)
                A.did(act.activation(gla_tmp, gla_la, ACT.Abs))
                A.settle()
                A.did(act.activation(gla_tmp, gla_tmp, ACT.Exp, scale=-1.0))
                A.settle()
                A.did(act.activation(gla_tmp, gla_tmp, ACT.Ln, bias=ones[:, 0:1]), given)
                act.wait_ge(asked, 2)
                A.did(act.activation(gla_la, gla_cum, ACT.Exp), given)
                A.did(act.activation(gla_tmp, gla_cum, ACT.Exp, scale=-1.0), given)
                act.wait_ge(asked, 3)
                A.did(act.activation(gla_tmp, gla_tmp, ACT.Exp), given)

            def rwkv_features():
                lora = u_feat[:, F_RWKV + 6, PAD:]
                act.wait_ge(sem("shifted"), 1)
                A.did(act.activation(lora[0:32, :], lora[0:32, :], ACT.Tanh), sem("lora_ready"))
                A.did(act.activation(lora[64:128, :], lora[64:128, :], ACT.Sigmoid), sem("lora_ready"))
                for dst, b in ((r_lw, "w0"), (r_a, "a0")):
                    for f in range(2):
                        bank = a_ring.take(act)
                        A.did(act.activation(dst[:, :, f, :], bank.rearrange("p (t s) -> p t s", t=TT), ACT.Sigmoid,
                                             bias=COLS(cols, b, f, f + 1)), a_ring.drained)
                for t in range(TT):
                    bank = a_ring.take(act)
                    A.did(act.copy(g_tok[:, t, :], bank[:, 0:W]), a_ring.drained)
                mark["rwkv_gates"] = a_ring.taken
                for t in range(TT // 2):
                    bank = a_ring.take(act)
                    A.did(act.activation(r_t1[:, 2 * t:2 * t + 2, :, :], bank.rearrange("p (t f s) -> p t f s", t=2, f=2), ACT.Sqrt),
                          a_ring.drained)
                mark["rwkv_norms"] = a_ring.taken
                asked, given = sem("rwkv_asked"), sem("rwkv_given")
                act.wait_ge(asked, 1)
                A.did(act.activation(r_t1, r_cw, ACT.Exp), given)
                act.wait_ge(asked, 2)
                A.did(act.activation(r_t2, r_cw, ACT.Exp, scale=-1.0), given)
                act.wait_ge(asked, 3)
                A.did(act.activation(r_t1, r_lw, ACT.Exp), given)
                act.wait_ge(asked, 4)
                A.did(act.activation(r_t2, r_t2, ACT.Exp), given)

            gla()
            group_root(H)
            rwkv_features()
            group_root(H)

            def transposed_rows(out):
                for t in range(TT):
                    for half in range(2):
                        bank = a_ring.take(act)
                        A.did(act.copy(out[:, 4 * half:4 * half + 4, t * P:(t + 1) * P], bank.rearrange("p (k s) -> p k s", k=4)),
                              a_ring.drained)

            def route():
                act.wait_ge(sem("gate_asked"), 1)
                A.did(act.activation(gate4[:, :, 0:TOP], gate4[:, :, 0:TOP], ACT.Exp), sem("gate_given"))

            def experts():
                for half in range(2):
                    bank = a_ring.take(act)
                    A.did(act.copy(xg[:, 4 * half:4 * half + 4, :], bank.rearrange("p (k r) -> p k r", k=4)), a_ring.drained)
                act.wait_ge(sem("routed"), 4)
                blocks, half_blocks = block_counts(act)
                act.sem_inc(ea_ring.drained, 3)
                with act.Fori(0, blocks) as i:
                    T = Turn(act, i, None, PER, CREDIT)
                    ea_ring.taken = 0

                    def swish(c):
                        T.wait(swish_asked, c + 1)
                        T.did(act.activation(swi[:, 512:768], swi[:, 0:256], ACT.Sigmoid, scale=SWIGLU_ALPHA), swish_given)

                    def out(dst, words, **split):
                        bank = ea_ring.take(T)[:, 0:words]
                        if split:
                            bank = bank.rearrange("p (k r) -> p k r", **split)
                        T.did(act.copy(dst, bank), ea_ring.drained)

                    swish(0)
                    swish(1)
                    out(hid_t[:, 0:2, :], 256, k=2)
                    swish(2)
                    out(hid_t[:, 2:4, :], 256, k=2)
                    swish(3)
                    out(hid_t[:, 4:6, :], 256, k=2)
                    out(xg[:, 0:4, :], 512, k=4)
                    out(hid_t[:, 6:8, :], 256, k=2)
                    out(from_t, 512)
                    out(y_blk[:, 0:512], 512)
                    out(y_blk[:, 512:1024], 512)
                    out(xg[:, 4:8, :], 512, k=4)
                for half in range(2):
                    bank = a_ring.take(act)
                    A.did(act.copy(xg[:, 4 * half:4 * half + 4, :], bank.rearrange("p (k r) -> p k r", k=4)), a_ring.drained)
                act.sem_inc(ha_ring.drained, 3)
                with act.Fori(0, half_blocks) as i:
                    T = Turn(act, i, None, HALF_PER, HALF_CREDIT)
                    ha_ring.taken = 0

                    def half_swish(pair):
                        T.wait(half_asked, pair + 1)
                        T.did(act.activation(swi[:, 512:768], swi[:, 0:256], ACT.Sigmoid, scale=SWIGLU_ALPHA), half_given)

                    def half_out(dst, words):
                        bank = ha_ring.take(T)[:, 0:words]
                        T.did(act.copy(dst, bank), ha_ring.drained)

                    def half_hidden_out(pair):
                        bank = ha_ring.take(T)[:, 0:256].rearrange("p (k g r) -> p g k r", k=2, g=2)
                        dst = hid_t[:, 4 * pair:4 * pair + 4, 0:HALF_ROWS].rearrange("p (g k) r -> p g k r", g=2)
                        T.did(act.copy(dst, bank), ha_ring.drained)

                    half_swish(0)
                    half_swish(1)
                    half_hidden_out(0)
                    half_out(xg[:, 0:4, :].rearrange("p k r -> p (k r)"), 512)
                    half_hidden_out(1)
                    half_out(from_t, 512)
                    half_out(y_blk[:, 0:512], 512)
                    half_out(xg[:, 4:8, :].rearrange("p k r -> p (k r)"), 512)

            def gated_embedding():
                rows_root(A, 0, META)
                transposed_rows(h_t)
                mark["ple_gates"] = a_ring.taken
                for n in range(2 * TT):
                    bank = a_ring.take(act)
                    if n >= TT:
                        act.wait_ge(sem("gate_used"), n - TT + 1)
                    A.did(act.activation(ple_gate[:, n % TT, :], bank, ACT.Sigmoid), a_ring.drained)
                    if n >= TT:
                        rows_root(A, n - TT)
                        rows_root(A, n - TT)

            transposed_rows(y_t)
            for t in range(TT):
                rows_root(A, t)
            transposed_rows(x1_t)
            route()
            experts()
            gated_embedding()

            def layer(T):
                la_ring.taken = 0

                def turned(meta_banks=2):
                    for t in range(NT2):
                        n = SIZE[t]
                        banks = 2 if t else meta_banks
                        k = KT // banks
                        for b in range(banks):
                            bank = la_ring.take(T)
                            T.did(act.copy(h2_t[:, k * b:k * b + k, OFF[t]:OFF[t] + n],
                                           bank[:, 0:k * n].rearrange("p (k s) -> p k s", k=k)), la_ring.drained)

                def project():
                    for n in range(4):
                        for t in range(1, NT2):
                            bank = la_ring.take(T)
                            T.did(act.copy(u2[:, t, n * 512:n * 512 + WIDTHS[n]], bank[:, 0:WIDTHS[n]]), la_ring.drained)
                    bank = la_ring.take(T)
                    for n in range(4):
                        T.did(act.copy(u2[0:META, 0, n * 512:n * 512 + WIDTHS[n]], bank[32 * n:32 * n + META, 0:WIDTHS[n]]),
                              la_ring.drained if n == 3 else None)
                    assert la_ring.taken == PROJECTED
                    T.settle()
                    for part, tiles in PARTS:
                        g = u2[0:part, tiles, U_G:U_G + RH * RV]
                        T.did(act.activation(g, g, ACT.Silu), sem("ret_gate_ready"))

                def forget_gate():
                    T.wait(sem("forget_asked"), 1)
                    T.did(act.activation(f_row[0:FH, 1, :], f_row[0:FH, 0, :], ACT.Abs))
                    T.settle()
                    T.did(act.activation(f_row[0:FH, 1, :], f_row[0:FH, 1, :], ACT.Exp, scale=-1.0))
                    T.settle()
                    T.did(act.activation(f_row[0:FH, 1, :], f_row[0:FH, 1, :], ACT.Ln, bias=ones[0:FH, 0:1]), sem("forget_given"))

                def forget():
                    waiting = []
                    turned_jobs = [0]

                    def turn_weights():
                        i, n = waiting.pop(0)
                        m = SIZE[i]
                        for first, last in ([(0, i + 1)] if i < 4 else [(0, 4), (4, 5)]):
                            bank = psum[:, 4 + turned_jobs[0] % 2, :]
                            T.wait(sem("fox_turned"), turned_jobs[0] + 1)
                            if first == 0:
                                if n >= 2:
                                    T.wait(sem("fox_out"), n - 1)
                                T.did(act.copy(fox_pt[0:META, n % 2, 0, 0:m], bank[0:META, 0:m]),
                                      sem("fox_turned_drained") if last == 1 else None)
                            if last > 1:
                                a = max(first, 1)
                                T.did(act.copy(fox_pt[:, n % 2, a:last, 0:m],
                                               bank[:, (a - first) * m:(last - first) * m].rearrange("p (j s) -> p j s", s=m)),
                                      sem("fox_turned_drained"))
                            turned_jobs[0] += 1

                    n = 0
                    for h in range(FH):
                        for i in range(NT2):
                            T.wait(sem("fox_max"), n + 1)
                            p = fox_p[0:SIZE[i], n % 3, 0:OFF[i] + SIZE[i]]
                            T.did(act.activation(p, p, ACT.Exp, bias=row_max[0:SIZE[i], n % 4:n % 4 + 1],
                                                 accum_out=row_sum[0:SIZE[i], n % 4:n % 4 + 1]), sem("fox_weights_ready"))
                            waiting.append((i, n))
                            n += 1
                            if len(waiting) > 2:
                                turn_weights()
                    turn_weights()
                    turn_weights()

                turned(1)
                project()
                forget_gate()
                for part, tiles in PARTS:
                    root(T, stat2[0:part, tiles.start * RH:tiles.stop * RH], False)
                forget()
                turned()
                for t in range(NT2):
                    rows_root(T, t, SIZE[t])
                turned()
                for f in range(FT):
                    for c in range(2):
                        bank = la_ring.take(T)
                        T.did(act.activation(ff_t[:, f, c * HALF:(c + 1) * HALF], bank[:, 0:HALF], ACT.Silu), la_ring.drained)
                for t in range(NT2):
                    rows_root(T, t, SIZE[t])

            act.sem_inc(la_ring.drained, 3)
            act.sem_inc(sem("fox_turned_drained"), 2)
            with act.Fori(0, LAYERS) as i:
                T = Turn(act, i, sem("layer_scalar_step"), LAYER_PER, LAYER_CREDIT)
                T.roots = 0
                layer(T)
                T.check()

        @block.vector
        def _(dve):
            V = Steps(dve, dve_step)
            V.roots = 0

            def then(ins, s=None):
                V.did(ins, s)
                V.settle()

            def project_block1():
                then(dve.memset(u_feat[:, :, 0:PAD], 0.0))
                for i in range(NF):
                    bank = v_ring.take(dve)
                    V.did(dve.tensor_copy(u_feat[:, i, PAD:], bank), v_ring.drained)

            def bias_rows():
                b = COLS(cols, "rows_b")
                dve.wait_ge(a_ring.filled, mark["projected"])
                V.settle()
                u = u_feat[:, F_ROWS, PAD:]
                V.did(dve.tensor_scalar(hrow[0:4, R_DT, :], u[0:4, :], b[0:4, :], None, ALU.add), rows_biased)
                V.did(dve.tensor_scalar(hrow[0:4, R_NF, :], u[64:68, :], b[64:68, :], -1.0, ALU.add, ALU.mult), rows_biased)
                V.did(dve.tensor_scalar(hrow[0:4, R_G, :], u[32:36, :], b[32:36, :], None, ALU.add), rows_biased)
                V.did(dve.memset(den, 0.0), rows_biased)

            def finish_rows():
                dve.wait_ge(rows_softplus, 1)
                then(dve.scalar_tensor_tensor(hrow[0:4, 0:2, :], hrow[0:4, 0:2, :], 0.0, hrow[0:4, 2:4, :], ALU.max, ALU.add))
                one = ones[0:4, 0:1].broadcast_to([4, SEQ])
                then(dve.tensor_scalar(hrow[0:4, 2, :], hrow[0:4, R_DT, :], expa[0:4, :], -1.0, ALU.mult, ALU.mult))
                V.did(dve.tensor_tensor_scan(hrow[0:4, R_A, :], one, hrow[0:4, 2, :], 0.0, ALU.mult, ALU.add))
                then(dve.tensor_tensor_scan(hrow[0:4, R_F, :], one, hrow[0:4, R_NF, :], 0.0, ALU.mult, ALU.subtract))
                then(dve.tensor_tensor(hrow[0:4, R_G, :], hrow[0:4, R_G, :], hrow[0:4, R_F, :], ALU.subtract))
                then(dve.tensor_tensor_scan(hrow[0:4, R_M, :], hrow[0:4, R_G, :], hrow[0:4, R_G, :], 0.0, ALU.max, ALU.max))
                V.did(dve.scalar_tensor_tensor(hrow[0:4, R_F, :], hrow[0:4, R_F, :], -1.0, hrow[0:4, R_M, :], ALU.mult, ALU.subtract), hrow_ready)

            def convolve():
                for i in range(8):
                    u = u_feat[:, F_SSD + i, :]
                    w = COLS(cols, "ssd_cw", 4 * i, 4 * i + 4) if i < 4 else COLS(cols, "m_cw", 4 * i - 16, 4 * i - 12)
                    acc = conv_acc[:, i % 2, :]
                    if i >= 2:
                        dve.wait_ge(conv_ready, i - 1)
                    then(dve.tensor_scalar(acc, u[:, 3:3 + SEQ], w[:, 3:4], None, ALU.mult))
                    for tap in (2, 1):
                        then(dve.scalar_tensor_tensor(acc, u[:, tap:tap + SEQ], w[:, tap:tap + 1], acc, ALU.mult, ALU.add))
                    V.did(dve.scalar_tensor_tensor(acc, u[:, 0:SEQ], w[:, 0:1], acc, ALU.mult, ALU.add), conv_summed)

            def head_columns():
                bank = v_ring.take(dve)
                then(dve.tensor_copy(small[:, 0:64], bank[:, 0:64]), v_ring.drained)
                V.did(dve.memset(den, 0.0), hcol_ready)

            def ssd_values():
                dve.wait_ge(conv_ready, 8)
                for t in range(TT):
                    bank = v_ring.take(dve)
                    V.did(dve.tensor_copy(xs_tok[:, t, :], bank[:, 0:W]), v_ring.drained)
                V.settle()

            def decayed_attention():
                def argument(n):
                    g, i = n // TT, n % TT
                    m, h = g // H, g % H
                    w = SEQ - i * P
                    V.settle()
                    V.did(dve.scalar_tensor_tensor(decay[:, n % 2, 0:w], row_cast[:, g % 2, i * P:], hcol[:, 1 + m, i, h:h + 1],
                                                   CONST1(c1, "causal", 0, w), ALU.subtract,
                                                   ALU.add if m == 0 else ALU.subtract), decay_arg)

                def weights(n):
                    g, i = n // TT, n % TT
                    m, h = g // H, g % H
                    w = SEQ - i * P
                    dve.wait_ge(decay_ready, n + 1)
                    if n >= 2:
                        dve.wait_ge(pv_done, n - 1)
                    bank = v_ring.take(dve)
                    V.did(dve.scalar_tensor_tensor(weigh[:, n % 2, 0:w], bank[:, 0:w],
                                                   hcol[:, 0, i, h:h + 1] if m == 0 else HD ** -0.5,
                                                   decay[:, n % 2, 0:w], ALU.mult, ALU.mult), v_ring.drained)

                def collect(g):
                    m, h = g // H, g % H
                    sums = psum[:, 6 + g % 2, :]
                    acc = sums[:, 0:TT * HD].rearrange("p (t d) -> p t d", t=TT)
                    dve.wait_ge(pv_done, TT * (g + 1))
                    if m == 0:
                        V.did(dve.scalar_tensor_tensor(y[:, :, h * HD:(h + 1) * HD], xs_tok[:, :, h * HD:(h + 1) * HD],
                                                       ROWS(rows, "ssd_d", h, h + 1), acc, ALU.mult, ALU.add), sums_drained)
                    else:
                        d = sums[:, TT * HD:TT * HD + TT]
                        dve.wait_ge(sem("floor_ready"), 1)
                        then(dve.tensor_copy(stat[:, 0:TT], d))
                        then(dve.scalar_tensor_tensor(den, stat[:, 0:TT], -1.0, stat[:, 0:TT], ALU.mult, ALU.max))
                        then(dve.tensor_tensor(den, den, hcol[:, 3, :, h], ALU.max))
                        then(dve.reciprocal(den, den))
                        V.did(dve.tensor_tensor(y[:, :, 3 * W + h * HD:3 * W + (h + 1) * HD], acc,
                                                den.rearrange("p (t o) -> p t o", o=1).broadcast_to([P, TT, HD]), ALU.mult), sums_drained)

                for g in range(2 * H):
                    bank = v_ring.take(dve)
                    then(dve.tensor_copy(row_cast[:, g % 2, :], bank), v_ring.drained)
                    for i in range(TT):
                        argument(g * TT + i)
                        if i:
                            weights(g * TT + i - 1)
                    weights(g * TT + TT - 1)
                    if g:
                        collect(g - 1)
                collect(2 * H - 1)
                V.settle()

            def group_norm(view, groups, centered, gain, bias=None, tmp=norm_tmp, eps=LN_EPS):
                n = W // groups
                t = TT * groups
                y4 = heads_of(view, groups)
                tmp4 = tmp.rearrange("p (t h d) -> p t h d", t=TT, h=groups)
                s = stat[:, 0:t].rearrange("p (t h) -> p t h", t=TT)
                s4 = stat[:, 0:t].rearrange("p (t h o) -> p t h o", t=TT, o=1).broadcast_to([P, TT, groups, n])
                if centered:
                    then(dve.tensor_reduce(s, y4, AX.X, ALU.add))
                    then(dve.tensor_scalar(stat[:, 0:t], stat[:, 0:t], 1.0 / n, None, ALU.mult))
                    then(dve.tensor_tensor(y4, y4, s4, ALU.subtract))
                then(dve.tensor_tensor(tmp4, y4, y4, ALU.mult))
                then(dve.tensor_reduce(s, tmp4, AX.X, ALU.add))
                then(dve.tensor_scalar(stat[:, 0:t], stat[:, 0:t], 1.0 / n, eps, ALU.mult, ALU.add), variance_ready)
                V.roots += 1
                dve.wait_ge(root_ready, V.roots)
                then(dve.reciprocal(stat[:, 0:t], stat[:, 0:t]))
                then(dve.tensor_tensor(y4, y4, s4, ALU.mult))
                g3 = gain.rearrange("p (o d) -> p o d", o=1).broadcast_to([P, TT, W])
                then(dve.tensor_tensor(view, view, g3, ALU.mult))
                if bias is not None:
                    b3 = bias.rearrange("p (o d) -> p o d", o=1).broadcast_to([P, TT, W])
                    then(dve.tensor_tensor(view, view, b3, ALU.add))

            dve.wait_ge(setup_landed, 16 * len(SETUP))
            project_block1()
            convolve()
            bias_rows()
            finish_rows()
            head_columns()
            ssd_values()
            decayed_attention()
            dve.wait_ge(z_ready, 3)
            then(dve.tensor_tensor(y[:, :, 0:W], y[:, :, 0:W], u_tok[:, :, T_Z:T_Z + W], ALU.mult))
            group_norm(y[:, :, 0:W], 1, False, ROWS(rows, "ssd_g"))
            then(dve.tensor_tensor(y[:, :, 3 * W:], y[:, :, 3 * W:], u_tok[:, :, T_MOG:T_MOG + W], ALU.mult))
            group_norm(y[:, :, 3 * W:], H, True, ROWS(rows, "m_g"))

            def gla():
                asked, given, ready = sem("gla_asked"), sem("gla_given"), sem("gla_ready")
                q, k = u_feat[:, F_GLA, PAD:], u_feat[:, F_GLA + 1, PAD:]
                bank = v_ring.take(dve)
                then(dve.tensor_scalar(gla_la, bank, COLS(cols, "gate_b"), None, ALU.add), v_ring.drained)
                V.did(dve.memset(gla_state[:, 0, :], 0.0), asked)
                dve.wait_ge(given, 1)
                then(dve.scalar_tensor_tensor(gla_la, gla_la, 0.0, gla_tmp, ALU.min, ALU.subtract))
                then(dve.tensor_scalar(gla_la, gla_la, 1.0 / 16.0, None, ALU.mult))
                dve.wait_ge(sem("const2_landed"), 16)
                then(dve.tensor_tensor_scan(gla_cum, CONST2(c2, "reset"), gla_la, 0.0, ALU.mult, ALU.add), asked)
                dve.wait_ge(given, 3)
                then(dve.scalar_tensor_tensor(q, q, (P // H) ** -0.5, gla_la, ALU.mult, ALU.mult))
                V.did(dve.tensor_copy(gla_eb, gla_la[:, CH - 1::CH]))
                then(dve.tensor_tensor(gla_kdec.rearrange("p t c -> p (t c)"), k, gla_tmp, ALU.mult))
                c3 = gla_cum.rearrange("p (c s) -> p c s", s=CH)
                V.did(dve.tensor_tensor(gla_tmp.rearrange("p (c s) -> p c s", s=CH), c3[:, :, CH - 1:CH].broadcast_to([P, 8, CH]), c3,
                                        ALU.subtract), asked)
                dve.wait_ge(given, 4)
                then(dve.tensor_tensor(gla_tmp, k, gla_tmp, ALU.mult))
                V.did(dve.tensor_copy(k, gla_kdec.rearrange("p t c -> p (t c)")), ready)
                V.settle()
                V.did(dve.memset(den, 0.0), ready)
                bank = v_ring.take(dve)
                then(dve.tensor_copy(gla_kdec.rearrange("p t c -> p (t c)"), bank), v_ring.drained)
                for c in range(7):
                    bank = v_ring.take(dve)
                    then(dve.tensor_tensor(gla_state[:, c + 1, :], bank[:, 0:W], CONST2(c2, "glamask"), ALU.mult), v_ring.drained)
                    then(dve.scalar_tensor_tensor(gla_state[:, c + 1, :], gla_state[:, c, :], gla_eb[:, c:c + 1], gla_state[:, c + 1, :],
                                                  ALU.mult, ALU.add), ready if c == 6 else None)
                incl = CONST2(c2, "mask4", P, 2 * P).rearrange("p (o s) -> p o s", o=1).broadcast_to([P, H, P])

                def mask_queries(t):
                    if t >= 2:
                        dve.wait_ge(v_ring.filled, scores_taken[t - 2])
                    V.settle()
                    for h in range(H):
                        ins = dve.tensor_scalar(gla_qm[:, t % 2 * 2 + h // 2, h % 2, :], q[:, t * P:(t + 1) * P],
                                                CONST2(c2, "glamask", h * HD, h * HD + 1), None, ALU.mult)
                        V.did(ins, sem("gla_masked") if h == H - 1 else None)

                scores_taken = []

                def mask_scores(t):
                    bank = v_ring.take(dve)
                    scores_taken.append(v_ring.taken)
                    V.did(dve.tensor_tensor(gla_st[:, t % 2], bank.rearrange("p (h s) -> p h s", h=H), incl, ALU.mult), v_ring.drained)

                mask_queries(0)
                mask_queries(1)
                mask_scores(0)
                for t in range(TT):
                    if t + 2 < TT:
                        mask_queries(t + 2)
                    if t + 1 < TT:
                        mask_scores(t + 1)
                    bank = v_ring.take(dve)
                    V.did(dve.tensor_copy(y[:, t, 2 * W:3 * W], bank[:, 0:W]), v_ring.drained)
                V.settle()

            def rwkv_features():
                ready, asked, given = sem("rwkv_ready"), sem("rwkv_asked"), sem("rwkv_given")

                def pair(i):
                    return u_feat[:, F_RWKV + i:F_RWKV + i + 2, PAD:].rearrange("p f (t s) -> p t f s", t=TT)

                def col(name):
                    return [COLS(cols, name, f, f + 1) for f in range(2)]

                def flat(v, f):
                    return v[:, :, f, :]

                for i in (6, *range(6)):
                    u = u_feat[:, F_RWKV + i, :]
                    s = feat_flat[:, 4096 + i % 2 * SEQ:4096 + (i % 2 + 1) * SEQ]
                    then(dve.tensor_tensor(s, u[:, 2:2 + SEQ], u[:, 3:3 + SEQ], ALU.subtract))
                    then(dve.scalar_tensor_tensor(u[:, PAD:], s, COLS(cols, "mu", i, i + 1), u[:, PAD:], ALU.mult, ALU.add),
                         sem("shifted") if i in (5, 6) else None)
                r, k = pair(0), pair(2)
                kk = r_kk
                for f in range(2):
                    V.did(dve.tensor_scalar(flat(kk, f), flat(k, f), col("k_k")[f], None, ALU.mult))
                V.did(dve.tensor_scalar(r_omka, COLS(cols, "k_a"), -1.0, 1.0, ALU.mult, ALU.add))
                V.settle()
                then(dve.tensor_tensor(r_tmp, kk, kk, ALU.mult), ready)
                for t in range(TT):
                    bank = v_ring.take(dve)
                    V.did(dve.tensor_copy(v_tok[:, t, :], bank[:, 0:W]), v_ring.drained)
                dve.wait_ge(a_ring.drained, mark["rwkv_gates"])
                then(dve.tensor_scalar(r_lw, r_lw, -float(np.exp(-0.5)), None, ALU.mult))
                reset = CONST2(c2, "reset", 0, P)
                for t in range(TT):
                    for f in range(2):
                        V.did(dve.tensor_tensor_scan(r_cw[:, t, f, :], reset, r_lw[:, t, f, :], 0.0, ALU.mult, ALU.add))
                for f in range(2):
                    V.did(dve.tensor_scalar(flat(r_t2, f), flat(r_a, f), col("k_a")[f], r_omka[:, f:f + 1], ALU.mult, ALU.add))
                V.settle()
                then(dve.tensor_tensor(k, k, r_t2, ALU.mult))
                dve.wait_ge(a_ring.drained, mark["rwkv_norms"])
                then(dve.tensor_scalar(r_t1, r_t1, 1e-12, None, ALU.max))
                then(dve.reciprocal(r_t1, r_t1))
                then(dve.tensor_tensor(kk, kk, r_t1, ALU.mult), asked)
                then(dve.tensor_tensor(r_tmp, r, k, ALU.mult))
                for f in range(2):
                    V.did(dve.tensor_scalar(flat(r_tmp, f), flat(r_tmp, f), col("r_k")[f], None, ALU.mult), ready if f else None)
                dve.wait_ge(given, 1)
                then(dve.tensor_tensor(r_at[:, :, :, 1, :], r, r_t1, ALU.mult), asked)
                then(dve.tensor_copy(r_wl, r_t1[:, :, :, CH - 1::CH]))
                then(dve.tensor_tensor(r_lw, r_cw, r_lw, ALU.subtract), asked)
                then(dve.tensor_tensor(r_a, kk, r_a, ALU.mult))
                bank = v_ring.take(dve)
                then(dve.tensor_copy(small[:, 120:136], bank[:, 0:16]), v_ring.drained)
                dve.wait_ge(given, 2)
                V.did(dve.tensor_tensor(r_bk[:, 0], r_a, r_t2, ALU.mult))
                then(dve.tensor_tensor(r_bk[:, 1], k, r_t2, ALU.mult))
                t5 = r_t2.rearrange("p t f (c s) -> p t (f c) s", s=CH)
                for t in range(TT):
                    ct = r_cw[:, t].rearrange("p f (c s) -> p (f c) s", s=CH)
                    V.did(dve.tensor_tensor(t5[:, t], ct[:, :, CH - 1:CH].broadcast_to([P, 4, CH]), ct, ALU.subtract),
                          asked if t == TT - 1 else None)
                dve.wait_ge(given, 3)
                then(dve.tensor_scalar(r_t1, r_t1, -1.0, None, ALU.mult))
                then(dve.tensor_tensor(r_at[:, :, :, 0, :], kk, r_t1, ALU.mult))
                dve.wait_ge(given, 4)
                V.did(dve.tensor_tensor(r_dec[:, 0], r_a, r_t2, ALU.mult))
                V.did(dve.tensor_tensor(r_dec[:, 1], k, r_t2, ALU.mult))
                V.settle()
                V.did(dve.memset(r_state[:, 0], 0.0))
                V.did(dve.memset(r_gt, 0.0), ready)
                V.settle()
                V.did(dve.memset(den, 0.0), sem("state_ready"))

            def mask_heads(t):
                for g in range(2):
                    V.did(dve.tensor_scalar(r_atm[:, :, g].rearrange("p f k s -> p f (k s)"), r_at[:, t].rearrange("p f k s -> p f (k s)"),
                                            CONST2(c2, "headsum", g, g + 1), None, ALU.mult), sem("rwkv_masked") if g else None)

            def rwkv_tile(t):
                def over_heads(mask):
                    return mask.rearrange("p (o s) -> p o s", o=1).broadcast_to([P, H, P])

                def over_pairs(mask):
                    return mask.rearrange("p (o u s) -> p o u s", o=1, u=1).broadcast_to([P, 2, 2, P])

                def four(bank):
                    return bank.rearrange("p (h s) -> p h s", h=H)

                def pairs(v):
                    return v.rearrange("p (f g) s -> p f g s", f=2)

                for f in range(2):
                    for kind in range(2):
                        bank = v_ring.take(dve)
                        V.did(dve.tensor_tensor(r_mt[:, f, kind].rearrange("p g q s -> p (g q s)"), bank, CONST2(c2, "mask4"), ALU.mult),
                              v_ring.drained)
                bank = v_ring.take(dve)
                then(dve.tensor_tensor(r_mlo, four(bank), over_heads(CONST2(c2, "lower")), ALU.mult), v_ring.drained)
                bank = v_ring.take(dve)
                V.did(dve.tensor_copy(r_anv[:, :, 0:HD], bank[:, 0:W].rearrange("p (h d) -> p h d", h=H)), v_ring.drained)
                bank = v_ring.take(dve)
                V.did(dve.tensor_copy(r_dtok, four(bank)), v_ring.drained)

                def level(n, upper, spread=over_heads):
                    return spread(CONST2(c2, "level", (2 * n + upper) * P, (2 * n + upper + 1) * P))

                V.settle()
                V.did(dve.tensor_tensor(r_x, r_mlo, level(0, 0), ALU.mult))
                V.did(dve.tensor_tensor(pairs(r_xt), r_mt[:, :, 0, :, 0, :], level(0, 1, over_pairs), ALU.mult))
                V.settle()
                V.did(dve.tensor_tensor(r_x, r_x, over_heads(ident), ALU.add))
                V.did(dve.tensor_tensor(r_xt, r_xt, over_heads(ident), ALU.add))
                bank = v_ring.take(dve)
                V.did(dve.tensor_copy(r_anv[:, :, HD:P], bank[:, 0:W].rearrange("p (h d) -> p h d", h=H)), v_ring.drained)
                def part_of_m(n):
                    V.did(dve.tensor_tensor(pairs(r_mot), r_mt[:, :, 0, :, 0, :], level(n, 1, over_pairs), ALU.mult), sem("level_ready"))

                V.settle()
                part_of_m(1)
                for n in range(1, 6):
                    bank = v_ring.take(dve)
                    V.did(dve.tensor_copy(r_prod, four(bank)), v_ring.drained)
                    V.settle()
                    if n < 5:
                        part_of_m(n + 1)
                    elif t + 1 < TT:
                        mask_heads(t + 1)
                    if n < 5:
                        bank = v_ring.take(dve)
                        V.did(dve.tensor_tensor(r_x, r_x, four(bank), ALU.add), v_ring.drained)
                    bank = v_ring.take(dve)
                    V.did(dve.tensor_tensor(r_xt, r_xt, four(bank), ALU.add), v_ring.drained)
                bank = v_ring.take(dve)
                V.did(dve.tensor_copy(r_xau, four(bank)), v_ring.drained)
                bank = v_ring.take(dve)
                V.did(dve.tensor_tensor(r_rot, bank[:, 0:2 * P].rearrange("p (f s) -> p f s", f=2), r_at[:, t, :, 1, :], ALU.add), v_ring.drained)
                for c in range(2):
                    bank = v_ring.take(dve)
                    for g in range(2):
                        part = slice(g * HD, (g + 1) * HD)
                        V.did(dve.tensor_copy(r_gt[part, c, :, part], bank[part, 0:P].rearrange("p (f v) -> p f v", f=2)),
                              v_ring.drained if g else None)
                for c in range(2):
                    n = 2 * t + c
                    bank = v_ring.take(dve)
                    V.settle()
                    for f in range(2):
                        V.did(dve.scalar_tensor_tensor(r_state[:, (n + 1) % 3, f, :], r_state[:, n % 3, f, :], r_wl[:, t, f, c:c + 1],
                                                       bank[:, f * P:(f + 1) * P], ALU.mult, ALU.add), v_ring.drained if f else None)
                    V.settle()
                    V.did(dve.memset(den, 0.0), sem("state_ready"))
                dve.wait_ge(sem("rwkv_out_filled"), t + 1)
                V.did(dve.tensor_copy(y[:, t, W:2 * W], psum[:, 6 + t % 2, 0:W]), sem("rwkv_out_drained"))

            gla()
            group_norm(y[:, :, 2 * W:3 * W], H, False, ROWS(rows, "gla_g"))
            then(dve.tensor_tensor(y[:, :, 2 * W:3 * W], y[:, :, 2 * W:3 * W], u_tok[:, :, T_GOG:T_GOG + W], ALU.mult))
            rwkv_features()
            mask_heads(0)
            for t in range(TT):
                rwkv_tile(t)
            V.settle()
            yr = y[:, :, W:2 * W]
            group_norm(yr, H, True, ROWS(rows, "rwkv_g"), ROWS(rows, "rwkv_b"), eps=GN_EPS_RWKV)
            then(dve.tensor_tensor(heads_of(norm_tmp.rearrange("p (t w) -> p t w", t=TT), H), heads_of(v_tok, H),
                                   r_bonus.rearrange("p t (h o) -> p t h o", o=1).broadcast_to([P, TT, H, HD]), ALU.mult))
            then(dve.tensor_tensor(yr, yr, norm_tmp.rearrange("p (t w) -> p t w", t=TT), ALU.add))
            then(dve.tensor_tensor(yr, yr, g_tok, ALU.mult), sem("mixed"))

            def norm_rows(S, row, t, par, ready=None, parts=P):
                stats, mean, deviation = ln_stats[0:parts, t, :], ln_mean[0:parts, t, 0:1], ln_mean[0:parts, t, 1:2]
                S.settle()
                for half in range(2):
                    S.did(dve.bn_stats(stats[:, half * 6:half * 6 + 6], row[:, half * 512:(half + 1) * 512]))
                S.settle()
                S.hold()
                S.did(dve.bn_aggr(ln_mean[0:parts, t, :], stats), variance_ready)
                S.settle()
                S.roots += 1
                S.did(dve.scalar_tensor_tensor(row, row, mean, par[0:parts, 0, :], ALU.subtract, ALU.mult))
                S.wait(root_ready, S.roots)
                S.did(dve.reciprocal(deviation, deviation))
                S.settle()
                S.did(dve.scalar_tensor_tensor(row, row, deviation, par[0:parts, 1, :], ALU.mult, ALU.add), ready)

            def mix_out():
                dve.wait_ge(sem("x_rows_landed"), 16)
                dve.wait_ge(sem("ln_landed"), 16)
                for half in range(2):
                    part = slice(half * 512, (half + 1) * 512)
                    for t in range(TT):
                        bank = v_ring.take(dve)
                        V.did(dve.scalar_tensor_tensor(x1[:, t, part], x1[:, t, part], ALPHA1, bank, ALU.mult, ALU.add), v_ring.drained)
                        if half == 1:
                            norm_rows(V, x1[:, t, :], t, ln_par, sem("x1_ready"))
                V.settle()

            def route():
                iota = CONST3(c3, "iota")
                routed = sem("routed")
                dve.wait_ge(sem("router_landed"), 16 * 4)
                bank = v_ring.take(dve)
                then(dve.tensor_tensor(logits, bank[:, 0:TT * E].rearrange("p (t e) -> p t e", t=TT),
                                       router_b.rearrange("p (o e) -> p o e", o=1).broadcast_to([P, TT, E]), ALU.add), v_ring.drained)
                for t in range(TT):
                    then(dve.max(top[:, t, :], logits[:, t, :]))
                    then(dve.max_index(top_i[:, t, :].bitcast(mybir.dt.uint32), top[:, t, :], logits[:, t, :]))
                then(dve.tensor_tensor(gate4[:, :, 0:TOP], top[:, :, 0:TOP], top[:, :, 0:1].broadcast_to([P, TT, TOP]), ALU.subtract),
                     sem("gate_asked"))
                then(dve.tensor_copy(top, top_i.bitcast(mybir.dt.uint32)))
                dve.wait_ge(sem("gate_given"), 1)
                sums = rank[:, 20:24]
                then(dve.tensor_reduce(sums.rearrange("p (t o) -> p t o", o=1), gate4[:, :, 0:TOP], AX.X, ALU.add))
                then(dve.reciprocal(sums, sums))
                then(dve.tensor_tensor(gate4[:, :, 0:TOP], gate4[:, :, 0:TOP],
                                       sums.rearrange("p (t o) -> p t o", o=1).broadcast_to([P, TT, TOP]), ALU.mult))
                for t in range(TT):
                    for n in range(TOP):
                        dst = gates[:, t, :] if n == 0 else assigned[:, t, :]
                        then(dve.tensor_scalar(dst, iota[:, 0:E], top[:, t, n:n + 1], gate4[:, t, n:n + 1], ALU.is_equal, ALU.mult))
                        if n:
                            then(dve.tensor_tensor(gates[:, t, :], gates[:, t, :], assigned[:, t, :], ALU.add))
                then(dve.tensor_scalar(assigned, gates, 0.0, None, ALU.is_gt), routed)
                bank = v_ring.take(dve)
                then(dve.tensor_copy(gates_t[0:E, :], bank[0:E, :]), v_ring.drained)
                bank = v_ring.take(dve)
                then(dve.scalar_tensor_tensor(pos, bank[:, 0:TT * E].rearrange("p (t e) -> p t e", t=TT), 1.0, assigned, ALU.add, ALU.mult),
                     v_ring.drained)
                then(dve.tensor_scalar(pos, pos, -1.0, None, ALU.add))
                bank = v_ring.take(dve)
                rows_of = rank[0:E, 12:13]
                then(dve.tensor_copy(rows_of, bank[0:E, 0:1]), v_ring.drained)
                flag = [rank[0:E, n:n + 1] for n in range(KINDS)]
                earlier = [rank[0:E, KINDS + n:KINDS + n + 1] for n in range(KINDS)]
                full, halved = rank[0:E, 10:11], rank[0:E, 11:12]
                V.did(dve.memset(earlier[0], 0.0))
                V.did(dve.tensor_scalar(flag[0], rows_of, float(HALF_ROWS), None, ALU.is_gt))
                for n in range(1, 4):
                    V.did(dve.tensor_scalar(flag[n], rows_of, float(P * n), None, ALU.is_gt))
                for n in range(MIN_BLOCKS):
                    V.settle()
                    V.did(dve.tensor_tensor(flag[0], flag[0], ident[0:E, n:n + 1], ALU.max))
                V.settle()
                then(dve.tensor_copy(earlier[1], flag[0]))
                V.did(dve.tensor_scalar(flag[4], flag[0], -1.0, 1.0, ALU.mult, ALU.add))
                for n in range(1, 4):
                    then(dve.tensor_tensor(earlier[n + 1] if n < 3 else full, earlier[n], flag[n], ALU.add))
                V.did(dve.tensor_copy(halved, flag[4]))
                then(dve.tensor_scalar(earlier[4], ident[0:E, 0:1], float(HALF_AT), None, ALU.mult), routed)
                bank = v_ring.take(dve)
                then(dve.tensor_copy(pos_t[0:E, :], bank[0:E, :]), v_ring.drained)
                bank = v_ring.take(dve)
                place = rank[0:E, 13:13 + KINDS]
                then(dve.tensor_copy(place, bank[0:E, 0:KINDS]), v_ring.drained)
                bank = v_ring.take(dve)
                then(dve.tensor_scalar(block_count, bank[:, 0:2], float(MIN_BLOCKS), None, ALU.max), v_ring.drained)
                V.did(dve.memset(hot[0:E, :], 0.0))
                V.did(dve.memset(base_w[0:E, :], 0.0))
                V.did(dve.tensor_copy(half_iota[:, 0:HALF_ROWS], iota[:, 0:HALF_ROWS]))
                V.did(dve.tensor_copy(half_iota[:, HALF_ROWS:], iota[:, 0:HALF_ROWS]))
                V.settle()
                column = logits.rearrange("p t e -> p (t e)")[0:E, 0:NB]
                for n in range(KINDS):
                    then(dve.tensor_scalar(column, iota[0:E, 0:NB], place[:, n:n + 1], flag[n], ALU.is_equal, ALU.mult))
                    V.did(dve.tensor_tensor(hot[0:E, :], hot[0:E, :], column, ALU.add), routed if n == KINDS - 1 else None)
                    if 1 <= n <= 3:
                        V.did(dve.scalar_tensor_tensor(base_w[0:E, :], column, float(P * n), base_w[0:E, :], ALU.mult, ALU.add))
                    V.settle()
                bank = v_ring.take(dve)
                V.did(dve.tensor_copy(block_expert, bank[:, 0:NB]))
                then(dve.tensor_copy(base_w, bank[:, P:P + NB]), v_ring.drained)
                bank = v_ring.take(dve)
                then(dve.tensor_tensor(block_pos, bank[:, 0:TT * NB].rearrange("p (t n) -> p t n", t=TT),
                                       base_w.rearrange("p (o n) -> p o n", o=1).broadcast_to([P, TT, NB]), ALU.subtract), v_ring.drained)
                bank = v_ring.take(dve)
                then(dve.tensor_copy(block_gate, bank[:, 0:TT * NB].rearrange("p (t n) -> p t n", t=TT)), v_ring.drained)
                for t in range(TT):
                    V.did(dve.tensor_scalar(to_block[:, t, :], iota, block_pos[:, t, 0:1], None, ALU.is_equal),
                          sem("first_block_ready") if t == TT - 1 else None)
                V.did(dve.memset(rank[0:E, 0:1], 0.0), routed)
                for t in range(TT):
                    for half in range(2):
                        part = slice(half * 512, (half + 1) * 512)
                        bank = v_ring.take(dve)
                        V.did(dve.scalar_tensor_tensor(ffn[:, t, part], x1[:, t, part], ALPHA1, bank, ALU.mult, ALU.add), v_ring.drained)
                V.settle()

            def experts():
                iota = CONST3(c3, "iota")
                own = sem("expert_vector_step")
                per = {**PER, own.name: 14}
                blocks, half_blocks = block_counts(dve)
                dve.sem_inc(ev_ring.drained, 12 + 3)
                with dve.Fori(0, blocks) as i:
                    T = Turn(dve, i, own, per, CREDIT)
                    ev_ring.taken = 0

                    def maps(out, n, gated, ready, iota=iota):
                        for t in range(TT):
                            at = block_pos[:, t, bass.ds(n, 1)]
                            if gated:
                                ins = dve.tensor_scalar(out[:, t, :], iota, at, block_gate[:, t, bass.ds(n, 1)], ALU.is_equal, ALU.mult)
                            else:
                                ins = dve.tensor_scalar(out[:, t, :], iota, at, None, ALU.is_equal)
                            T.did(ins, ready if t == TT - 1 else None)

                    for c in range(4):
                        part = slice(c * 512, (c + 1) * 512)
                        if c == 0:
                            T.wait(bias_landed, 16)
                        bank = ev_ring.take(T)
                        T.did(dve.tensor_tensor(swi[:, 0:512], bank, b_gu[:, part], ALU.add), ev_ring.drained)
                        T.settle()
                        T.did(dve.tensor_scalar(swi[:, 0:256], swi[:, 0:256], SWIGLU_LIMIT, None, ALU.min), swish_asked)
                        T.did(dve.tensor_scalar(swi[:, 256:512], swi[:, 256:512], SWIGLU_LIMIT, -SWIGLU_LIMIT, ALU.min, ALU.max))
                        T.wait(swish_given, c + 1)
                        T.did(dve.tensor_tensor(swi[:, 512:768], swi[:, 0:256], swi[:, 512:768], ALU.mult))
                        T.settle()
                        T.did(dve.scalar_tensor_tensor(hid[:, c * 256:(c + 1) * 256], swi[:, 256:512], 1.0, swi[:, 512:768], ALU.add, ALU.mult),
                              hidden_ready)
                        T.settle()
                        if c == 0:
                            maps(from_block, i, True, from_ready)
                        if c == 1:
                            T.wait(ea_ring.filled, 1)
                            maps(to_block, i + 1, False, to_ready)
                    for t in range(TT):
                        for half in range(2):
                            part = slice(half * 512, (half + 1) * 512)
                            bank = ev_ring.take(T)
                            T.did(dve.tensor_tensor(ffn[:, t, part], ffn[:, t, part], bank, ALU.add), ev_ring.drained)
                    assert T.count[own.name] == per[own.name]
                    T.settle()
                dve.wait_ge(ev_ring.drained, blocks * 12 + (12 + 3))
                dve.wait_ge(ea_ring.filled, blocks * 9 + 9)
                for t in range(TT):
                    V.did(dve.tensor_scalar(to_block[:, t, :], half_iota, block_pos[:, t, HALF_AT:HALF_AT + 1], None, ALU.is_equal),
                          sem("first_block_ready") if t == TT - 1 else None)
                own = sem("half_vector_step")
                per = {**HALF_PER, own.name: 10}
                dve.sem_inc(hv_ring.drained, 12 + 3)
                with dve.Fori(0, half_blocks) as i:
                    T = Turn(dve, i, own, per, HALF_CREDIT)
                    hv_ring.taken = 0
                    for pair in range(2):
                        gate, up, sig = swi[:, 0:256], swi[:, 256:512], swi[:, 512:768]
                        if pair == 0:
                            T.wait(half_bias, 32)
                        for c, dst in enumerate((gate, up)):
                            bank = hv_ring.take(T)
                            at = pair * 512 + c * 256
                            T.did(dve.tensor_tensor(dst, bank[:, 0:256], b_gu[:, at:at + 256], ALU.add), hv_ring.drained)
                            T.settle()
                            if c == 0:
                                T.did(dve.tensor_scalar(dst, dst, SWIGLU_LIMIT, None, ALU.min), half_asked)
                            else:
                                T.did(dve.tensor_scalar(dst, dst, SWIGLU_LIMIT, -SWIGLU_LIMIT, ALU.min, ALU.max))
                        T.wait(half_given, pair + 1)
                        T.did(dve.tensor_tensor(sig, gate, sig, ALU.mult))
                        T.settle()
                        T.did(dve.scalar_tensor_tensor(hid[:, pair * 256:(pair + 1) * 256], up, 1.0, sig, ALU.add, ALU.mult), half_hidden)
                        T.settle()
                        if pair == 0:
                            maps(from_block, i + HALF_AT, True, half_from_ready, half_iota)
                            T.wait(ha_ring.drained, 0)
                            maps(to_block, i + HALF_AT + 1, False, half_to_ready, half_iota)
                    for t in range(TT):
                        for half in range(2):
                            part = slice(half * 512, (half + 1) * 512)
                            bank = hv_ring.take(T)
                            T.did(dve.tensor_tensor(ffn[:, t, part], ffn[:, t, part], bank, ALU.add), hv_ring.drained)
                    assert T.count[own.name] == per[own.name]
                    T.settle()
                dve.wait_ge(hv_ring.drained, half_blocks * 12 + (12 + 3))
                V.did(dve.memset(den, 0.0), sem("ffn_ready"))
                dve.sem_inc(sem("early_slots_free"), 1)

            def gated_embedding():
                dve.wait_ge(sem("ln_landed"), 48)
                dve.wait_ge(sem("meta_landed"), 16)
                norm_rows(V, h2[0:META, 0, :], 0, ln_emb, sem("layer_start"), META)
                for n in range(2 * TT):
                    t, part = n % TT, slice(n // TT * 512, (n // TT + 1) * 512)
                    bank = v_ring.take(dve)
                    dve.wait_ge(a_ring.drained, mark["ple_gates"] + n + 1)
                    V.settle()
                    then(dve.tensor_tensor(ple_gate[:, t, :], ple_gate[:, t, :], bank, ALU.mult), v_ring.drained)
                    then(dve.tensor_tensor(ffn[:, t, part], ffn[:, t, part], ple_gate[:, t, :], ALU.add), sem("gate_used"))
                    if n >= TT:
                        norm_rows(V, ffn[:, t, :], t, ln_par)
                        norm_rows(V, ffn[:, t, :], t, ln_emb, sem("layer_start"))

            mix_out()
            route()
            experts()
            gated_embedding()
            V.settle()

            def layer(T):
                lv_ring.taken = 0

                def then(ins, s=None):
                    T.did(ins, s)
                    T.settle()

                def project():
                    for u in range(6):
                        for c in range(2):
                            bank = lv_ring.take(T)
                            T.did(dve.tensor_scalar(qk_f[:, u, c * HALF:(c + 1) * HALF], bank[:, 0:HALF], HD ** -0.5 if u < 3 else 1.0, None,
                                                    ALU.mult), lv_ring.drained)
                    for c in range(2):
                        bank = lv_ring.take(T)
                        T.did(dve.tensor_scalar(f_row[0:FH, 0, c * HALF:(c + 1) * HALF], bank[0:FH, 0:HALF], f_b[0:FH, :], None, ALU.add),
                              lv_ring.drained)
                    T.settle()
                    T.did(dve.memset(stat2, 0.0), sem("forget_asked"))

                def forget_gate():
                    T.wait(sem("forget_given"), 1)
                    x = f_row[0:FH, 0, :]
                    then(dve.scalar_tensor_tensor(x, x, 0.0, f_row[0:FH, 1, :], ALU.min, ALU.subtract))
                    then(dve.tensor_tensor_scan(f_row[0:FH, 1, :], ones[0:FH, 0:1].broadcast_to([FH, LEN]), x, 0.0, ALU.mult, ALU.add))

                def rotate_tile(n_th):
                    t = ROTATED[n_th]
                    n = SIZE[t]
                    x = u2[0:n, t, U_QK:U_QK + 8 * RK].rearrange("p (h k d) -> p h k d", h=8, k=2)
                    out = work[0:n, n_th % 2, :].rearrange("p (h d) -> p h d", h=8)
                    a, b = (f_row[0:n, 0, j * 192:(j + 1) * 192].rearrange("p (h d) -> p h d", h=8) for j in range(2))
                    cos, sin = (CONST4(c4, name, t * 24, (t + 1) * 24)[0:n].rearrange("p (o d) -> p o d", o=1).broadcast_to([n, 8, 24])
                                for name in ("cos", "sin"))
                    T.did(dve.tensor_tensor(a, x[:, :, 0, :], cos, ALU.mult))
                    then(dve.tensor_tensor(b, x[:, :, 1, :], sin, ALU.mult))
                    then(dve.tensor_tensor(out[:, :, 0:24], a, b, ALU.subtract))
                    T.did(dve.tensor_tensor(a, x[:, :, 0, :], sin, ALU.mult))
                    then(dve.tensor_tensor(b, x[:, :, 1, :], cos, ALU.mult))
                    then(dve.tensor_tensor(out[:, :, 24:48], a, b, ALU.add), sem("rotated_ready"))

                def rotate_first():
                    T.wait(sem("layer_params_landed"), 16 * 5)
                    then(dve.memset(work.rearrange("p b s -> p (b s)"), 0.0))
                    for t in range(2):
                        T.wait(la_ring.drained, 9 + 1 + t)
                        rotate_tile(t)

                def rotate():
                    for t in range(2, NT2):
                        T.wait(lv_ring.filled, rotated_jobs + t - 1)
                        if ROTATED[t] == 0:
                            T.wait(la_ring.drained, PROJECTED)
                        rotate_tile(t)
                        collect_rotated(t - 2)
                    collect_rotated(NT2 - 2)
                    collect_rotated(NT2 - 1)

                rotated_jobs = 14

                def collect_rotated(n_th):
                    t = ROTATED[n_th]
                    n = SIZE[t]
                    bank = lv_ring.take(T)
                    T.did(dve.tensor_copy(rotated[:, :, OFF[t]:OFF[t] + n], bank[:, 0:4 * n].rearrange("p (u s) -> p u s", u=4)), lv_ring.drained)
                    T.settle()

                def retention():
                    T.wait(sem("retention_decay_landed"), 16)

                    def collect(h):
                        T.wait(sem("retention_done"), 6 * (h + 1))
                        for part, tiles in PARTS:
                            sums = psum[0:part, 6 + h % 2, tiles.start * RV:tiles.stop * RV].rearrange("p (t d) -> p t d", d=RV)
                            T.did(dve.tensor_copy(u2[0:part, tiles, U_V + h * RV:U_V + (h + 1) * RV], sums),
                                  sem("retained_drained") if part == P else None)

                    for h in range(RH):
                        for seg, (i, a, b) in enumerate(SEGMENTS):
                            n = 6 * h + seg
                            if n >= 2:
                                T.wait(sem("retention_done"), n - 1)
                            bank = lv_ring.take(T)
                            T.did(dve.tensor_tensor(work[0:SIZE[i], seg % 2, 0:b - a], bank[0:SIZE[i], 0:b - a],
                                                    retained[0:SIZE[i], h, a - OFF[i]:b - OFF[i]], ALU.mult), lv_ring.drained)
                        if h:
                            collect(h - 1)
                    collect(RH - 1)
                    T.settle()

                def ret_norm():
                    T.wait(sem("ret_gate_ready"), 2)
                    for part, tiles in PARTS:
                        t = tiles.stop - tiles.start
                        v = u2[0:part, tiles, U_V:U_V + RH * RV]
                        v4 = v.rearrange("p t (h d) -> p t h d", h=RH)
                        sq = retained.rearrange("p h s -> p (h s)")[0:part, 0:t * RH * RV].rearrange("p (t h d) -> p t h d", t=t, h=RH)
                        flat = stat2[0:part, tiles.start * RH:tiles.stop * RH]
                        s = flat.rearrange("p (t h) -> p t h", t=t)
                        s4 = flat.rearrange("p (t h o) -> p t h o", t=t, o=1).broadcast_to([part, t, RH, RV])
                        then(dve.tensor_reduce(s, v4, AX.X, ALU.add))
                        then(dve.tensor_scalar(flat, flat, 1.0 / RV, None, ALU.mult))
                        then(dve.tensor_tensor(v4, v4, s4, ALU.subtract))
                        then(dve.tensor_tensor(sq, v4, v4, ALU.mult))
                        then(dve.tensor_reduce(s, sq, AX.X, ALU.add))
                        then(dve.tensor_scalar(flat, flat, 1.0 / RV, LN_EPS, ALU.mult, ALU.add), variance_ready)
                        T.roots += 1
                        T.wait(root_ready, T.roots)
                        then(dve.reciprocal(flat, flat))
                        then(dve.tensor_tensor(v4, v4, s4, ALU.mult))
                        g = ROWS2(rows2, "ret_g")[0:part].rearrange("p (o d) -> p o d", o=1).broadcast_to([part, t, RH * RV])
                        then(dve.tensor_tensor(v, v, g, ALU.mult))
                        then(dve.tensor_tensor(v, v, u2[0:part, tiles, U_G:U_G + RH * RV], ALU.mult))

                def pool():
                    for t in reversed(range(NT2)):
                        n = SIZE[t]
                        bank = lv_ring.take(T)
                        T.did(dve.tensor_copy(work[:, t % 2, 0:2 * n], bank[:, 0:2 * n]), lv_ring.drained)
                        for g in range(2):
                            bank = lv_ring.take(T)
                            T.did(dve.tensor_tensor(u2[0:n, t, U_U + g * P:U_U + (g + 1) * P], bank[0:n, 0:P],
                                                    ROWS2(rows2, "pool_scale", g * P, (g + 1) * P)[0:n], ALU.mult), lv_ring.drained)

                def forget():
                    bank = lv_ring.take(T)
                    T.settle()
                    T.did(dve.tensor_copy(c_col[0:META, 0, :], bank[0:META, 0:FH]))
                    then(dve.tensor_copy(c_col[:, 1:, :], bank[:, FH:NT2 * FH].rearrange("p (t h) -> p t h", t=TT)), lv_ring.drained)
                    waiting = []

                    def finish():
                        h, i, n = waiting.pop(0)
                        m = SIZE[i]
                        T.wait(sem("fox_out"), n + 1)
                        then(dve.reciprocal(row_sum[0:m, n % 4:n % 4 + 1], row_sum[0:m, n % 4:n % 4 + 1]))
                        T.did(dve.tensor_scalar(u2[0:m, i, U_QK + h * HD:U_QK + (h + 1) * HD], psum[0:m, 6 + n % 2, 0:HD],
                                                row_sum[0:m, n % 4:n % 4 + 1], None, ALU.mult), sem("fox_out_drained"))
                        T.settle()

                    n = 0
                    for h in range(FH):
                        for c in range(2):
                            bank = lv_ring.take(T)
                            T.settle()
                            T.did(dve.tensor_scalar(fox_c[:, h % 2, c * HALF:(c + 1) * HALF], bank[:, 0:HALF], -1.0, None, ALU.mult),
                                  lv_ring.drained)
                        T.settle()
                        for i in range(NT2):
                            m, w = SIZE[i], OFF[i] + SIZE[i]
                            T.wait(sem("fox_scores"), n + 1)
                            if n >= 3:
                                T.wait(sem("fox_turned"), FOX_TURNED[n - 3])
                            pair = psum[0:m, n % 2 * 2:n % 2 * 2 + 2, :].rearrange("p b s -> p (b s)")
                            p = fox_p[0:m, n % 3, 0:w]
                            then(dve.scalar_tensor_tensor(p, pair[:, 0:w], c_col[0:m, i, h:h + 1], fox_c[0:m, h % 2, 0:w], ALU.add, ALU.add),
                                 sem("fox_scores_drained"))
                            diag = p[:, OFF[i]:w]
                            then(dve.tensor_tensor(diag, diag, CONST4(c4, "row_causal")[0:m, 0:m], ALU.add))
                            if n >= 4:
                                finish()
                            then(dve.tensor_reduce(row_max[0:m, n % 4:n % 4 + 1], p, AX.X, ALU.max, negate=True), sem("fox_max"))
                            waiting.append((h, i, n))
                            n += 1
                    for _ in range(4):
                        finish()
                    T.did(dve.memset(stat2, 0.0), sem("mix2_ready"))

                def add_rows(nth, normed, half_done=None):
                    for half in range(2):
                        for t in range(NT2):
                            m, part = SIZE[t], slice(half * 512, (half + 1) * 512)
                            bank = lv_ring.take(T)
                            rows = h2[0:m, t, part]
                            for quarter in range(0 if t else 3, -1, -1):
                                T.did(dve.scalar_tensor_tensor(rows, rows, ALPHA2 if quarter == (0 if t else 3) else 1.0,
                                                               bank[quarter * 32:quarter * 32 + m, :], ALU.mult, ALU.add),
                                      None if quarter else lv_ring.drained)
                                if quarter:
                                    T.settle()
                            if half == 1:
                                norm_rows(T, h2[0:m, t, :], t, ln_par2, normed, m)
                        if half == 0:
                            if half_done is not None:
                                T.did(dve.memset(stat2, 0.0), half_done)
                            T.wait(sem("layer_ln_landed"), 16 * nth)

                rotate_first()
                project()
                forget_gate()
                rotate()
                retention()
                pool()
                ret_norm()
                forget()
                add_rows(1, sem("mid_ready"))
                for f in range(FT):
                    for c in range(2):
                        bank = lv_ring.take(T)
                        g = ff_t[:, f, c * HALF:(c + 1) * HALF]
                        T.wait(la_ring.drained, PROJECTED + 2 * 2 * NT2 + 2 * f + c + 1)
                        T.did(dve.tensor_tensor(g, g, bank[:, 0:HALF], ALU.mult), lv_ring.drained)
                add_rows(2, sem("layer_start"), sem("early_slots_free"))

            dve.sem_inc(lv_ring.drained, 3)
            dve.sem_inc(sem("retained_drained"), 2)
            dve.sem_inc(sem("fox_out_drained"), 2)
            assert V.roots == EARLY_ROOTS
            with dve.Fori(0, LAYERS) as i:
                T = Turn(dve, i, sem("layer_vector_step"), LAYER_PER, LAYER_CREDIT, sem("passed"))
                T.roots = 0
                layer(T)
                T.check()


def units(w):
    w = np.ascontiguousarray(w)
    k, n = w.shape
    pieces = -(-n // 512)
    out = np.zeros((pieces, P, k // P, 512), np.float32)
    for i in range(pieces):
        part = w[:, i * 512:(i + 1) * 512]
        out[i, :, :, 0:part.shape[1]] = part.reshape(k // P, P, -1).transpose(1, 0, 2)
    return out.reshape(pieces, P, -1)


def columns(v):
    return np.asarray(v).reshape(-1, P).T


def layout_block1(a):
    w = np.asarray(a["w_in"])[0]
    names = dict(z=W, xbc=512, dt=H, rwkv=896, gqk=W, gv=W, gd=16, gog=W, mqk=512, mv=W, i=H, f=H, mog=W)
    at, part = 0, {}
    for name, n in names.items():
        part[name] = w[:, at:at + n]
        at += n
    assert at == w.shape[1]
    rows = np.zeros((D, P), np.float32)
    for name, at in (("dt", 0), ("i", 32), ("f", 64), ("gd", 96)):
        rows[:, at:at + part[name].shape[1]] = part[name]
    order = [part["xbc"], part["mqk"], part["gqk"], part["rwkv"], rows, part["gog"], part["z"], part["mv"],
             part["mog"], part["gv"]]
    w_in = units(np.concatenate(order, 1))
    io = {"x_t": np.ascontiguousarray(np.asarray(a["x"])[0].T.reshape(KT, P, SEQ).transpose(1, 0, 2))}
    io["weights1"] = np.concatenate([w_in, units(np.asarray(a["w_out"])[0])])
    io["const1"] = const1()
    io["const2"] = const2()
    cols = np.zeros((P, COLS.width), np.float32)
    for name, tiles in (("ssd", 4), ("m", 4)):
        cw = np.asarray(a[{"ssd": "ssd_conv_w", "m": "mlstm_conv_w"}[name]])[0]
        COLS(cols, name + "_cw")[:] = cw.reshape(4, tiles, P).transpose(2, 1, 0).reshape(P, 16)
        COLS(cols, name + "_cb")[:] = columns(a[{"ssd": "ssd_conv_b", "m": "mlstm_conv_b"}[name]])
    for name, key in (("mu", "rwkv_mu"), ("w0", "rwkv_w0"), ("a0", "rwkv_a0"), ("k_k", "rwkv_k_k"),
                      ("k_a", "rwkv_k_a"), ("r_k", "rwkv_r_k"), ("gate_b", "gla_gate_b")):
        COLS(cols, name)[:] = columns(a[key])
    b = COLS(cols, "rows_b")
    for key, at in (("ssd_dt_bias", 0), ("mlstm_i_b", 32), ("mlstm_f_b", 64)):
        b[at:at + H, 0] = np.asarray(a[key])[0]
    COLS(cols, "a_log")[0:H, 0] = np.asarray(a["ssd_a_log"])[0]
    io["cols"] = cols
    rows = [np.asarray(a[key]).reshape(-1) for key in
            ("ssd_d", "ssd_norm_g", "rwkv_ln_g", "rwkv_ln_b", "gla_norm_g", "mlstm_norm_g")]
    io["rows"] = np.concatenate(rows)[None]
    io["lora_up"] = np.concatenate([np.asarray(a[k])[0] for k in ("rwkv_w_up", "rwkv_a_up", "rwkv_g_up")])
    io["gate_up"] = np.asarray(a["gla_gate_up"])[0]
    io["const3"] = const3()
    io["x"] = np.ascontiguousarray(np.asarray(a["x"])[0].reshape(TT, P, D).transpose(1, 0, 2))
    io["p_t"] = np.ascontiguousarray(np.asarray(a["p"])[0, 0].T.reshape(2, P, SEQ).transpose(1, 0, 2))
    for n in "12":
        io["ln" + n] = np.concatenate([np.asarray(a[f"ln{n}_g"])[0], np.asarray(a[f"ln{n}_b"])[0]])[None]
    io["router_w"] = np.ascontiguousarray(np.asarray(a["router_w"])[0].reshape(KT, P, E).transpose(1, 0, 2))
    io["router_b"] = np.asarray(a["router_b"])
    io["b_down"] = np.asarray(a["exp_b_down"])[0]
    io["b_gu"] = np.ascontiguousarray(np.asarray(a["exp_b_gu"])[0].reshape(E, 2, 4, 256).transpose(0, 2, 1, 3).reshape(E, 2 * D))
    io["ple_gate"] = units(np.asarray(a["ple_gate_w"])[0])
    io["ple_proj"] = np.ascontiguousarray(np.asarray(a["ple_proj"])[0].reshape(2, P, D).transpose(1, 0, 2)).reshape(P, 2 * D)
    gu = np.asarray(a["exp_w_gu"])[0].reshape(E, KT, P, 2, 4, 256)
    io["exp_gu"] = np.ascontiguousarray(gu.transpose(0, 4, 2, 1, 3, 5)).reshape(E * 4, P, PIECE)
    down = np.asarray(a["exp_w_down"])[0].reshape(E, KT, P, 2, 512)
    io["exp_down"] = np.ascontiguousarray(down.transpose(0, 3, 2, 1, 4)).reshape(E * 2, P, PIECE)
    return io


def layout_block2(a):
    g = {k[:-2]: np.asarray(v) for k, v in a.items() if k.endswith("_2")}
    pieces = []
    for l in range(LAYERS):
        w = g["w_in"][l]
        names = dict(qr=192, kr=192, vr=384, gr=384, u=256, qf=384, kf=384, vf=384, f=FH)
        at, part = 0, {}
        for name, n in names.items():
            part[name] = w[:, at:at + n]
            at += n
        pieces.append(units(np.concatenate([part[n] for n in ("qr", "kr", "vr", "gr", "u", "vf", "qf", "kf")], 1)))
        pieces.append(units(g["w_out"][l]))
        w1, w3 = (g[n][l].reshape(D, FT // 2, 256) for n in ("w_ffn1", "w_ffn3"))
        pieces.append(units(np.concatenate([w1, w3], 2).reshape(D, 2 * FF)))
        w2 = np.zeros((3 * D, D), np.float32)
        w2[0:FF] = g["w_ffn2"][l]
        w2 = w2.reshape(3, KT, P, 2, 512).transpose(3, 0, 2, 1, 4)
        pieces.append(w2.reshape(6, P, PIECE))
    io = {"weights2": np.concatenate(pieces)}
    f_w = g["w_in"][:, :, -FH:].reshape(LAYERS, KT, P, FH).transpose(0, 2, 1, 3)
    io["f_w"] = np.ascontiguousarray(f_w).reshape(LAYERS, P, KT * FH)
    io["f_b"] = g["b_f"].reshape(LAYERS, FH, 1)
    pool = np.zeros((LAYERS, 2, HD, 2, 2, HD), np.float32)
    for i in range(2):
        pool[:, i, :, :, i, :] = g["pool_w"].reshape(LAYERS, 2, 2, HD, HD)[:, :, i].transpose(0, 2, 1, 3)
    io["pool_w"] = pool.reshape(LAYERS, P, 4 * HD)
    io["rows2"] = np.concatenate([g["ret_gn_g"], g["pool_scale"]], 1)
    io["meta"] = g["meta"]
    io["ln_emb"] = np.concatenate([g["ln_emb_g"], g["ln_emb_b"]])[None]
    io["ln_mid"] = np.concatenate([g["ln1_g"], g["ln1_b"]], 1)
    io["ln_end"] = np.concatenate([g["ln2_g"], g["ln2_b"]], 1)
    io["const4"] = const4()
    io["retention_decay"] = retention_decay()
    return io


def layout(a):
    io = {**layout_block1(a), **layout_block2(a)}
    return {name: np.ascontiguousarray(v) for name, v in io.items()}


def kernel(**inputs):
    import concourse.bacc as bacc
    from concourse.bass_utils import run_bass_kernel_spmd

    arrays = layout(inputs)
    nc = bacc.Bacc("TRN2", target_bir_lowering=False, num_devices=1)
    io = {name: nc.dram_tensor(name, v.shape, F32, kind="ExternalInput").ap() for name, v in arrays.items()}
    out = nc.dram_tensor("out", (1, SEQ, D), F32, kind="ExternalOutput").ap()
    io["out"] = out.rearrange("o s d -> (o s) d")
    build(nc, io)
    result = run_bass_kernel_spmd(nc, [arrays], core_ids=[0])
    return result.results[0]["out"]
```
